# Optimizing a Trainium2 kernel written in Bass

```python
import jax, jax.numpy as jnp
from jax import lax
import numpy as np
import math

D_MODEL = 1024
BATCH = 1
SEQ = 256
DEPTH = 1

CTX_LEN = 256
GRID_W = 64
N_MIXERS = 2
EPS = 1e-6
N_MOD = 6
HG_EXPAND = 128
HG_HEADS = D_MODEL // HG_EXPAND
HG_DV = D_MODEL // HG_HEADS
HG_CHUNK = 64
N_HG_PROJ = 5
POOL_WINDOWS = (2, 4, 8, 16)
POOL_GROUPS = len(POOL_WINDOWS)
POOL_GDIM = D_MODEL // POOL_GROUPS
N_EXPERTS = 16
N_EXPERT_GROUPS = 4
EXPERTS_PER_GROUP = N_EXPERTS // N_EXPERT_GROUPS
TOP_K = 2
D_EXPERT = 256


def rms_norm(x, g):
    xf = x.astype(jnp.float32)
    y = xf * lax.rsqrt(jnp.mean(xf * xf, axis=-1, keepdims=True) + EPS)
    return (y * g.astype(jnp.float32)).astype(x.dtype)

def modulate(x, g, shift, scale):
    return rms_norm(x, g) * (1.0 + scale) + shift

def _heads(t):
    b, l, _ = t.shape
    return t.reshape(b, l, HG_HEADS, -1).transpose(0, 2, 1, 3).astype(jnp.float32)

def _rev(t):
    return jnp.flip(t, axis=2)

def _lower_bound(logits, slot):
    p = jax.nn.softmax(logits.astype(jnp.float32), axis=0)
    return jnp.cumsum(p, axis=0)[slot].reshape(HG_HEADS, 1, HG_EXPAND)

def _gate(z, lb):
    log_f = jnp.logaddexp(jnp.log(lb), jnp.log1p(-lb) + jax.nn.log_sigmoid(z))
    k = (1.0 - lb) * jax.nn.sigmoid(-z)
    return log_f, k

def _gla_scan(q, k, v, log_f, s0):
    b, h, l, _ = q.shape
    dv = v.shape[-1]
    n = l // HG_CHUNK
    rs = lambda t: t.reshape(b, h, n, HG_CHUNK, t.shape[-1])
    q, k, v, log_f = rs(q), rs(k), rs(v), rs(log_f)
    cum = jnp.cumsum(log_f, axis=3)
    ref = cum[:, :, :, HG_CHUNK // 2 - 1:HG_CHUNK // 2, :]
    scores = jnp.einsum('bhnck,bhnsk->bhncs', q * jnp.exp(cum - ref), k * jnp.exp(ref - cum))
    tri = jnp.tril(jnp.ones((HG_CHUNK, HG_CHUNK), dtype=bool))
    scores = jnp.where(tri, scores, 0.0)
    intra = jnp.einsum('bhncs,bhnsv->bhncv', scores, v)
    last = cum[:, :, :, -1:, :]
    chunk_kv = jnp.einsum('bhnck,bhncv->nbhkv', k * jnp.exp(last - cum), v)
    chunk_decay = jnp.moveaxis(jnp.exp(last[:, :, :, 0, :]), 2, 0)

    def step(s, inp):
        dec, kv = inp
        return dec[..., None] * s + kv, s

    s_final, s_prev = lax.scan(step, s0, (chunk_decay, chunk_kv))
    inter = jnp.einsum('bhnck,nbhkv->bhncv', q * jnp.exp(cum), s_prev)
    return (intra + inter).reshape(b, h, l, dv), s_final

def _hgrn_inputs(h, w_in):
    q, v, zf, zb, g = jnp.split(h @ w_in, N_HG_PROJ, axis=-1)
    return jax.nn.silu(_heads(q)), _heads(v), _heads(zf), _heads(zb), g

def _hgrn_readout(o, g, gnorm, w_out):
    b, h, l, dv = o.shape
    o = o * lax.rsqrt(jnp.mean(o * o, axis=-1, keepdims=True) + EPS) * gnorm.astype(jnp.float32)
    o = o.transpose(0, 2, 1, 3).reshape(b, l, h * dv)
    y = (o * jax.nn.silu(g.astype(jnp.float32))).astype(g.dtype)
    return y @ w_out

def hgrn2_mixer(h_lat, h_ctx, w_in, lb_fwd, lb_bwd, gnorm, w_out, slot, need_ctx):
    lbf = _lower_bound(lb_fwd, slot)
    lbb = _lower_bound(lb_bwd, slot)
    qc, vc, zfc, zbc, gc = _hgrn_inputs(h_ctx, w_in)
    ql, vl, zfl, zbl, gl = _hgrn_inputs(h_lat, w_in)
    s0 = jnp.zeros((h_lat.shape[0], HG_HEADS, HG_EXPAND, HG_DV), jnp.float32)
    lf, kf = _gate(zfc, lbf)
    o_cf, s_f = _gla_scan(qc, kf, vc, lf, s0)
    lf, kf = _gate(zfl, lbf)
    o_lf, _ = _gla_scan(ql, kf, vl, lf, s_f)
    lbk, kb = _gate(zbc, lbb)
    o_cb, s_b = _gla_scan(_rev(qc), _rev(kb), _rev(vc), _rev(lbk), s0)
    lbk, kb = _gate(zbl, lbb)
    o_lb, _ = _gla_scan(_rev(ql), _rev(kb), _rev(vl), _rev(lbk), s_b)
    y_lat = _hgrn_readout(o_lf + _rev(o_lb), gl, gnorm, w_out)
    y_ctx = _hgrn_readout(o_cf + _rev(o_cb), gc, gnorm, w_out) if need_ctx else None
    return y_lat, y_ctx

def _box_sum(u, win, axis):
    n = u.shape[axis]
    cs = jnp.cumsum(u, axis=axis)
    pad = [(0, 0)] * u.ndim
    pad[axis] = (1, 0)
    cs = jnp.pad(cs, pad)
    t = jnp.arange(n)
    lo = jnp.clip(t - win // 2, 0, n)
    hi = jnp.clip(t - win // 2 + win, 0, n)
    return jnp.take(cs, hi, axis=axis) - jnp.take(cs, lo, axis=axis), hi - lo

def _grid_mean(u, win):
    b, l, d = u.shape
    rows = l // GRID_W
    g = u.reshape(b, rows, GRID_W, d)
    s, cnt_c = _box_sum(g, win, 2)
    s, cnt_r = _box_sum(s, win, 1)
    cnt = (cnt_r[:, None] * cnt_c[None, :]).astype(u.dtype)
    return (s / cnt[None, :, :, None]).reshape(b, l, d)

def _seq_mean(u, win):
    s, cnt = _box_sum(u, win, 1)
    return s / cnt.astype(u.dtype)[None, :, None]

def _pool_mix(h, mean_fn, w_in, w_grp, p_scale, w_out):
    u = (h @ w_in).astype(jnp.float32)
    parts = []
    for gi, win in enumerate(POOL_WINDOWS):
        ug = u[..., gi * POOL_GDIM:(gi + 1) * POOL_GDIM]
        parts.append((mean_fn(ug, win) - ug) @ w_grp[gi].astype(jnp.float32))
    y = jnp.concatenate(parts, axis=-1) * p_scale.astype(jnp.float32)
    return y.astype(h.dtype) @ w_out

def pool_mixer(h_lat, h_ctx, w_in, w_grp, p_scale, w_out, need_ctx):
    y_lat = _pool_mix(h_lat, _grid_mean, w_in, w_grp, p_scale, w_out)
    y_ctx = _pool_mix(h_ctx, _seq_mean, w_in, w_grp, p_scale, w_out) if need_ctx else None
    return y_lat, y_ctx

def moe_ffn(h, router_w, router_b, w_gate, w_up, w_down):
    n = h.shape[0]
    s = jax.nn.sigmoid((h @ router_w).astype(jnp.float32))
    sel = (s + router_b.astype(jnp.float32)).reshape(n, N_EXPERT_GROUPS, EXPERTS_PER_GROUP)
    top_v, top_i = lax.top_k(sel, TOP_K)
    best = jnp.argmax(jnp.sum(top_v, axis=-1), axis=-1)
    loc = jnp.take_along_axis(top_i, best[:, None, None], axis=1)[:, 0]
    ids = best[:, None] * EXPERTS_PER_GROUP + loc
    w = jnp.take_along_axis(s, ids, axis=1)
    w = w / jnp.sum(w, axis=-1, keepdims=True)
    combine = jnp.sum(jax.nn.one_hot(ids, N_EXPERTS, dtype=jnp.float32) * w[..., None], axis=1)
    y = jnp.zeros(h.shape, jnp.float32)
    for e in range(N_EXPERTS):
        a = jax.nn.silu(h @ w_gate[e]) * (h @ w_up[e])
        y = y + combine[:, e:e + 1] * (a @ w_down[e]).astype(jnp.float32)
    return y.astype(h.dtype)

def first_inputs(seed: int = 0) -> dict:
    key = jax.random.key(seed)
    ks = jax.random.split(key, 24)
    n_a = (DEPTH + N_MIXERS - 1) // N_MIXERS
    n_b = DEPTH // N_MIXERS
    nrm = lambda k, shape, sc: jax.random.normal(k, shape, jnp.float32) * sc
    d = D_MODEL
    return {
        "x": nrm(ks[0], (BATCH, SEQ, d), 1.0),
        "c": nrm(ks[1], (BATCH, d), 1.0),
        "ctx": nrm(ks[2], (BATCH, CTX_LEN, d), 1.0),
        "c_ctx": nrm(ks[3], (d,), 1.0),
        "w_mod": nrm(ks[4], (DEPTH, d, N_MOD * d), 0.5 * d ** -0.5),
        "b_mod": nrm(ks[5], (DEPTH, N_MOD * d), 0.01),
        "norm1_g": 1.0 + nrm(ks[6], (DEPTH, d), 0.05),
        "norm2_g": 1.0 + nrm(ks[7], (DEPTH, d), 0.05),
        "hg_w_in": nrm(ks[8], (n_a, d, N_HG_PROJ * d), d ** -0.5),
        "hg_lb_fwd": nrm(ks[9], (n_a + 1, d), 0.5),
        "hg_lb_bwd": nrm(ks[10], (n_a + 1, d), 0.5),
        "hg_gnorm": 1.0 + nrm(ks[11], (n_a, HG_DV), 0.05),
        "hg_w_out": nrm(ks[12], (n_a, d, d), d ** -0.5),
        "pool_w_in": nrm(ks[13], (n_b, d, d), d ** -0.5),
        "pool_w_grp": nrm(ks[14], (n_b, POOL_GROUPS, POOL_GDIM, POOL_GDIM), POOL_GDIM ** -0.5),
        "pool_scale": 1.0 + nrm(ks[15], (n_b, d), 0.1),
        "pool_w_out": nrm(ks[16], (n_b, d, d), d ** -0.5),
        "router_w": nrm(ks[17], (d, N_EXPERTS), d ** -0.5),
        "router_b": nrm(ks[18], (N_EXPERTS,), 0.01),
        "moe_w_gate": nrm(ks[19], (DEPTH, N_EXPERTS, d, D_EXPERT), d ** -0.5),
        "moe_w_up": nrm(ks[20], (DEPTH, N_EXPERTS, d, D_EXPERT), d ** -0.5),
        "moe_w_down": nrm(ks[21], (DEPTH, N_EXPERTS, D_EXPERT, d), D_EXPERT ** -0.5),
        "final_g": 1.0 + nrm(ks[22], (d,), 0.05),
    }

def first_block(x, c, ctx, c_ctx, w_mod, b_mod, norm1_g, norm2_g, hg_w_in, hg_lb_fwd, hg_lb_bwd, hg_gnorm,
              hg_w_out, pool_w_in, pool_w_grp, pool_scale, pool_w_out, router_w, router_b, moe_w_gate,
              moe_w_up, moe_w_down, final_g):
    x_lat, x_ctx = x, ctx
    d = x.shape[-1]
    for i in range(DEPTH):
        need_ctx = i < DEPTH - 1
        slot = i // N_MIXERS
        mod = jax.nn.silu(c) @ w_mod[i] + b_mod[i]
        sh1, sc1, g1, sh2, sc2, g2 = jnp.split(mod[:, None, :], N_MOD, axis=-1)
        mod_c = jax.nn.silu(c_ctx) @ w_mod[i] + b_mod[i]
        csh1, csc1, cg1, csh2, csc2, cg2 = jnp.split(mod_c, N_MOD, axis=-1)
        h_lat = modulate(x_lat, norm1_g[i], sh1, sc1)
        h_ctx = modulate(x_ctx, norm1_g[i], csh1, csc1)
        if i % N_MIXERS == 0:
            y_lat, y_ctx = hgrn2_mixer(h_lat, h_ctx, hg_w_in[slot], hg_lb_fwd, hg_lb_bwd, hg_gnorm[slot],
                                       hg_w_out[slot], slot, need_ctx)
        else:
            y_lat, y_ctx = pool_mixer(h_lat, h_ctx, pool_w_in[slot], pool_w_grp[slot], pool_scale[slot],
                                      pool_w_out[slot], need_ctx)
        x_lat = x_lat + g1 * y_lat
        h2_lat = modulate(x_lat, norm2_g[i], sh2, sc2).reshape(-1, d)
        n_lat = h2_lat.shape[0]
        if need_ctx:
            x_ctx = x_ctx + cg1 * y_ctx
            h2_ctx = modulate(x_ctx, norm2_g[i], csh2, csc2).reshape(-1, d)
            ff = moe_ffn(jnp.concatenate([h2_lat, h2_ctx], axis=0), router_w, router_b,
                         moe_w_gate[i], moe_w_up[i], moe_w_down[i])
            x_ctx = x_ctx + cg2 * ff[n_lat:].reshape(x_ctx.shape)
            ff_lat = ff[:n_lat]
        else:
            ff_lat = moe_ffn(h2_lat, router_w, router_b, moe_w_gate[i], moe_w_up[i], moe_w_down[i])
        x_lat = x_lat + g2 * ff_lat.reshape(x_lat.shape)
    return rms_norm(x_lat, final_g)


DEPTH_2 = 4

CHUNK = 64
N_MIXERS_2 = 3
N_RET = (DEPTH_2 + 2) // 3
N_CONV = (DEPTH_2 + 1) // 3
N_SB = DEPTH_2 // 3
RET_HEADS = 4
RET_DK = D_MODEL // RET_HEADS
RET_DV = 2 * D_MODEL // RET_HEADS
ROPE_BASE = 10000.0
CONV_WIDTH = 31
SB_HEADS = 16
SB_DH = D_MODEL // SB_HEADS
SB_BLOCK = 128
D_FF = 4 * D_MODEL


def rms_norm_2(x, w):
    xf = x.astype(jnp.float32)
    y = xf * lax.rsqrt(jnp.mean(xf * xf, axis=-1, keepdims=True) + EPS)
    return (y * w.astype(jnp.float32)).astype(x.dtype)

def layer_norm(x, w, b):
    xf = x.astype(jnp.float32)
    mu = jnp.mean(xf, axis=-1, keepdims=True)
    var = jnp.mean(jnp.square(xf - mu), axis=-1, keepdims=True)
    y = (xf - mu) * lax.rsqrt(var + EPS)
    return y * w.astype(jnp.float32) + b.astype(jnp.float32)

def apply_rotary(t, seq_len):
    half = t.shape[-1] // 2
    inv_freq = ROPE_BASE ** (-jnp.arange(half, dtype=jnp.float32) / half)
    ang = jnp.arange(seq_len, dtype=jnp.float32)[:, None] * inv_freq[None, :]
    cos = jnp.cos(ang)[:, None, :]
    sin = jnp.sin(ang)[:, None, :]
    t1, t2 = t[..., :half], t[..., half:]
    return jnp.concatenate([t1 * cos - t2 * sin, t1 * sin + t2 * cos], axis=-1)

def retention_chunkwise(q, k, v):
    b, s, h, _ = q.shape
    n = s // CHUNK

    def to_chunks(t):
        return t.reshape(b, n, CHUNK, h, -1).transpose(1, 0, 3, 2, 4)

    log_g = jnp.log(1.0 - jnp.exp2(-5.0 - jnp.arange(h, dtype=jnp.float32)))
    idx = jnp.arange(CHUNK, dtype=jnp.float32)
    intra_decay = jnp.exp(log_g[:, None, None] * jnp.abs(idx[:, None] - idx[None, :]))
    q_decay = jnp.exp(log_g[:, None] * (idx + 1.0))[..., None]
    k_decay = jnp.exp(log_g[:, None] * (CHUNK - 1.0 - idx))[..., None]
    chunk_decay = jnp.exp(log_g * CHUNK)[:, None, None]

    def step(state, inp):
        qc, kc, vc = inp
        scores = jnp.einsum('bhcd,bhsd->bhcs', qc, kc) * intra_decay
        out = (jnp.einsum('bhcs,bhse->bhce', scores, vc)
               + jnp.einsum('bhcd,bhde->bhce', qc * q_decay, state))
        state = state * chunk_decay + jnp.einsum('bhsd,bhse->bhde', kc * k_decay, vc)
        return state, out

    state0 = jnp.zeros((b, h, q.shape[-1], v.shape[-1]), jnp.float32)
    _, out = lax.scan(step, state0, (to_chunks(q), to_chunks(k), to_chunks(v)))
    return out.transpose(1, 0, 3, 2, 4).reshape(b, s, h, -1)

def retention_mixer(xn, w_in, q_gain, k_gain, gn_w, gn_b, w_out):
    b, s, _ = xn.shape
    proj = xn @ w_in
    q, k, v, g = jnp.split(proj, [D_MODEL, 2 * D_MODEL, 4 * D_MODEL], axis=-1)
    q = rms_norm_2(q.reshape(b, s, RET_HEADS, RET_DK), q_gain).astype(jnp.float32)
    k = rms_norm_2(k.reshape(b, s, RET_HEADS, RET_DK), k_gain).astype(jnp.float32)
    v = v.reshape(b, s, RET_HEADS, RET_DV).astype(jnp.float32)
    q = apply_rotary(q, s)
    k = apply_rotary(k, s) * (RET_DK ** -0.5)
    y = retention_chunkwise(q, k, v)
    mu = jnp.mean(y, axis=-1, keepdims=True)
    var = jnp.mean(jnp.square(y - mu), axis=-1, keepdims=True)
    y = (y - mu) * lax.rsqrt(var + EPS)
    y = y * gn_w.astype(jnp.float32).reshape(RET_HEADS, RET_DV) + gn_b.astype(jnp.float32).reshape(RET_HEADS, RET_DV)
    y = y.reshape(b, s, 2 * D_MODEL).astype(xn.dtype)
    return (jax.nn.silu(g) * y) @ w_out

def conformer_conv_mixer(xn, pw1_w, pw1_b, dw_w, dw_b, ln_w, ln_b, pw2_w, pw2_b):
    h = xn @ pw1_w + pw1_b
    a, gate = jnp.split(h, 2, axis=-1)
    h = a * jax.nn.sigmoid(gate)
    h = lax.conv_general_dilated(
        h, dw_w[:, None, :].astype(h.dtype), window_strides=(1,),
        padding=[(CONV_WIDTH - 1, 0)],
        dimension_numbers=('NWC', 'WIO', 'NWC'),
        feature_group_count=D_MODEL) + dw_b
    h = layer_norm(h, ln_w, ln_b)
    h = jax.nn.silu(h).astype(xn.dtype)
    return h @ pw2_w + pw2_b

def stick_breaking_mixer(xn, w_in, q_gain, k_gain, w_out):
    b, s, _ = xn.shape
    proj = xn @ w_in
    q, k, v = jnp.split(proj, 3, axis=-1)
    q = rms_norm_2(q.reshape(b, s, SB_HEADS, SB_DH), q_gain).astype(jnp.float32).transpose(0, 2, 1, 3)
    k = rms_norm_2(k.reshape(b, s, SB_HEADS, SB_DH), k_gain).astype(jnp.float32).transpose(0, 2, 1, 3)
    v = v.reshape(b, s, SB_HEADS, SB_DH).astype(jnp.float32).transpose(0, 2, 1, 3)
    scale = SB_DH ** -0.5
    outs = []
    for b0 in range(0, s, SB_BLOCK):
        kend = b0 + SB_BLOCK
        z = jnp.einsum('bhqd,bhkd->bhqk', q[:, :, b0:kend], k[:, :, :kend]) * scale
        t_idx = b0 + jnp.arange(SB_BLOCK)
        s_idx = jnp.arange(kend)
        mask = s_idx[None, :] < t_idx[:, None]
        log_1mb = jnp.where(mask, jax.nn.log_sigmoid(-z), 0.0)
        log_w = jax.nn.log_sigmoid(z) + lax.cumsum(log_1mb, axis=3, reverse=True) - log_1mb
        a = jnp.where(mask, jnp.exp(log_w), 0.0)
        outs.append(jnp.einsum('bhqk,bhkd->bhqd', a, v[:, :, :kend]))
    y = jnp.concatenate(outs, axis=2).transpose(0, 2, 1, 3).reshape(b, s, D_MODEL).astype(xn.dtype)
    return y @ w_out

def squared_relu_mlp(xn, w1, w2):
    h = jax.nn.relu(xn @ w1)
    return (h * h) @ w2

def second_inputs(seed: int = 0) -> dict:
    key = jax.random.key(seed)
    ks = iter(jax.random.split(key, 32))
    f32 = jnp.float32

    def nrm(shape, scale):
        return jax.random.normal(next(ks), shape, f32) * scale

    def gain(shape):
        return 1.0 + 0.02 * jax.random.normal(next(ks), shape, f32)

    D = D_MODEL
    return {
        "x": jax.random.normal(next(ks), (BATCH, SEQ, D), f32),
        "norm_mix": gain((DEPTH_2, D)),
        "norm_ffn": gain((DEPTH_2, D)),
        "ret_w_in": nrm((N_RET, D, 6 * D), D ** -0.5),
        "ret_q_norm": gain((N_RET, RET_DK)),
        "ret_k_norm": gain((N_RET, RET_DK)),
        "ret_gn_w": gain((N_RET, 2 * D)),
        "ret_gn_b": nrm((N_RET, 2 * D), 0.01),
        "ret_w_out": nrm((N_RET, 2 * D, D), (2 * D) ** -0.5),
        "conv_pw1_w": nrm((N_CONV, D, 2 * D), D ** -0.5),
        "conv_pw1_b": nrm((N_CONV, 2 * D), 0.01),
        "conv_dw_w": nrm((N_CONV, CONV_WIDTH, D), CONV_WIDTH ** -0.5),
        "conv_dw_b": nrm((N_CONV, D), 0.01),
        "conv_ln_w": gain((N_CONV, D)),
        "conv_ln_b": nrm((N_CONV, D), 0.01),
        "conv_pw2_w": nrm((N_CONV, D, D), D ** -0.5),
        "conv_pw2_b": nrm((N_CONV, D), 0.01),
        "sb_w_in": nrm((N_SB, D, 3 * D), D ** -0.5),
        "sb_q_norm": gain((N_SB, SB_DH)),
        "sb_k_norm": gain((N_SB, SB_DH)),
        "sb_w_out": nrm((N_SB, D, D), D ** -0.5),
        "ffn_w1": nrm((DEPTH_2, D, D_FF), D ** -0.5),
        "ffn_w2": nrm((DEPTH_2, D_FF, D), D_FF ** -0.5),
        "final_norm": gain((D,)),
    }

def second_block(x, norm_mix, norm_ffn,
              ret_w_in, ret_q_norm, ret_k_norm, ret_gn_w, ret_gn_b, ret_w_out,
              conv_pw1_w, conv_pw1_b, conv_dw_w, conv_dw_b, conv_ln_w, conv_ln_b, conv_pw2_w, conv_pw2_b,
              sb_w_in, sb_q_norm, sb_k_norm, sb_w_out,
              ffn_w1, ffn_w2, final_norm):
    for i in range(DEPTH_2):
        kind = i % N_MIXERS_2
        j = i // N_MIXERS_2
        h = rms_norm_2(x, norm_mix[i])
        if kind == 0:
            m = retention_mixer(h, ret_w_in[j], ret_q_norm[j], ret_k_norm[j],
                                ret_gn_w[j], ret_gn_b[j], ret_w_out[j])
        elif kind == 1:
            m = conformer_conv_mixer(h, conv_pw1_w[j], conv_pw1_b[j], conv_dw_w[j], conv_dw_b[j],
                                     conv_ln_w[j], conv_ln_b[j], conv_pw2_w[j], conv_pw2_b[j])
        else:
            m = stick_breaking_mixer(h, sb_w_in[j], sb_q_norm[j], sb_k_norm[j], sb_w_out[j])
        x = x + m
        x = x + squared_relu_mlp(rms_norm_2(x, norm_ffn[i]), ffn_w1[i], ffn_w2[i])
    return rms_norm_2(x, final_norm)


def setup_inputs(seed=0):
    out = dict(first_inputs(seed))
    for name, value in second_inputs(seed + 1).items():
        if name != "x":
            out[name + "_2"] = value
    return out


def reference(
    x, c, ctx, c_ctx, w_mod, b_mod, norm1_g, norm2_g, hg_w_in, hg_lb_fwd, hg_lb_bwd, hg_gnorm,
    hg_w_out, pool_w_in, pool_w_grp, pool_scale, pool_w_out, router_w, router_b, moe_w_gate,
    moe_w_up, moe_w_down, final_g, norm_mix_2, norm_ffn_2, ret_w_in_2, ret_q_norm_2,
    ret_k_norm_2, ret_gn_w_2, ret_gn_b_2, ret_w_out_2, conv_pw1_w_2, conv_pw1_b_2, conv_dw_w_2,
    conv_dw_b_2, conv_ln_w_2, conv_ln_b_2, conv_pw2_w_2, conv_pw2_b_2, sb_w_in_2, sb_q_norm_2,
    sb_k_norm_2, sb_w_out_2, ffn_w1_2, ffn_w2_2, final_norm_2,
):
    x = first_block(
        x, c, ctx, c_ctx, w_mod, b_mod, norm1_g, norm2_g, hg_w_in, hg_lb_fwd, hg_lb_bwd,
        hg_gnorm, hg_w_out, pool_w_in, pool_w_grp, pool_scale, pool_w_out, router_w, router_b,
        moe_w_gate, moe_w_up, moe_w_down, final_g,
    )
    return second_block(
        x, norm_mix_2, norm_ffn_2, ret_w_in_2, ret_q_norm_2, ret_k_norm_2, ret_gn_w_2,
        ret_gn_b_2, ret_w_out_2, conv_pw1_w_2, conv_pw1_b_2, conv_dw_w_2, conv_dw_b_2,
        conv_ln_w_2, conv_ln_b_2, conv_pw2_w_2, conv_pw2_b_2, sb_w_in_2, sb_q_norm_2,
        sb_k_norm_2, sb_w_out_2, ffn_w1_2, ffn_w2_2, final_norm_2,
    )


_drawn_inputs = setup_inputs


def setup_inputs(seed=0):
    import zlib

    import numpy as np

    out = dict(_drawn_inputs(seed))
    spreads = {}
    factors = {'ctx': 3.501,
     'c_ctx': 4.236,
     'hg_lb_fwd': 2.786,
     'hg_lb_bwd': 2.729,
     'ret_q_norm_2': 3.88,
     'ret_k_norm_2': 3.925,
     'ret_gn_w_2': 4.004,
     'ret_gn_b_2': 7.964,
     'conv_pw1_b_2': 8.0,
     'conv_dw_b_2': 5.817,
     'conv_ln_w_2': 5.491,
     'conv_ln_b_2': 8.0,
     'conv_pw2_b_2': 7.091,
     'sb_q_norm_2': 8.0,
     'sb_k_norm_2': 26.847,
     'final_norm_2': 8.208}
    for name, (base, spread) in spreads.items():
        noise = np.random.default_rng([zlib.crc32(name.encode()), seed]).standard_normal(out[name].shape)
        drawn = base * np.exp(spread * noise) if base else spread * noise
        out[name] = __import__('jax').numpy.asarray(drawn.astype(out[name].dtype))
    for name, factor in factors.items():
        out[name] = (out[name] * factor).astype(out[name].dtype)
    return out
```

```python
from contextlib import ExitStack

import concourse.bass as bass
from concourse import mybir

F32 = mybir.dt.float32
F32R = mybir.dt.float32r
I32 = mybir.dt.int32
ALU = mybir.AluOpType
ACT = mybir.ActivationFunctionType
AX = mybir.AxisListType.X
MUL, ADD, SUB = ALU.mult, ALU.add, ALU.subtract

D = 1024
EPS = 1e-6
NEG = -1e30

C_ID, C_ONE, C_BLK, C_SEL, C_MF, C_MB, C_RF, C_RB = 0, 128, 256, 384, 512, 640, 768, 1280
C_END = 1792
C_RET, C_COS, C_SIN, C_SB, C_LT = 1792, 3328, 3584, 3840, 4224
C_ALL = 4240

PARAMS = [
    [("c", 8), ("c_ctx", 8), ("norm1_g", 8), ("norm2_g", 8), ("hg_lb_fwd", 16), ("hg_lb_bwd", 16),
     ("b_mod", 48), ("hg_gnorm", 1)],
    [("norm_mix_2", 32), ("norm_ffn_2", 32), ("ret_q_norm_2", 4), ("ret_k_norm_2", 4), ("ret_gn_w_2", 32)],
    [("ret_gn_b_2", 32), ("conv_pw1_b_2", 16), ("conv_dw_b_2", 8), ("conv_ln_w_2", 8), ("conv_ln_b_2", 8),
     ("sb_q_norm_2", 1), ("sb_k_norm_2", 1)],
    [("conv_dw_w_2", 124)],
    [("conv_dw_w_2", 124)],
]


class Engine:

    def __init__(self, eng, sem):
        self.e, self.sem, self.n, self.seen = eng, sem, 0, {}

    def mark(self, ins):
        ins.then_inc(self.sem, 1)
        self.n += 1
        return (self.sem, self.n)

    def __call__(self, ins):
        t = self.mark(ins)
        self.wait(t)
        return t

    def now(self):
        return (self.sem, self.n)

    def wait(self, *tokens):
        for t in tokens:
            if t is not None and t[1] > self.seen.get(t[0], 0):
                self.e.wait_ge(t[0], t[1])
                self.seen[t[0]] = t[1]


def build(nc, I, out):
    with ExitStack() as ctx:
        sem = lambda n: ctx.enter_context(nc.semaphore(n))
        sb = lambda n, s, d=F32: ctx.enter_context(nc.sbuf_tensor(n, s, d))
        V, A, P, G, S = (Engine(e, sem(n)) for e, n in (
            (nc.vector, "s_dve"), (nc.scalar, "s_act"), (nc.tensor, "s_pe"), (nc.gpsimd, "s_pool"), (nc.sync, "s_sp")))
        ve, ac, pe, po = nc.vector, nc.scalar, nc.tensor, nc.gpsimd
        s_out = sem("s_out")

        bank = [ctx.enter_context(nc.psum_tensor(f"bank{i}", [128, 512], F32)) for i in range(8)]

        X = [sb(f"X{i}", [128, D])[:, :] for i in range(2)]
        NR, NS = 3, 3
        raw = [sb(f"raw{i}", [128, 2048]) for i in range(NR)]
        whi = [sb(f"whi{i}", [128, 2048], F32R) for i in range(NS)]
        wlo = [sb(f"wlo{i}", [128, 2048], F32R) for i in range(NS)]
        HH, HL = sb("HH", [128, 4096], F32R), sb("HL", [128, 4096], F32R)
        YH, YL = sb("YH", [128, 2048], F32R), sb("YL", [128, 2048], F32R)
        CST = sb("CST", [128, C_END])
        PRM = sb("PRM", [128, 560])
        SM = sb("SM", [128, 256])
        CS = sb("CS", [128, 32], F32R)
        ARENA = sb("ARENA", [128, 14600])
        ar = lambda o, n: ARENA[:, o:o + n]
        ident, ones, blk = CST[:, 0:128], CST[:, 128:256], CST[:, 256:384]
        f32 = lambda ap: ap.bitcast(F32)

        s_ld = [sem(f"s_ld{i}") for i in range(NR)]
        group = {}

        def small(dst, src, name):
            if name not in group:
                group[name] = [sem(f"s_{name}"), 0]
            g = group[name]
            nc.sync.dma_start(dst, src).then_inc(g[0], 16)
            g[1] += 16
            return (g[0], g[1])

        small(CST[:, :], I["consts"][:, 0:C_END], "in")
        col, pt, base = {}, [], 0
        for k, rows in enumerate(PARAMS):
            r, dst = 0, ar(4096 + 128 * k, 128)
            for name, n in rows:
                ap = I[name]
                if name == "conv_dw_w_2":
                    src = ap.rearrange("o w (t p) -> (o w t) p", p=128)[124 * (k - 3):124 * (k - 2), :]
                elif name in ("sb_q_norm_2", "sb_k_norm_2"):
                    small(dst[r:r + 1, 0:64], ap, "in")
                    src, dst2 = ap, dst[r:r + 1, 64:128]
                elif len(ap.shape) == 1:
                    src = ap.rearrange("(t p) -> t p", p=128)
                else:
                    src = ap.rearrange("o (t p) -> (o t) p", p=128)
                small(dst2 if name.startswith("sb_") else dst[r:r + n, :], src, "in")
                col.setdefault(name, base + r)
                r += n
            pt.append((dst, r, base))
            base += r
        for i in range(2):
            t_x = small(X[i][:, :], I["x"][0, 128 * i:128 * i + 128, :], "in")
        XC = [ar(12000 + 1024 * i, 1024) for i in range(2)]
        for i in range(2):
            t_in = small(XC[i], I["ctx"][0, 128 * i:128 * i + 128, :], "in")
        prm = lambda name, i, n=1: PRM[:, col[name] + i:col[name] + i + n]

        def kcols(w, k0, nk, n0, nn):
            return w[128 * k0:128 * (k0 + nk), n0:n0 + nn].rearrange("(k p) n -> p k n", p=128), nk, nn

        items = []

        def plan(w, k0, nk, n0, nn):
            items.append(kcols(w, k0, nk, n0, nn))

        wm, wi = I["w_mod"][0], I["hg_w_in"][0]

        def plan_mod(c):
            plan(wm, 0, 4, 512 * c, 512)
            plan(wm, 4, 4, 512 * c, 512)

        def plan_b(w, n0, count):
            for j in range(count):
                plan(w, 0, 8, n0 + 256 * j, 256)

        for c in range(4):
            plan_mod(c)
        plan_b(wi, 0, 4)
        for c in range(2):
            plan(wi, 0, 4, 1024 + 512 * c, 512)
            plan(wi, 4, 4, 1024 + 512 * c, 512)
        for u in range(8):
            plan_b(wi, 2048 + 1024 * (u % 2) + 256 * (u // 2), 1)
            plan_mod(4 + u)
        plan_b(wi, 4096, 4)

        def plan_a(w, nk, n0=0):
            for j in range(nk // 2):
                plan(w, 2 * j, 2, n0, 1024)

        plan_a(I["hg_w_out"][0], 8)
        for e in range(17):
            if e < 16:
                plan(I["moe_w_gate"][0, e], 0, 8, 0, 256)
                plan(I["moe_w_up"][0, e], 0, 8, 0, 256)
            if e:
                plan(I["moe_w_down"][0, e - 1], 0, 2, 0, 1024)

        def plan_ffn(i):
            for j in range(17):
                if j < 16:
                    plan(I["ffn_w1_2"][i], 0, 8, 256 * j, 256)
                if j:
                    plan(I["ffn_w2_2"][i], 2 * (j - 1), 2, 0, 1024)

        def plan_ret(i):
            w = I["ret_w_in_2"][i]
            plan_b(w, 0, 8)
            plan_a(w, 8, 2048)
            plan_a(w, 8, 3072)
            for h in range(5):
                if h < 4:
                    plan_b(w, 4096 + 512 * h, 2)
                if h:
                    for j in range(2):
                        plan(I["ret_w_out_2"][i], 4 * (h - 1) + 2 * j, 2, 0, 1024)

        plan_ret(0)
        plan_ffn(0)
        for j in range(4):
            plan_b(I["conv_pw1_w_2"][0], 256 * j, 1)
            plan_b(I["conv_pw1_w_2"][0], 1024 + 256 * j, 1)
        plan_a(I["conv_pw2_w_2"][0], 8)
        plan_ffn(1)
        plan_b(I["sb_w_in_2"][0], 0, 8)
        plan_a(I["sb_w_in_2"][0], 8, 2048)
        plan_a(I["sb_w_out_2"][0], 8)
        plan_ffn(2)
        plan_ret(1)
        plan_ffn(3)

        loaded, low, used = {}, {}, {}
        state = {"next": 0}

        def load(i):
            if i >= len(items):
                return
            src, nk, nn = items[i]
            S.wait(low.get(i - NR))
            nc.sync.dma_start(raw[i % NR][:, :].rearrange("p (k n) -> p k n", k=nk), src).then_inc(s_ld[i % NR], 16)
            loaded[i] = (s_ld[i % NR], 16 * (i // NR + 1))

        def split(i):
            if i >= len(items):
                return
            A.wait(loaded[i], used.get(i - NS))
            t = A.mark(ac.copy(whi[i % NS][:, :], raw[i % NR][:, :]))
            G.wait(t, loaded[i])
            low[i] = G.mark(po.tensor_tensor(wlo[i % NS][:, :], raw[i % NR][:, :], f32(whi[i % NS][:, :]), SUB))
            load(i + NR)

        for i in range(NR):
            load(i)

        def take():
            i = state["next"]
            state["next"] += 1
            if i == 0:
                for j in range(NS - 1):
                    split(j)
            split(i + NS - 1)
            P.wait(low[i])
            nk = items[i][1]
            return i, [w[i % NS][:, :].rearrange("p (k n) -> p k n", k=nk) for w in (whi, wlo)]

        def done(i, token):
            used[i] = token

        class Banks:

            def __init__(self, which):
                self.q = [(b, ()) for b in which]

            def get(self):
                b, toks = self.q.pop(0)
                P.wait(*toks)
                return b

            def put(self, b, *toks):
                self.q.append((b, toks))

        R = Banks([4, 5, 6, 7])
        acc_free = [()] * 4

        def mm3(ps, lh, ll, rh, rl, start, stop):
            pe.matmul(ps, lh, rh, start=start, stop=False)
            pe.matmul(ps, lh, rl, start=False, stop=False)
            return pe.matmul(ps, ll, rh, start=False, stop=stop)

        H8 = [h[:, 0:2048].rearrange("p (k n) -> p k n", k=8) for h in (HH, HL)]
        H16 = [h[:, :].rearrange("p (k n) -> p k n", k=8) for h in (HH, HL)]
        Y8 = [h[:, :].rearrange("p (k n) -> p k n", k=8) for h in (YH, YL)]

        def proj_b(acts=None, n=256):
            a = acts or H8
            bs = [R.get() for _ in range(n // 256)]
            i, w = take()
            for m in range(2):
                b = bs[m] if n == 512 else bs[0]
                ps = bank[b][:, 0:512] if n == 512 else bank[b][:, 256 * m:256 * m + 256]
                c = slice(128 * m, 128 * m + 128)
                for k in range(8):
                    last = mm3(ps, w[0][:, k, c], w[1][:, k, c], a[0][:, k, 0:n], a[1][:, k, 0:n], k == 0, k == 7)
            t = P.mark(last)
            done(i, t)
            return bs, t

        def proj_a(acts, k0, first, last_, ready=()):
            i, w = take()
            P.wait(*ready)
            for m in range(2):
                for h in range(2):
                    q = 2 * m + h
                    if first:
                        P.wait(*acc_free[q])
                    for k in range(2):
                        c = slice(128 * m, 128 * m + 128)
                        r = slice(512 * h, 512 * h + 512)
                        x = mm3(bank[q][:, :], acts[0][:, k0 + k, c], acts[1][:, k0 + k, c], w[0][:, k, r],
                                w[1][:, k, r], first and k == 0, last_ and k == 1)
            t = P.mark(x)
            done(i, t)
            return t

        V.wait(t_in)
        P.wait(t_in)
        A.wait(t_in)
        for k, (src, n, off) in enumerate(pt):
            b = R.get()
            t = P.mark(pe.transpose(bank[b][:, 0:n], src[0:n, :], ident[0:n, 0:n]))
            V.wait(t)
            R.put(b, V(ve.tensor_copy(PRM[:, off:off + n], bank[b][:, 0:n])))
        eps = SM[:, 0:1]
        V(ve.memset(eps, EPS))
        one = SM[:, 1:2]
        V(ve.memset(one, 1.0))
        t_prm = V.now()

        A.wait(t_prm)
        cs = SM[:, 2:18].rearrange("p (v k) -> p k v", v=2)
        A(ac.activation(SM[:, 2:18], prm("c", 0, 16), ACT.Silu))
        CSv = CS[:, :].rearrange("p (k v) -> p k v", v=4)
        A(ac.copy(CSv[:, :, 0:2], cs))
        V.wait(A.now())
        t_cs = V(ve.tensor_tensor(CSv[:, :, 2:4], cs, f32(CSv[:, :, 0:2]), SUB))

        LB, LB1 = SM[:, 18:34], SM[:, 34:50]
        for d, name in enumerate(("hg_lb_fwd", "hg_lb_bwd")):
            a0, a1 = prm(name, 0, 8), prm(name, 8, 8)
            mx, e0, e1 = SM[:, 50:58], SM[:, 58:66], SM[:, 66:74]
            V(ve.tensor_tensor(mx, a0, a1, ALU.max))
            V(ve.tensor_tensor(e0, a0, mx, SUB))
            V(ve.tensor_tensor(e1, a1, mx, SUB))
            A.wait(V.now())
            A(ac.activation(SM[:, 58:74], SM[:, 58:74], ACT.Exp))
            V.wait(A.now())
            V(ve.tensor_tensor(mx, e0, e1, ADD))
            V(ve.reciprocal(mx, mx))
            V(ve.tensor_tensor(LB[:, 8 * d:8 * d + 8], e0, mx, MUL))
            V(ve.tensor_tensor(LB1[:, 8 * d:8 * d + 8], e1, mx, MUL))

        MODT = SM[:, 80:144].rearrange("p (v t) -> p v t", t=16)
        MR = sb("MR", [4, 512])
        G1B, G2B = sb("G1B", [128, D]), sb("G2B", [128, D])
        TM = SM[:, 208:224]
        bm = I["b_mod"]
        t_gb = (small(G1B[:, :], bm[0:1, 2048:3072].to_broadcast([128, 1024]), "gate"),
                small(G2B[:, :], bm[0:1, 5120:6144].to_broadcast([128, 1024]), "gate"))[1]
        slot = {0: 0, 1: 1, 3: 2, 4: 3}

        def mod_chunk(c):
            b = R.get()
            P.wait(t_cs)
            for half in range(2):
                i, w = take()
                for k in range(4):
                    for r in range(2):
                        x = pe.matmul(bank[b][0:4, :], CSv[:, 4 * half + k, :], w[r][:, k, :],
                                      start=half == 0 and k == 0 and r == 0, stop=half == 1 and k == 3 and r == 1)
                t = P.mark(x)
                done(i, t)
            A.wait(t, P.now(), V.now())
            t = A(ac.copy(MR[:, :], bank[b][0:4, :]))
            R.put(b, t)
            which, half = c // 2, c % 2
            b = R.get()
            P.wait(t)
            if which in slot:
                for k in range(4):
                    x = pe.transpose(bank[b][:, 4 * k:4 * k + 4], MR[:, 128 * k:128 * k + 128], ident[0:4, 0:4])
                V.wait(P.mark(x))
                t = V(ve.tensor_copy(TM, bank[b][:, 0:16]))
                R.put(b, t)
                tm = TM.rearrange("p (k v) -> p k v", v=4)
                o = MODT[:, slot[which], 8 * half:8 * half + 8].rearrange("p (k v) -> p k v", v=2)
                V(ve.tensor_tensor(o, tm[:, :, 0:2], tm[:, :, 2:4], ADD))
                bb = prm("b_mod", 8 * which + 4 * half, 4).rearrange("p (k v) -> p k v", v=1).to_broadcast([128, 4, 2])
                V(ve.tensor_tensor(o, o, bb, ADD))
            else:
                x = pe.matmul(bank[b][:, :], CST[0:4, C_SEL:C_SEL + 128], MR[:, :], start=True, stop=True)
                V.wait(P.mark(x), t_gb)
                g = (G1B if which == 2 else G2B)[:, 512 * half:512 * half + 512]
                R.put(b, V(ve.tensor_tensor(g, g, bank[b][:, :], ADD)))

        for c in range(4):
            mod_chunk(c)
        MS = SM[:, 224:256]
        for v in range(2):
            sc = MODT[:, 1, :].rearrange("p (t v) -> p v t", v=2)[:, v, :]
            V(ve.scalar_tensor_tensor(MS[:, 8 * v:8 * v + 8], sc, 1.0, prm("norm1_g", 0, 8), ADD, MUL))
        sh1 = MODT[:, 0, :].rearrange("p (t v) -> p v t", v=2)

        XN = [ar(1024 * i, 1024) for i in range(2)]
        FT = ar(2048, 2048).rearrange("p (k n) -> p k n", k=8)
        ST = sb("ST", [128, 8])

        def rstd(xs, t=()):
            A.wait(*t, V.now(), P.now())
            for i in range(2):
                A(ac.activation(XN[i], xs[i], ACT.Square, accum_out=ST[:, i:i + 1]))
            A(ac.activation(ST[:, 0:2], ST[:, 0:2], ACT.Sqrt, bias=eps, scale=1.0 / D))
            V.wait(A.now())
            V(ve.reciprocal(ST[:, 2:4], ST[:, 0:2]))

        def norm(xs, scale, shift, dst, t=()):
            rstd(xs, t)
            A.wait(V.now())
            t1 = A(ac.mul(XN[1], xs[1], ST[:, 3:4]))
            t0 = V(ve.tensor_scalar(XN[0], xs[0], ST[:, 2:3], None, MUL))
            P.wait(t0, t1)
            ta = []

            def low_part(q):
                kk = slice(2 * q, 2 * q + 2)
                V.wait(ta[q])
                V(ve.tensor_tensor(dst[1][:, kk, :], FT[:, kk, :], f32(dst[0][:, kk, :]), SUB))

            for q in range(4):
                b = R.get()
                for m in range(2):
                    for i in range(2):
                        k = 2 * q + m
                        x = pe.transpose(bank[b][:, 256 * m + 128 * i:256 * m + 128 * i + 128],
                                         XN[i][:, 128 * k:128 * k + 128], ident)
                V.wait(P.mark(x))
                for m in range(2):
                    k = 2 * q + m
                    ps = bank[b][:, 256 * m:256 * m + 256]
                    if shift is None:
                        V.mark(ve.tensor_scalar(FT[:, k, :], ps, scale[:, k:k + 1], None, MUL))
                    else:
                        V.mark(ve.tensor_scalar(FT[:, k, :], ps, scale[:, k:k + 1], shift[:, k:k + 1], MUL, ADD))
                R.put(b, V.now())
                A.wait(V.now())
                ta.append(A.mark(ac.copy(dst[0][:, 2 * q:2 * q + 2, :], FT[:, 2 * q:2 * q + 2, :])))
                if q:
                    low_part(q - 1)
            low_part(3)
            P.wait(V.now())

        def hi_lo(hi, lo, src):
            A.wait(V.now())
            V.wait(A.mark(ac.copy(hi, src)))
            return V(ve.tensor_tensor(lo, src, f32(hi), SUB))

        norm(X, MS[:, 0:8], sh1[:, 0, :], [h[:, :, 0:256] for h in H16])
        norm(XC, MS[:, 8:16], sh1[:, 1, :], [h[:, :, 256:512] for h in H16])

        QO = ar(0, 2048).rearrange("p (t n) -> p t n", t=8)
        VT = ar(2048, 4096).rearrange("p (i n) -> p i n", i=4)
        o0 = 6144
        kk_ = ar(o0, 1024).rearrange("p (h n) -> p h n", h=2)
        cum = ar(o0 + 1024, 1024).rearrange("p (h n) -> p h n", h=2)
        tmp = ar(o0 + 2048, 1024).rearrange("p (h n) -> p h n", h=2)
        KDT = ar(o0 + 3072, 1024).rearrange("p (h i n) -> p h i n", h=2, i=4)
        QE = ar(o0 + 4096, 512).rearrange("p (h n) -> p h n", h=2)
        KE = ar(o0 + 4608, 512).rearrange("p (h n) -> p h n", h=2)
        QI = ar(o0 + 5120, 512).rearrange("p (h n) -> p h n", h=2)
        SA = ar(o0 + 5632, 1024).rearrange("p (h i n) -> p h i n", h=2, i=4)
        SC = [ar(o0 + 6656 + 512 * i, 512) for i in range(2)]
        DEC = sb("DEC", [128, 16])

        A.wait(V.now(), P.now())
        V.wait(A.now(), P.now())
        for d in range(2):
            V(ve.memset(SC[d], 0.0))
        for j in range(4):
            (b,), t = proj_b(H16)
            A.wait(t)
            t = A(ac.activation(QO[:, 2 * j:2 * j + 2, :], bank[b][:, :], ACT.Silu))
            R.put(b, t)
        for c in range(2):
            for half in range(2):
                i, w = take()
                for m in range(4):
                    if half == 0:
                        P.wait(*acc_free[m])
                    for k in range(4):
                        q = 4 * half + k
                        cc = slice(128 * m, 128 * m + 128)
                        x = mm3(bank[m][:, :], H16[0][:, q, cc], H16[1][:, q, cc], w[0][:, k, :], w[1][:, k, :],
                                q == 0, q == 7)
                t = P.mark(x)
                done(i, t)
            A.wait(t)
            V.wait(t)
            for m in range(4):
                dst = VT[:, m, 512 * c:512 * c + 512]
                if m % 2:
                    acc_free[m] = (A(ac.copy(dst, bank[m][:, :])),)
                else:
                    acc_free[m] = (V(ve.tensor_copy(dst, bank[m][:, :])),)
        t_v = (A.now(), V.now())

        zq = {}

        def unit_proj(u):
            zq[u] = proj_b(H16, 512)

        def unit_vec(u):
            p, d = u // 2, u % 2
            bs, t = zq[u]
            A.wait(t, V.now(), P.now())
            for h in range(2):
                A.mark(ac.activation(kk_[:, h, :], bank[bs[h]][:, :], ACT.Sigmoid, scale=-1.0))
                A.mark(ac.activation(cum[:, h, :], bank[bs[h]][:, :], ACT.Sigmoid))
                R.put(bs[h], A.now())
            V.wait(A.now())
            for h in range(2):
                q = 8 * d + 2 * p + h
                V.mark(ve.tensor_scalar(cum[:, h, :], cum[:, h, :], LB1[:, q:q + 1], LB[:, q:q + 1], MUL, ADD))
                V.mark(ve.tensor_scalar(kk_[:, h, :], kk_[:, h, :], LB1[:, q:q + 1], None, MUL))
            A.wait(V.now())
            A(ac.activation(tmp, cum, ACT.Ln))
            V.wait(A.now(), V.now())
            for h in range(2):
                if d == 0:
                    V(ve.tensor_tensor_scan(cum[:, h, :], CST[:, C_RF:C_RF + 512], tmp[:, h, :], 0.0, MUL, ADD))
                else:
                    V(ve.tensor_tensor_scan(cum[:, h, ::-1], CST[:, C_RB + 511:C_RB - 1:-1], tmp[:, h, ::-1], 0.0,
                                            MUL, ADD))
            cl = cum[:, :, 0:256].rearrange("p h (c n) -> p h c n", c=4)
            tl = tmp[:, :, 0:256].rearrange("p h (c n) -> p h c n", c=4)
            bc = lambda i: cl[:, :, :, i:i + 1].to_broadcast([128, 2, 4, 64])
            ref, last = (31, 63) if d == 0 else (32, 0)
            A.wait(V.now())
            A(ac.activation(DEC[:, 8 * d:8 * d + 8].rearrange("p (h c) -> p h c", h=2), cl[:, :, :, last], ACT.Exp))
            A(ac.activation(QI, cum[:, :, 0:256], ACT.Exp))
            V.wait(A.now())
            V(ve.tensor_tensor(QI, QI, QO[:, 2 * p:2 * p + 2, :], MUL))
            V(ve.tensor_tensor(tl, cl, bc(ref), SUB))
            A.wait(V.now())
            A(ac.activation(QE, tmp[:, :, 0:256], ACT.Exp))
            A(ac.activation(KE, tmp[:, :, 0:256], ACT.Exp, scale=-1.0))
            V.wait(A.now())
            V(ve.tensor_tensor(QE, QE, QO[:, 2 * p:2 * p + 2, :], MUL))
            t_qe = V(ve.tensor_tensor(KE, KE, kk_[:, :, 0:256], MUL))
            V(ve.tensor_tensor(tl, cl, bc(last), SUB))
            lc = 511 if d == 0 else 256
            V(ve.tensor_tensor(tmp[:, :, 256:512], cum[:, :, 256:512],
                               cum[:, :, lc:lc + 1].to_broadcast([128, 2, 256]), SUB))
            A.wait(V.now())
            A(ac.activation(tmp, tmp, ACT.Exp, scale=-1.0))
            V.wait(A.now())
            t_kd = V(ve.tensor_tensor(tmp, tmp, kk_, MUL))
            return t_qe, t_kd

        def unit_scores(u, t_qe, t_kd):
            d = u % 2
            P.wait(t_qe)
            b = R2.get()
            for h in range(2):
                for j in range(2):
                    s = slice(128 * j, 128 * j + 128)
                    q = 2 * h + j
                    x = pe.matmul(bank[b][:, 128 * q:128 * q + 128], KE[:, h, s], QE[:, h, s],
                                  start=True, stop=True)
            t = P.mark(x)
            P.wait(t_kd)
            bs = []
            for h in range(2):
                bb = R2.get()
                for i in range(4):
                    x = pe.transpose(bank[bb][:, 128 * i:128 * i + 128], tmp[:, h, 128 * i:128 * i + 128], ident)
                bs.append((bb, P.mark(x)))
            V.wait(t)
            m = CST[:, (C_MF, C_MB)[d]:(C_MF, C_MB)[d] + 128].bitcast(I32)
            mb = m.rearrange("p (q n) -> p q n", q=1).to_broadcast([128, 4, 128])
            t = V(ve.copy_predicated(SC[d].rearrange("p (q n) -> p q n", q=4), mb,
                                     bank[b][:, :].rearrange("p (q n) -> p q n", q=4)))
            R2.put(b, t)
            A.wait(bs[0][1])
            R2.put(bs[0][0], A(ac.copy(KDT[:, 0, :, :], bank[bs[0][0]][:, :])))
            V.wait(bs[1][1])
            R2.put(bs[1][0], V(ve.tensor_copy(KDT[:, 1, :, :], bank[bs[1][0]][:, :])))
            return t

        def unit_state(u):
            p, d = u // 2, u % 2
            P.wait(V.now(), A.now())
            order = [0, 1, 2] if d == 0 else [3, 2, 1]
            for h in range(2):
                b = R2.get()
                hc = slice(128 * (2 * p + h), 128 * (2 * p + h) + 128)
                for i in range(2):
                    x = pe.matmul(bank[b][:, 0:128], KDT[:, h, 2 + i, :], VT[:, 2 + i, hc], start=i == 0, stop=i == 1)
                for n, c in sorted(enumerate(order), key=lambda nc_: nc_[1] % 2):
                    r = slice(64 * (c % 2), 64 * (c % 2) + 64)
                    P.wait(P.mark(x))
                    x = pe.matmul(bank[b][:, 128 * (n + 1):128 * (n + 2)], KDT[r, h, c // 2, :], VT[r, c // 2, hc],
                                  start=True, stop=True)
                V.wait(P.mark(x))
                V(ve.tensor_copy(SA[:, h, 0, :], bank[b][:, 0:128]))
                for n, c in enumerate(order):
                    V(ve.scalar_tensor_tensor(SA[:, h, n + 1, :], SA[:, h, n, :],
                                              DEC[:, 8 * d + 4 * h + c:8 * d + 4 * h + c + 1],
                                              bank[b][:, 128 * (n + 1):128 * (n + 2)], MUL, ADD))
                R2.put(b, V.now())

        def unit_out(u):
            p, d = u // 2, u % 2
            P.wait(V.now())
            if d == 0:
                P.wait(*acc_free[0])
            first = d == 0
            order = [0, 1, 2, 3] if d == 0 else [3, 2, 1, 0]
            for h in range(2):
                hc = slice(128 * (2 * p + h), 128 * (2 * p + h) + 128)
                for j in range(2):
                    q = 2 * h + j
                    pe.matmul(bank[0][:, 128 * q:128 * q + 128], VT[:, j, hc], SC[d][:, 128 * q:128 * q + 128],
                              start=first, stop=False, skip_group_check=True)
                    first = False
                for n, c in enumerate(order):
                    x = pe.matmul(bank[0][:, 256 * h + 64 * c:256 * h + 64 * c + 64], SA[:, h, n, :],
                                  QI[:, h, 64 * c:64 * c + 64], start=False,
                                  stop=d == 1 and h == 1 and n == 3, skip_group_check=True)
            t = P.mark(x)
            if d == 1:
                V.wait(t)
                acc_free[0] = (V(ve.tensor_copy(QO[:, 2 * p:2 * p + 2, :], bank[0][:, :])),)

        acc_free[0] = acc_free[0] + t_v
        R2 = Banks([])
        for q in (1, 2, 3):
            R2.put(q, *acc_free[q])
        for u in range(9):
            if u < 8:
                unit_proj(u)
            if u:
                unit_scores(u - 1, *tk)
                unit_state(u - 1)
                unit_out(u - 1)
            if u < 8:
                tk = unit_vec(u)
                mod_chunk(4 + u)

        for q, toks in R2.q:
            acc_free[q] = toks

        SQ = ar(o0, 2048).rearrange("p (t n) -> p t n", t=8)
        RS = ar(o0 + 2048, 2048).rearrange("p (t n) -> p t n", t=8)
        A.wait(V.now(), P.now())
        A(ac.activation(SQ, QO, ACT.Square))
        P.wait(A.now())
        for j in range(4):
            b = R.get()
            t = P.mark(pe.matmul(bank[b][:, :], ones, SQ[:, 2 * j:2 * j + 2, :], start=True, stop=True))
            A.wait(t)
            R.put(b, A(ac.activation(RS[:, 2 * j:2 * j + 2, :], bank[b][:, :], ACT.Sqrt, bias=eps, scale=1.0 / 128)))
        V.wait(A.now())
        V(ve.reciprocal(RS, RS))
        V(ve.scalar_tensor_tensor(QO, QO, prm("hg_gnorm", 0), RS, MUL, MUL))
        SG = SQ
        A.wait(V.now(), P.now())
        for j in range(4):
            (b,), t = proj_b(H16)
            A.wait(t)
            t = A(ac.activation(SG[:, 2 * j:2 * j + 2, :], bank[b][:, :], ACT.Silu))
            R.put(b, t)
            V.wait(t)
            s = slice(2 * j, 2 * j + 2)
            V(ve.tensor_tensor(QO[:, s, :], QO[:, s, :], SG[:, s, :], MUL))
            t_y = hi_lo(Y8[0][:, s, :], Y8[1][:, s, :], QO[:, s, :])

        TMPA = sb("TMPA", [128, 512])

        def add_out(t, gate=None, bias=None):
            V.wait(t)
            for q in range(4):
                m, h = q // 2, q % 2
                x = X[m][:, 512 * h:512 * h + 512]
                g = slice(512 * h, 512 * h + 512)
                if gate is not None:
                    acc_free[q] = (V(ve.tensor_tensor(TMPA[:, :], bank[q][:, :], gate[:, g], MUL)),)
                    V(ve.tensor_tensor(x, x, TMPA[:, :], ADD))
                else:
                    acc_free[q] = (V(ve.tensor_tensor(x, x, bank[q][:, :], ADD)),)
                    if bias is not None:
                        V(ve.tensor_tensor(x, x, bias[:, g], ADD))

        for j in range(4):
            t = proj_a(Y8, 2 * j, j == 0, j == 3, (t_y,))
        add_out(t, gate=G1B[:, :])

        V(ve.scalar_tensor_tensor(MS[:, 16:24], MODT[:, 3, :].rearrange("p (t v) -> p v t", v=2)[:, 0, :], 1.0,
                                  prm("norm2_g", 0, 8), ADD, MUL))
        sh2 = MODT[:, 2, :].rearrange("p (t v) -> p v t", v=2)[:, 0, :]
        norm(X, MS[:, 16:24], sh2, H8)

        o0 = 4096
        RW = ar(o0, 128)
        RB = ar(o0 + 128, 16)
        LT = ar(o0 + 144, 16)
        S.wait(V.now(), A.now(), P.now())
        small(RW, I["router_w"].rearrange("(k p) e -> p k e", p=128), "router")
        small(RB, I["router_b"].rearrange("(o e) -> o e", o=1).to_broadcast([128, 16]), "router")
        t_r = small(LT, I["consts"][:, C_LT:C_LT + 16], "router")
        FG = ar(o0 + 7424, 1024)
        t_g = small(FG, I["final_g"].rearrange("(o n) -> o n", o=1).to_broadcast([128, 1024]), "first")
        CB = ar(o0 + 256, 4096).rearrange("p (e n) -> p e n", e=16)
        o0 = o0 + 256 + 4096
        z = lambda k, n=16: ar(o0 + 64 * k, n)
        rw = RW.rearrange("p (k e) -> p k e", k=8)
        b = R.get()
        P.wait(t_r)
        for i in range(2):
            for k in range(8):
                x = pe.matmul(bank[b][:, 16 * i:16 * i + 16], FT[:, k, 128 * i:128 * i + 128], rw[:, k, :],
                              start=k == 0, stop=k == 7)
        t = P.mark(x)
        A.wait(t, V.now())
        sg = z(0, 32)
        t = A(ac.activation(sg, bank[b][:, 0:32], ACT.Sigmoid))
        R.put(b, t)
        V.wait(t, t_r)
        cmb = z(1, 32)

        def rank(dst, v, n, tie, c1, c2):
            g = v.shape[1]
            vi = v.rearrange("p g (i j) -> p g i j", j=1).to_broadcast([128, g, n, n])
            vj = v.rearrange("p g (i j) -> p g i j", i=1).to_broadcast([128, g, n, n])
            tt = tie.rearrange("p (g i j) -> p g i j", g=1, i=n).to_broadcast([128, g, n, n])
            V(ve.tensor_tensor(c1, vj, vi, ALU.is_gt))
            V(ve.tensor_tensor(c2, vj, vi, ALU.is_equal))
            V(ve.tensor_tensor(c2, c2, tt, MUL))
            V(ve.tensor_tensor(c1, c1, c2, ADD))
            V(ve.tensor_reduce(dst, c1, AX, ADD))

        for i in range(2):
            s = sg[:, 16 * i:16 * i + 16]
            sel = z(2).rearrange("p (g e) -> p g e", g=4)
            c1 = z(3, 64).rearrange("p (g i j) -> p g i j", g=4, i=4)
            c2 = z(4, 64).rearrange("p (g i j) -> p g i j", g=4, i=4)
            rk = z(5).rearrange("p (g e) -> p g e", g=4)
            V(ve.tensor_tensor(z(2), s, RB, ADD))
            rank(rk, sel, 4, LT, c1, c2)
            V(ve.tensor_scalar(rk, rk, 1.5, None, ALU.is_lt))
            V(ve.tensor_tensor(sel, sel, rk, MUL))
            gs = z(6, 4)
            V(ve.tensor_reduce(gs, sel, AX, ADD))
            gr = z(7, 4)
            rank(gr.rearrange("p (g e) -> p g e", g=1), gs.rearrange("p (g e) -> p g e", g=1), 4, LT,
                 c1[:, 0:1], c2[:, 0:1])
            V(ve.tensor_scalar(gr, gr, 0.5, None, ALU.is_lt))
            V(ve.tensor_tensor(rk, rk, gr.rearrange("p (g e) -> p g e", e=1).to_broadcast([128, 4, 4]), MUL))
            V(ve.tensor_tensor(z(5), z(5), s, MUL))
            V(ve.tensor_reduce(z(8, 1), z(5), AX, ADD))
            V(ve.reciprocal(z(8, 1), z(8, 1)))
            V(ve.tensor_scalar(cmb[:, 16 * i:16 * i + 16], z(5), z(8, 1), None, MUL))
        P.wait(V.now())
        for q in range(8):
            b = R.get()
            for m in range(2):
                for i in range(2):
                    e = 2 * q + m
                    w = cmb[:, 16 * i + e:16 * i + e + 1].to_broadcast([128, 128])
                    x = pe.matmul(bank[b][:, 256 * m + 128 * i:256 * m + 128 * i + 128], w, ident, start=True, stop=True)
            A.wait(P.mark(x))
            R.put(b, A(ac.copy(CB[:, 2 * q:2 * q + 2, :], bank[b][:, :])))
        t_cb = A.now()
        V.wait(t_cb)

        o0 = o0 + 1024
        TG = [ar(o0 + 1024 * i, 512).rearrange("p (m n) -> p m n", m=2) for i in range(2)]
        TU = [ar(o0 + 1024 * i + 512, 512).rearrange("p (m n) -> p m n", m=2) for i in range(2)]
        ring_y = {}

        def yslot(n):
            s = 2 * (n % 4)
            return Y8[0][:, s:s + 2, :], Y8[1][:, s:s + 2, :]

        for e in range(17):
            if e < 16:
                (b,), tg = proj_b()
                A.wait(tg, ring_y.get(("v", e - 2)))
                tg = A.mark(ac.activation(TG[e % 2], bank[b][:, :], ACT.Silu))
                R.put(b, tg)
                (b,), tu = proj_b()
                V.wait(tg, tu)
                R.put(b, V(ve.tensor_tensor(TU[e % 2], TG[e % 2], bank[b][:, :], MUL)))
                cb = CB[:, e:e + 1, :].to_broadcast([128, 2, 256])
                V(ve.tensor_tensor(TU[e % 2], TU[e % 2], cb, MUL))
                A.wait(ring_y.get(("p", e - 4)))
                V.wait(ring_y.get(("p", e - 4)))
                hi, lo = yslot(e)
                ring_y["v", e] = hi_lo(hi, lo, TU[e % 2])
            if e:
                t = proj_a(Y8, 2 * ((e - 1) % 4), e == 1, e == 16, (ring_y["v", e - 1],))
                ring_y["p", e - 1] = t
        V.wait(t_g)
        add_out(t, gate=G2B[:, :])
        rstd(X)
        for i in range(2):
            V(ve.scalar_tensor_tensor(X[i], X[i], ST[:, 2 + i:3 + i], FG, MUL, MUL))

        def ffn(i):
            norm(X, prm("norm_ffn_2", 8 * i, 8), None, H8)
            ry = {}
            for j in range(17):
                if j < 16:
                    (b,), t = proj_b()
                    tr, th = TG[j % 2], TU[j % 2]
                    A.wait(t, ry.get(("v", j - 2)))
                    t = A(ac.activation(tr, bank[b][:, :], ACT.Relu))
                    R.put(b, t)
                    hi, lo = yslot(j)
                    A.wait(ry.get(("p", j - 4)))
                    th_ = A.mark(ac.activation(hi, tr, ACT.Square))
                    V.wait(t)
                    V(ve.tensor_tensor(th, tr, tr, MUL))
                    V.wait(th_, ry.get(("p", j - 4)))
                    ry["v", j] = V(ve.tensor_tensor(lo, th, f32(hi), SUB))
                if j:
                    t = proj_a(Y8, 2 * ((j - 1) % 4), j == 1, j == 16, (ry["v", j - 1],))
                    ry["p", j - 1] = t
            add_out(t)

        def head_norm(src_ps, gain, m_ones, width, dst, t, sq):
            A.wait(t, V.now())
            ta = A(ac.activation(sq, src_ps, ACT.Square))
            V.wait(t, ta)
            for m in range(2):
                V.mark(ve.tensor_scalar(dst[:, m, :], src_ps[:, 256 * m:256 * m + 256], gain[m], None, MUL))
            return ta, V.now()

        def ret(i, li):
            norm(X, prm("norm_mix_2", 8 * li, 8), None, H8)
            o = 4096
            QK = [ar(2048 * s, 2048).rearrange("p (h m n) -> p h m n", h=4, m=2) for s in range(2)]
            VV = ar(o, 4096).rearrange("p (i n) -> p i n", i=2)
            RM = ar(o + 4096, 1536).rearrange("p (h n) -> p h n", h=4)
            COS, SIN = ar(o + 5632, 256), ar(o + 5888, 256)
            SQ2 = ar(o + 6144, 512)
            RSD = ar(o + 6656, 256)
            M1, M2 = ar(o + 6912, 512), ar(o + 7424, 512)
            QG = ar(o + 7936, 512).rearrange("p (m n) -> p m n", m=2)
            o2 = o + 8448
            PP = SQ2[:, 0:384]
            SGT = ar(o2, 1024).rearrange("p (t n) -> p t n", t=4)
            YN = [ar(o2 + 1024 + 512 * s, 512) for s in range(2)]
            YT = ar(o + 6912, 1024).rearrange("p (t n) -> p t n", t=4)
            S.wait(V.now(), A.now(), P.now())
            t_c = small(ar(o + 4096, 2048), I["consts"][:, C_RET:C_RET + 2048], f"ret{i}")
            V.wait(t_c, P.now(), A.now())
            A.wait(P.now(), V.now())
            cosb = COS.rearrange("p (m n) -> p m n", m=1).to_broadcast([128, 2, 256])
            sinb = SIN.rearrange("p (m n) -> p m n", m=1).to_broadcast([128, 2, 256])
            m1, m2 = (x.rearrange("p (m n) -> p m n", m=2) for x in (M1, M2))
            pend = None

            def rotate(h8, sq_t):
                s, h = h8 // 4, h8 % 4
                b = R.get()
                P.wait(sq_t)
                for m in range(2):
                    x = pe.matmul(bank[b][:, 0:256], ones, SQ2[:, 256 * m:256 * m + 256], start=m == 0, stop=m == 1)
                A.wait(P.mark(x), V.now())
                t = A(ac.activation(RSD, bank[b][:, 0:256], ACT.Sqrt, bias=eps, scale=1.0 / 256))
                R.put(b, t)
                V.wait(t)
                V(ve.reciprocal(RSD, RSD))
                V(ve.tensor_tensor(QG, QG, RSD.rearrange("p (m n) -> p m n", m=1).to_broadcast([128, 2, 256]), MUL))
                V.mark(ve.tensor_tensor(m1, QG, cosb, MUL))
                V(ve.tensor_tensor(m2, QG, sinb, MUL))
                dst = QK[s][:, h, :, :]
                V(ve.tensor_tensor(dst[:, 0, :], m1[:, 0, :], m2[:, 1, :], SUB))
                V(ve.tensor_tensor(dst[:, 1, :], m2[:, 0, :], m1[:, 1, :], ADD))

            for h8 in range(9):
                if h8 < 8:
                    bs, t = proj_b()
                if pend is not None:
                    rotate(*pend)
                if h8 < 8:
                    g = [prm(("ret_q_norm_2", "ret_k_norm_2")[h8 // 4], 2 * i + m) for m in range(2)]
                    A.wait(P.now())
                    ta, tv = head_norm(bank[bs[0]][:, :], g, ones, 256, QG, t, SQ2)
                    V.wait(V.now())
                    R.put(bs[0], ta, tv)
                    pend = (h8, ta)
            for c in range(2):
                for j in range(4):
                    t = proj_a(H8, 2 * j, j == 0, j == 3)
                A.wait(t)
                V.wait(t)
                for q in range(4):
                    m, h = q // 2, q % 2
                    dst = VV[:, m, 1024 * c + 512 * h:1024 * c + 512 * h + 512]
                    if q % 2:
                        acc_free[q] = (A(ac.copy(dst, bank[q][:, :])),)
                    else:
                        acc_free[q] = (V(ve.tensor_copy(dst, bank[q][:, :])),)
            t_vv = (A.now(), V.now())
            t_yl = None
            for h in range(5):
                if h < 4:
                    b = R.get()
                    P.wait(*t_vv, V.now())
                    q, k = QK[0][:, h, :, :], QK[1][:, h, :, :]
                    for m in range(2):
                        pe.matmul(bank[b][:, 0:256], k[:, m, 0:128], q[:, m, :], start=m == 0, stop=m == 1)
                    for m in range(2):
                        x = pe.matmul(bank[b][:, 256:384], k[:, m, 128:256], q[:, m, 128:256], start=m == 0, stop=m == 1)
                    t = P.mark(x)
                    V.wait(t)
                    t_p = V(ve.tensor_tensor(PP, bank[b][:, 0:384], RM[:, h, :], MUL))
                    R.put(b, t_p)
                    for j in range(2):
                        (b,), t = proj_b()
                        A.wait(t, V.now())
                        R.put(b, A(ac.activation(SGT[:, 2 * j:2 * j + 2, :], bank[b][:, :], ACT.Silu)))
                    vc = slice(512 * h, 512 * h + 512)
                    P.wait(t_p)
                    by = [R.get(), R.get()]
                    x = pe.matmul(bank[by[0]][:, :], PP[:, 0:128], VV[:, 0, vc], start=True, stop=True)
                    ty0 = P.mark(x)
                    pe.matmul(bank[by[1]][:, :], PP[:, 128:256], VV[:, 0, vc], start=True, stop=False)
                    x = pe.matmul(bank[by[1]][:, :], PP[:, 256:384], VV[:, 1, vc], start=False, stop=True)
                    ty1 = P.mark(x)
                    for m in range(2):
                        V.wait((ty0, ty1)[m])
                        V(ve.bn_stats(SM[:, 208:214], bank[by[m]][:, :]))
                        V(ve.bn_aggr(SM[:, 214 + 2 * m:216 + 2 * m], SM[:, 208:214]))
                    A.wait(V.now())
                    for m in range(2):
                        A(ac.activation(SM[:, 218 + m:219 + m], SM[:, 215 + 2 * m:216 + 2 * m], ACT.Sqrt, bias=eps))
                    V.wait(A.now())
                    V(ve.reciprocal(SM[:, 218:220], SM[:, 218:220]))
                    for m in range(2):
                        t = V(ve.tensor_scalar(YN[m], bank[by[m]][:, :], SM[:, 214 + 2 * m:215 + 2 * m],
                                               SM[:, 218 + m:219 + m], SUB, MUL))
                        R.put(by[m], t)
                if h:
                    for j in range(2):
                        k0 = 4 * ((h - 1) % 2) + 2 * j
                        t_o = proj_a(Y8, k0, h == 1 and j == 0, h == 4 and j == 1, (t_yl,))
                if h < 4:
                    P.wait(t)
                    for jj in range(2):
                        b = R.get()
                        for m in range(2):
                            for s in range(2):
                                f = 2 * jj + m
                                x = pe.transpose(bank[b][:, 256 * m + 128 * s:256 * m + 128 * s + 128],
                                                 YN[s][:, 128 * f:128 * f + 128], ident)
                        A.wait(P.mark(x), V.now())
                        for m in range(2):
                            f = 4 * h + 2 * jj + m
                            A.mark(ac.activation(YT[:, 2 * jj + m, :], bank[b][:, 256 * m:256 * m + 256], ACT.Identity,
                                                 scale=prm("ret_gn_w_2", 16 * i + f), bias=prm("ret_gn_b_2", 16 * i + f)))
                        R.put(b, A.now())
                    V.wait(A.now())
                    V(ve.tensor_tensor(YT, YT, SGT, MUL))
                    A.wait(P.now())
                    V.wait(P.now())
                    s = slice(4 * (h % 2), 4 * (h % 2) + 4)
                    t_yl = hi_lo(Y8[0][:, s, :], Y8[1][:, s, :], YT)
            add_out(t_o)

        ret(0, 0)
        ffn(0)

        norm(X, prm("norm_mix_2", 8, 8), None, H8)
        o = 4096
        HP = ar(o, 2288).rearrange("p (t n) -> p t n", t=8)
        CA = ar(o + 2288, 2048).rearrange("p (t n) -> p t n", t=8)
        CG = ar(o + 4336, 512).rearrange("p (m n) -> p m n", m=2)
        CQ = ar(o + 4848, 2048).rearrange("p (t n) -> p t n", t=8)
        BO = ar(o + 6896, 1024)
        LR = ar(o + 7920, 256)
        S.wait(V.now(), A.now(), P.now())
        t_bo = small(BO, I["conv_pw2_b_2"].to_broadcast([128, 1024]), "conv")
        V.wait(P.now(), A.now())
        A.wait(P.now(), V.now())
        V(ve.memset(HP[:, :, 0:30], 0.0))
        for j in range(4):
            (ba,), ta = proj_b()
            (bg,), tg = proj_b()
            A.wait(tg, V.now())
            for m in range(2):
                A.mark(ac.activation(CG[:, m, :], bank[bg][:, 256 * m:256 * m + 256], ACT.Sigmoid,
                                     bias=prm("conv_pw1_b_2", 8 + 2 * j + m)))
            R.put(bg, A.now())
            V.wait(ta, A.now())
            for m in range(2):
                f = 2 * j + m
                V(ve.scalar_tensor_tensor(HP[:, f, 30:286], bank[ba][:, 256 * m:256 * m + 256],
                                          prm("conv_pw1_b_2", f), CG[:, m, :], ADD, MUL))
            R.put(ba, V.now())
            for m in range(2):
                f = 2 * j + m
                V(ve.tensor_scalar(CA[:, f, :], HP[:, f, 0:256], prm("conv_dw_w_2", f), prm("conv_dw_b_2", f), MUL, ADD))
                for w in range(1, 31):
                    V(ve.scalar_tensor_tensor(CA[:, f, :], HP[:, f, w:w + 256], prm("conv_dw_w_2", 8 * w + f),
                                              CA[:, f, :], MUL, ADD))

        def col_mean(src):
            b = R.get()
            for k in range(8):
                x = pe.matmul(bank[b][:, 0:256], ones, src[:, k, :], start=k == 0, stop=k == 7)
            return b, P.mark(x)

        P.wait(V.now())
        b, t = col_mean(CA)
        A.wait(t, V.now())
        t = A(ac.mul(LR, bank[b][:, 0:256], 1.0 / D))
        R.put(b, t)
        V.wait(t)
        lrb = LR.rearrange("p (t n) -> p t n", t=1).to_broadcast([128, 8, 256])
        V(ve.tensor_tensor(CA, CA, lrb, SUB))
        A.wait(V.now())
        A(ac.activation(CQ, CA, ACT.Square))
        P.wait(A.now())
        b, t = col_mean(CQ)
        A.wait(t)
        t = A(ac.activation(LR, bank[b][:, 0:256], ACT.Sqrt, bias=eps, scale=1.0 / D))
        R.put(b, t)
        V.wait(t)
        V(ve.reciprocal(LR, LR))
        V(ve.tensor_tensor(CA, CA, lrb, MUL))
        A.wait(V.now(), P.now())
        for f in range(8):
            A.mark(ac.activation(CQ[:, f, :], CA[:, f, :], ACT.Silu, scale=prm("conv_ln_w_2", f),
                                 bias=prm("conv_ln_b_2", f)))
        V.wait(A.now())
        A.wait(A.now())
        t_y = hi_lo(Y8[0], Y8[1], CQ)
        for j in range(4):
            t = proj_a(Y8, 2 * j, j == 0, j == 3, (t_y,))
        V.wait(t_bo)
        add_out(t, bias=BO)
        ffn(1)

        norm(X, prm("norm_mix_2", 16, 8), None, H8)
        QK = [ar(2048 * s, 2048).rearrange("p (k n) -> p k n", k=8) for s in range(2)]
        o = 4096
        VS = ar(o, 2048).rearrange("p (i n) -> p i n", i=2)
        YS = [ar(o + 2048 + 1024 * i, 1024) for i in range(2)]
        SQ3, RS3 = ar(o + 4096, 512), ar(o + 4608, 512)
        MSK = ar(o + 5120, 384)
        ZERO = ar(o + 5504, 256)
        ZZ = [ar(o + 5760 + 384 * i, 384) for i in range(2)]
        UU = [ar(o + 6528 + 384 * i, 384) for i in range(2)]
        GG = [ar(o + 7296 + 384 * i, 384) for i in range(2)]
        CC = [ar(o + 8064 + 386 * i, 386) for i in range(2)]
        AT = [ar(o + 8836 + 384 * i, 384) for i in range(2)]
        S.wait(V.now(), A.now(), P.now())
        t_m = small(MSK, I["consts"][:, C_SB:C_SB + 384], "sb")
        V.wait(P.now(), A.now(), t_m)
        A.wait(P.now(), V.now())
        V(ve.memset(ZERO, 0.0))
        for i in range(2):
            V(ve.memset(CC[i], 1.0))
        pend = None

        def fin_norm(j, ta):
            dst = QK[j // 4][:, 2 * (j % 4):2 * (j % 4) + 2, :]
            b = R.get()
            P.wait(ta)
            t = P.mark(pe.matmul(bank[b][:, :], blk, SQ3, start=True, stop=True))
            A.wait(t, V.now())
            t = A(ac.activation(RS3, bank[b][:, :], ACT.Sqrt, bias=eps, scale=1.0 / 64))
            R.put(b, t)
            V.wait(t)
            V(ve.reciprocal(RS3, RS3))
            V(ve.tensor_tensor(dst, dst, RS3.rearrange("p (m n) -> p m n", m=2), MUL))

        for j in range(9):
            if j < 8:
                bs, t = proj_b()
            if pend is not None:
                fin_norm(*pend)
            if j < 8:
                g = [prm(("sb_q_norm_2", "sb_k_norm_2")[j // 4], 0)] * 2
                A.wait(P.now())
                ta, tv = head_norm(bank[bs[0]][:, :], g, blk, 64, QK[j // 4][:, 2 * (j % 4):2 * (j % 4) + 2, :], t, SQ3)
                V.wait(V.now())
                R.put(bs[0], ta, tv)
                pend = (j, ta)
        for j in range(4):
            t = proj_a(H8, 2 * j, j == 0, j == 3)
        A.wait(t)
        V.wait(t)
        for q in range(4):
            m, h = q // 2, q % 2
            dst = VS[:, m, 512 * h:512 * h + 512]
            if q % 2:
                acc_free[q] = (A(ac.copy(dst, bank[q][:, :])),)
            else:
                acc_free[q] = (V(ve.tensor_copy(dst, bank[q][:, :])),)
        P.wait(A.now(), V.now())
        hist = {}

        def sb_vec(h):
            i = h % 2
            q, k = QK[0], QK[1]
            r, f = slice(64 * (h % 2), 64 * (h % 2) + 64), h // 2
            b = R.get()
            pe.matmul(bank[b][:, 0:128], q[r, f, 0:128], k[r, f, 0:128], start=True, stop=True)
            x = pe.matmul(bank[b][:, 128:384], q[r, f, 128:256], k[r, f, 0:256], start=True, stop=True)
            V.wait(P.mark(x), hist.get(("a", h - 2)))
            t = V(ve.scalar_tensor_tensor(ZZ[i], bank[b][:, 0:384], 0.125, MSK, MUL, ADD))
            R.put(b, t)
            A.wait(t)
            tu = A.mark(ac.activation(UU[i], ZZ[i], ACT.Sigmoid, scale=-1.0))
            hist["a", h] = A.mark(ac.activation(GG[i], ZZ[i], ACT.Sigmoid))
            V.wait(tu)
            c = CC[i]
            V(ve.tensor_tensor_scan(c[:, 127::-1], UU[i][:, 127::-1], ZERO[:, 0:128], 1.0, MUL, ADD))
            V(ve.tensor_tensor_scan(c[:, 384:128:-1], UU[i][:, 383:127:-1], ZERO, 1.0, MUL, ADD))
            V.wait(hist["a", h])
            V(ve.tensor_tensor(GG[i][:, 0:128], GG[i][:, 0:128], c[:, 1:129], MUL))
            V(ve.tensor_tensor(GG[i][:, 128:384], GG[i][:, 128:384], c[:, 130:386], MUL))
            return V.now()

        def sb_out(h, t):
            i = h % 2
            P.wait(t)
            b = R.get()
            for s in range(3):
                x = pe.transpose(bank[b][:, 128 * s:128 * s + 128], GG[i][:, 128 * s:128 * s + 128], ident)
            A.wait(P.mark(x))
            t = A(ac.copy(AT[i], bank[b][:, 0:384]))
            R.put(b, t)
            P.wait(t)
            vc = slice(64 * h, 64 * h + 64)
            q, oc = h // 8, slice(64 * (h % 8), 64 * (h % 8) + 64)
            pe.matmul(bank[q][:, oc], AT[i][:, 0:128], VS[:, 0, vc], start=True, stop=True)
            pe.matmul(bank[2 + q][:, oc], AT[i][:, 128:256], VS[:, 0, vc], start=True, stop=False)
            x = pe.matmul(bank[2 + q][:, oc], AT[i][:, 256:384], VS[:, 1, vc], start=False, stop=True)
            return P.mark(x)

        tt = {}
        for h in range(17):
            if h < 16:
                tt[h] = sb_vec(h)
            if h:
                t_o = sb_out(h - 1, tt[h - 1])
                V.wait(t_o)
                A.wait(t_o)
        A.wait(t_o)
        for q in range(4):
            dst = YS[q // 2][:, 512 * (q % 2):512 * (q % 2) + 512]
            if q % 2:
                acc_free[q] = (A(ac.copy(dst, bank[q][:, :])),)
            else:
                acc_free[q] = (V(ve.tensor_copy(dst, bank[q][:, :])),)
        P.wait(A.now(), V.now())
        for q in range(4):
            b = R.get()
            for m in range(2):
                for i in range(2):
                    k = 2 * q + m
                    x = pe.transpose(bank[b][:, 256 * m + 128 * i:256 * m + 128 * i + 128],
                                     YS[i][:, 128 * k:128 * k + 128], ident)
            t = P.mark(x)
            A.wait(t)
            s = slice(2 * q, 2 * q + 2)
            t = A(ac.copy(Y8[0][:, s, :], bank[b][:, :]))
            V.wait(t)
            t_y = V(ve.tensor_tensor(Y8[1][:, s, :], bank[b][:, :].rearrange("p (m n) -> p m n", m=2),
                                     f32(Y8[0][:, s, :]), SUB))
            R.put(b, t_y)
        for j in range(4):
            t = proj_a(Y8, 2 * j, j == 0, j == 3, (t_y,))
        add_out(t)
        ffn(2)
        ret(1, 3)
        ffn(3)

        FN = ar(4096, 1024)
        S.wait(V.now(), A.now(), P.now())
        t_f = small(FN, I["final_norm_2"].rearrange("(o n) -> o n", o=1).to_broadcast([128, 1024]), "final")
        rstd(X)
        V.wait(t_f)
        for i in range(2):
            t = V(ve.scalar_tensor_tensor(XN[i], X[i][:, :], ST[:, 2 + i:3 + i], FN, MUL, MUL))
            S.wait(t)
            nc.sync.dma_start(out[0, 128 * i:128 * i + 128, :], XN[i]).then_inc(s_out, 16)
        nc.sync.wait_ge(s_out, 32)
        assert state["next"] == len(items)


_INS = [
    "x", "c", "ctx", "c_ctx", "w_mod", "b_mod", "norm1_g", "norm2_g", "hg_w_in", "hg_lb_fwd", "hg_lb_bwd", "hg_gnorm",
    "hg_w_out", "router_w", "router_b", "moe_w_gate", "moe_w_up", "moe_w_down", "final_g", "norm_mix_2", "norm_ffn_2",
    "ret_w_in_2", "ret_q_norm_2", "ret_k_norm_2", "ret_gn_w_2", "ret_gn_b_2", "ret_w_out_2", "conv_pw1_w_2",
    "conv_pw1_b_2", "conv_dw_w_2", "conv_dw_b_2", "conv_ln_w_2", "conv_ln_b_2", "conv_pw2_w_2", "conv_pw2_b_2",
    "sb_w_in_2", "sb_q_norm_2", "sb_k_norm_2", "sb_w_out_2", "ffn_w1_2", "ffn_w2_2", "final_norm_2",
]


def constants():
    import numpy as np

    c = np.zeros((128, C_ALL), np.float32)
    p = np.arange(128)
    c[:, C_ID:C_ID + 128] = np.eye(128)
    c[:, C_ONE:C_ONE + 128] = 1.0
    c[:, C_BLK:C_BLK + 128] = p[:, None] // 64 == p[None, :] // 64
    c[[0, 2], C_SEL:C_SEL + 128] = 1.0
    same = p[:, None] // 64 == p[None, :] // 64
    c[:, C_MF:C_MF + 128] = same & (p[:, None] <= p[None, :])
    c[:, C_MB:C_MB + 128] = same & (p[:, None] >= p[None, :])
    t = np.arange(512)
    c[:, C_RF:C_RF + 512] = np.where(t < 256, t % 64 != 0, t != 256)
    c[:, C_RB:C_RB + 512] = np.where(t < 256, t % 64 != 63, t != 511)
    s, q = np.arange(256)[:, None], np.arange(256)[None, :]
    for h in range(4):
        lg = np.log(1.0 - 2.0 ** (-5.0 - h))
        m = np.where(s // 64 == q // 64, np.exp(lg * np.abs(q - s)), np.where(s // 64 < q // 64, np.exp(lg * (q - s)), 0.0))
        m = m / 16.0
        c[:, C_RET + 384 * h:C_RET + 384 * h + 256] = m[0:128, :]
        c[:, C_RET + 384 * h + 256:C_RET + 384 * h + 384] = m[128:256, 128:256]
    f = np.float32(10000.0) ** (-np.arange(128, dtype=np.float32) / np.float32(128))
    ang = (np.arange(256, dtype=np.float32)[None, :] * f[:, None].astype(np.float32)).astype(np.float64)
    c[:, C_COS:C_COS + 256] = np.cos(ang)
    c[:, C_SIN:C_SIN + 256] = np.sin(ang)
    diag = np.where(p[None, :] < p[:, None], 0.0, NEG)
    c[:, C_SB:C_SB + 128] = diag
    c[:, C_SB + 256:C_SB + 384] = diag
    c[:, C_LT:C_LT + 16] = (np.arange(4)[None, :] < np.arange(4)[:, None]).reshape(-1)
    return c


def kernel(**inputs):
    import numpy as _np
    import concourse.bacc as _bacc
    from concourse import mybir as _mybir
    from concourse.bass_utils import run_bass_kernel_spmd as _run

    nc = _bacc.Bacc("TRN2", target_bir_lowering=False, num_devices=1)
    arrays, args = {}, {}
    for name in _INS + ["consts"]:
        a = constants() if name == "consts" else _np.ascontiguousarray(inputs[name])
        arrays[f"in_{name}"] = a
        args[name] = nc.dram_tensor(f"in_{name}", a.shape, _mybir.dt.from_np(a.dtype), kind="ExternalInput").ap()
    out = nc.dram_tensor("out_0", (1, 256, 1024), F32, kind="ExternalOutput").ap()
    build(nc, args, out)
    r = _run(nc, [arrays], core_ids=[0])
    return r.results[0]["out_0"]
```

```python
from contextlib import ExitStack

import concourse.bass as bass
from concourse import mybir

F32 = mybir.dt.float32
F32R = mybir.dt.float32r
I32 = mybir.dt.int32
ALU = mybir.AluOpType
ACT = mybir.ActivationFunctionType
AX = mybir.AxisListType.X
MUL, ADD, SUB = ALU.mult, ALU.add, ALU.subtract

D = 1024
EPS = 1e-6
LOW_ON_DVE = 8
NEG = -1e30

C_ID, C_ONE, C_BLK, C_SEL, C_MF, C_MB, C_RF, C_RB = 0, 128, 256, 384, 512, 640, 768, 1280
C_END = 1792
C_RET, C_COS, C_SIN, C_SB, C_LT = 1792, 3328, 3584, 3840, 4224
C_ALL = 4240

PARAMS = [
    [("c", 8), ("c_ctx", 8), ("norm1_g", 8), ("norm2_g", 8), ("hg_lb_fwd", 16), ("hg_lb_bwd", 16),
     ("b_mod", 48), ("hg_gnorm", 1)],
    [("norm_mix_2", 32), ("norm_ffn_2", 32), ("ret_q_norm_2", 4), ("ret_k_norm_2", 4), ("ret_gn_w_2", 32)],
    [("ret_gn_b_2", 32), ("conv_pw1_b_2", 16), ("conv_dw_b_2", 8), ("conv_ln_w_2", 8), ("conv_ln_b_2", 8),
     ("sb_q_norm_2", 1), ("sb_k_norm_2", 1)],
    [("conv_dw_w_2", 124)],
    [("conv_dw_w_2", 124)],
]


class Engine:

    def __init__(self, eng, sem):
        self.e, self.sem, self.n, self.seen = eng, sem, 0, {}

    def mark(self, ins):
        ins.then_inc(self.sem, 1)
        self.n += 1
        return (self.sem, self.n)

    def __call__(self, ins):
        t = self.mark(ins)
        self.wait(t)
        return t

    def now(self):
        return (self.sem, self.n)

    def wait(self, *tokens):
        for t in tokens:
            if t is not None and t[1] > self.seen.get(t[0], 0):
                self.e.wait_ge(t[0], t[1])
                self.seen[t[0]] = t[1]


def build(nc, I, out):
    with ExitStack() as ctx:
        sem = lambda n: ctx.enter_context(nc.semaphore(n))
        sb = lambda n, s, d=F32: ctx.enter_context(nc.sbuf_tensor(n, s, d))
        V, A, P, G, S = (Engine(e, sem(n)) for e, n in (
            (nc.vector, "s_dve"), (nc.scalar, "s_act"), (nc.tensor, "s_pe"), (nc.gpsimd, "s_pool"), (nc.sync, "s_sp")))
        ve, ac, pe, po = nc.vector, nc.scalar, nc.tensor, nc.gpsimd
        s_out = sem("s_out")

        bank = [ctx.enter_context(nc.psum_tensor(f"bank{i}", [128, 512], F32)) for i in range(8)]

        X = [sb(f"X{i}", [128, D])[:, :] for i in range(2)]
        NR, NS = 3, 3
        raw = [sb(f"raw{i}", [128, 2048]) for i in range(NR)]
        whi = [sb(f"whi{i}", [128, 2048], F32R) for i in range(NS)]
        wlo = [sb(f"wlo{i}", [128, 2048], F32R) for i in range(NS)]
        HH, HL = sb("HH", [128, 4096], F32R), sb("HL", [128, 4096], F32R)
        YH, YL = sb("YH", [128, 2048], F32R), sb("YL", [128, 2048], F32R)
        CST = sb("CST", [128, C_END])
        PRM = sb("PRM", [128, 560])
        SM = sb("SM", [128, 256])
        CS = sb("CS", [128, 32], F32R)
        ARENA = sb("ARENA", [128, 14592])
        ar = lambda o, n: ARENA[:, o:o + n]
        ident, ones, blk = CST[:, 0:128], CST[:, 128:256], CST[:, 256:384]
        f32 = lambda ap: ap.bitcast(F32)

        s_ld = [sem(f"s_ld{i}") for i in range(NR)]
        group = {}

        def small(dst, src, name):
            if name not in group:
                group[name] = [sem(f"s_{name}"), 0]
            g = group[name]
            nc.sync.dma_start(dst, src).then_inc(g[0], 16)
            g[1] += 16
            return (g[0], g[1])

        col, pt, base = {}, [], 0

        def load_rows(k, name):
            nonlocal base
            r, dst = 0, ar(4096 + 128 * k, 128)
            for what, n in PARAMS[k]:
                ap = I[what]
                if what == "conv_dw_w_2":
                    src = ap.rearrange("o w (t p) -> (o w t) p", p=128)[124 * (k - 3):124 * (k - 2), :]
                    t = small(dst[r:r + n, :], src, name)
                elif what in ("sb_q_norm_2", "sb_k_norm_2"):
                    small(dst[r:r + 1, 0:64], ap, name)
                    t = small(dst[r:r + 1, 64:128], ap, name)
                elif len(ap.shape) == 1:
                    t = small(dst[r:r + n, :], ap.rearrange("(t p) -> t p", p=128), name)
                else:
                    t = small(dst[r:r + n, :], ap.rearrange("o (t p) -> (o t) p", p=128), name)
                col.setdefault(what, base + r)
                r += n
            pt.append((dst, r, base))
            base += r
            return t

        small(CST[:, :], I["consts"][:, 0:C_END], "first")
        t_c0 = load_rows(0, "first")
        XC = [ar(12000 + 1024 * i, 1024) for i in range(2)]
        prm = lambda name, i, n=1: PRM[:, col[name] + i:col[name] + i + n]

        def kcols(w, k0, nk, n0, nn):
            return w[128 * k0:128 * (k0 + nk), n0:n0 + nn].rearrange("(k p) n -> p k n", p=128), nk, nn

        items = []

        def plan(w, k0, nk, n0, nn):
            items.append(kcols(w, k0, nk, n0, nn))

        wm, wi = I["w_mod"][0], I["hg_w_in"][0]

        def plan_mod(c):
            plan(wm, 0, 4, 512 * c, 512)
            plan(wm, 4, 4, 512 * c, 512)

        def plan_b(w, n0, count):
            for j in range(count):
                plan(w, 0, 8, n0 + 256 * j, 256)

        for c in range(4):
            plan_mod(c)
        plan_b(wi, 0, 4)
        for c in range(2):
            plan(wi, 0, 4, 1024 + 512 * c, 512)
            plan(wi, 4, 4, 1024 + 512 * c, 512)
        def plan_z(u):
            plan_b(wi, 2048 + 1024 * (u % 2) + 256 * (u // 2), 1)

        plan_z(0)
        plan_z(1)
        for u in range(8):
            plan_mod(4 + u)
            if u < 6:
                plan_z(u + 2)
        plan_b(wi, 4096, 4)

        def plan_a(w, nk, n0=0):
            for j in range(nk // 2):
                plan(w, 2 * j, 2, n0, 1024)

        plan_a(I["hg_w_out"][0], 8)
        for e in range(17):
            if e < 16:
                plan(I["moe_w_gate"][0, e], 0, 8, 0, 256)
                plan(I["moe_w_up"][0, e], 0, 8, 0, 256)
            if e:
                plan(I["moe_w_down"][0, e - 1], 0, 2, 0, 1024)

        def plan_ffn(i):
            for j in range(17):
                if j < 16:
                    plan(I["ffn_w1_2"][i], 0, 8, 256 * j, 256)
                if j:
                    plan(I["ffn_w2_2"][i], 2 * (j - 1), 2, 0, 1024)

        def plan_ret(i):
            w = I["ret_w_in_2"][i]
            plan_b(w, 0, 8)
            plan_a(w, 8, 2048)
            plan_a(w, 8, 3072)
            for h in range(5):
                if h < 4:
                    plan_b(w, 4096 + 512 * h, 2)
                if h:
                    for j in range(2):
                        plan(I["ret_w_out_2"][i], 4 * (h - 1) + 2 * j, 2, 0, 1024)

        plan_ret(0)
        plan_ffn(0)
        for j in range(4):
            plan_b(I["conv_pw1_w_2"][0], 256 * j, 1)
            plan_b(I["conv_pw1_w_2"][0], 1024 + 256 * j, 1)
        plan_a(I["conv_pw2_w_2"][0], 8)
        plan_ffn(1)
        plan_b(I["sb_w_in_2"][0], 0, 8)
        plan_a(I["sb_w_in_2"][0], 8, 2048)
        plan_a(I["sb_w_out_2"][0], 8)
        plan_ffn(2)
        plan_ret(1)
        plan_ffn(3)

        loaded, low, used = {}, {}, {}
        state = {"next": 0}

        def load(i):
            if i >= len(items):
                return
            src, nk, nn = items[i]
            S.wait(low.get(i - NR))
            nc.sync.dma_start(raw[i % NR][:, :].rearrange("p (k n) -> p k n", k=nk), src).then_inc(s_ld[i % NR], 16)
            loaded[i] = (s_ld[i % NR], 16 * (i // NR + 1))

        def split(i):
            if i >= len(items):
                return
            A.wait(loaded[i], used.get(i - NS))
            t = A.mark(ac.copy(whi[i % NS][:, :], raw[i % NR][:, :]))
            E, e = (V, ve) if i < LOW_ON_DVE else (G, po)
            E.wait(t, loaded[i])
            low[i] = E.mark(e.tensor_tensor(wlo[i % NS][:, :], raw[i % NR][:, :], f32(whi[i % NS][:, :]), SUB))
            load(i + NR)

        for i in range(NR):
            load(i)
        for i in range(2):
            t_x = small(X[i], I["x"][0, 128 * i:128 * i + 128, :], "x")
        for i in range(2):
            t_x = small(XC[i], I["ctx"][0, 128 * i:128 * i + 128, :], "x")
        for k in range(1, 5):
            t_in = load_rows(k, "rows")

        def take():
            i = state["next"]
            state["next"] += 1
            if i == 0:
                for j in range(NS - 1):
                    split(j)
            split(i + NS - 1)
            P.wait(low[i])
            nk = items[i][1]
            return i, [w[i % NS][:, :].rearrange("p (k n) -> p k n", k=nk) for w in (whi, wlo)]

        def done(i, token):
            used[i] = token

        class Banks:

            def __init__(self, which):
                self.q = [(b, ()) for b in which]

            def get(self):
                b, toks = self.q.pop(0)
                P.wait(*toks)
                return b

            def put(self, b, *toks):
                self.q.append((b, toks))

        R = Banks([4, 5, 6, 7])
        acc_free = [()] * 4
        bank_done = [None] * 4

        def mm3(ps, lh, ll, rh, rl, start, stop):
            pe.matmul(ps, lh, rh, start=start, stop=False)
            pe.matmul(ps, lh, rl, start=False, stop=False)
            return pe.matmul(ps, ll, rh, start=False, stop=stop)

        H8 = [h[:, 0:2048].rearrange("p (k n) -> p k n", k=8) for h in (HH, HL)]
        H16 = [h[:, :].rearrange("p (k n) -> p k n", k=8) for h in (HH, HL)]
        Y8 = [h[:, :].rearrange("p (k n) -> p k n", k=8) for h in (YH, YL)]

        def proj_b(acts=None, n=256, ready=None):
            a = acts or H8
            bs = [R.get() for _ in range(n // 256)]
            i, w = take()
            for k in range(8):
                if ready is not None and k % 2 == 0:
                    P.wait(ready[k // 2])
                for m in range(2):
                    ps = bank[bs[m]][:, 0:512] if n == 512 else bank[bs[0]][:, 256 * m:256 * m + 256]
                    c = slice(128 * m, 128 * m + 128)
                    first = k == 0 and (m == 0 or n == 512)
                    ah, al = a[0][:, k, 0:n], a[1][:, k, 0:n]
                    pe.matmul(ps, w[0][:, k, c], ah, start=first, stop=False, skip_group_check=True)
                    pe.matmul(ps, w[0][:, k, c], al, start=False, stop=False, skip_group_check=True)
                    last = pe.matmul(ps, w[1][:, k, c], ah, start=False, stop=k == 7, skip_group_check=True)
            t = P.mark(last)
            done(i, t)
            return bs, t

        def proj_a(acts, k0, first, last_, ready=()):
            i, w = take()
            P.wait(*ready)
            for h in range(2):
                for m in range(2):
                    q = 2 * m + h
                    if first:
                        P.wait(*acc_free[q])
                    for k in range(2):
                        c = slice(128 * m, 128 * m + 128)
                        r = slice(512 * h, 512 * h + 512)
                        x = mm3(bank[q][:, :], acts[0][:, k0 + k, c], acts[1][:, k0 + k, c], w[0][:, k, r],
                                w[1][:, k, r], first and k == 0, last_ and k == 1)
                    if last_:
                        bank_done[q] = P.mark(x)
            t = bank_done[q] if last_ else P.mark(x)
            done(i, t)
            return t

        eps = SM[:, 0:1]
        V(ve.memset(eps, EPS))
        RT = sb("RT", [128, 160])
        RW, RB, LT = RT[:, 0:128], RT[:, 128:144], RT[:, 144:160]
        small(RW, I["router_w"].rearrange("(k p) e -> p k e", p=128), "router")
        small(RB, I["router_b"].rearrange("(o e) -> o e", o=1).to_broadcast([128, 16]), "router")
        t_r = small(LT, I["consts"][:, C_LT:C_LT + 16], "router")

        def columns(k, t):
            src, n, off = pt[k]
            b = R.get()
            P.wait(t)
            V.wait(P.mark(pe.transpose(bank[b][:, 0:n], src[0:n, :], ident[0:n, 0:n])))
            R.put(b, V(ve.tensor_copy(PRM[:, off:off + n], bank[b][:, 0:n])))

        columns(0, t_c0)
        t_prm = V.now()

        XN = [ar(1024 * i, 1024) for i in range(2)]
        FT = ar(2048, 2048).rearrange("p (k n) -> p k n", k=8)
        ST = sb("ST", [128, 16])
        RBC = sb("RBC", [128, 256])
        pool_read = {"FT": None}
        x_done = [None] * 4

        def square_half(x, n):
            A.wait(A.now())
            A.mark(ac.activation(XN[0][:, 0:512], x, ACT.Square, accum_out=ST[:, n:n + 1]))

        def sum_squares(xs, t, at=0):
            A.wait(t)
            for q in range(4):
                square_half(xs[q // 2][:, 512 * (q % 2):512 * (q % 2) + 512], at + q)

        def rstd(at=0):
            V.wait(A.now())
            p = ST[:, at:at + 4].rearrange("p (i h) -> p i h", h=2)
            V(ve.tensor_tensor(ST[:, 10:12], p[:, :, 0], p[:, :, 1], ADD))
            A.wait(V.now())
            A(ac.activation(ST[:, 12:14], ST[:, 10:12], ACT.Sqrt, bias=eps, scale=1.0 / D))
            V.wait(A.now())
            return V(ve.reciprocal(ST[:, 8:10], ST[:, 12:14]))

        def norm(xs, scale, shift, dst, at=0):
            bs = []
            for q in range(4):
                P.wait(x_done[q // 2], x_done[2 + q // 2])
                b = R.get()
                for m in range(2):
                    for i in range(2):
                        k = 2 * q + m
                        x = pe.transpose(bank[b][:, 256 * m + 128 * i:256 * m + 128 * i + 128],
                                         xs[i][:, 128 * k:128 * k + 128], ident)
                bs.append((b, P.mark(x)))
            P.wait(rstd(at), *acc_free[0])
            for i in range(2):
                x = pe.matmul(bank[0][:, 128 * i:128 * i + 128], ST[:, 8 + i:9 + i].to_broadcast([128, 128]), ident,
                              start=True, stop=True)
            V.wait(P.mark(x))
            t = V(ve.tensor_copy(RBC[:, :], bank[0][:, 0:256]))
            acc_free[0] = (t,)
            V.wait(pool_read["FT"])
            ta, ready = [], []

            def low_part(q):
                kk = slice(2 * q, 2 * q + 2)
                E, e = (V, ve) if q % 2 == 0 else (G, po)
                E.wait(ta[q])
                ready.append(E.mark(e.tensor_tensor(dst[1][:, kk, :], FT[:, kk, :], f32(dst[0][:, kk, :]), SUB)))

            for q in range(4):
                b, t = bs[q]
                V.wait(t)
                for m in range(2):
                    k = 2 * q + m
                    V.mark(ve.scalar_tensor_tensor(FT[:, k, :], bank[b][:, 256 * m:256 * m + 256], scale[:, k:k + 1],
                                                   RBC[:, :], MUL, MUL))
                R.put(b, V.now())
                if shift is not None:
                    V.wait(V.now())
                    for m in range(2):
                        k = 2 * q + m
                        V.mark(ve.tensor_scalar(FT[:, k, :], FT[:, k, :], shift[:, k:k + 1], None, ADD))
                A.wait(V.now())
                ta.append(A.mark(ac.copy(dst[0][:, 2 * q:2 * q + 2, :], FT[:, 2 * q:2 * q + 2, :])))
                if q:
                    low_part(q - 1)
            low_part(3)
            pool_read["FT"] = ready[3]
            return ready

        A.wait(t_prm)
        cs = SM[:, 2:18].rearrange("p (v k) -> p k v", v=2)
        A(ac.activation(SM[:, 2:18], prm("c", 0, 16), ACT.Silu))
        CSv = CS[:, :].rearrange("p (k v) -> p k v", v=4)
        A(ac.copy(CSv[:, :, 0:2], cs))
        V.wait(A.now())
        t_cs = V(ve.tensor_tensor(CSv[:, :, 2:4], cs, f32(CSv[:, :, 0:2]), SUB))

        MODT = SM[:, 80:144].rearrange("p (v t) -> p v t", t=16)
        MR = sb("MR", [4, 512])
        G1B, G2B = sb("G1B", [128, D]), sb("G2B", [128, D])
        TM = SM[:, 208:224]
        bm = I["b_mod"]
        t_gb = (small(G1B[:, :], bm[0:1, 2048:3072].to_broadcast([128, 1024]), "gate"),
                small(G2B[:, :], bm[0:1, 5120:6144].to_broadcast([128, 1024]), "gate"))[1]
        slot = {0: 0, 1: 1, 3: 2, 4: 3}
        mod_state = {}
        MRS = [MR[:, :], ar(6000, 512)[0:4, :]]

        def mod_rows(c, RB):
            b = RB.get()
            P.wait(t_cs)
            for half in range(2):
                i, w = take()
                for k in range(4):
                    for r in range(2):
                        x = pe.matmul(bank[b][0:4, :], CSv[:, 4 * half + k, :], w[r][:, k, :],
                                      start=half == 0 and k == 0 and r == 0, stop=half == 1 and k == 3 and r == 1)
                t = P.mark(x)
                done(i, t)
            mr = MRS[c % 2] if c < 4 else MR[:, :]
            A.wait(t, mod_state.get(c - (2 if c < 4 else 1)))
            t = A(ac.copy(mr, bank[b][0:4, :]))
            RB.put(b, t)
            return t

        def mod_cols(c, t, RB):
            which, half = c // 2, c % 2
            mr = MRS[c % 2] if c < 4 else MR[:, :]
            b = RB.get()
            P.wait(t)
            if which in slot:
                for k in range(4):
                    x = pe.transpose(bank[b][:, 4 * k:4 * k + 4], mr[:, 128 * k:128 * k + 128], ident[0:4, 0:4])
                mod_state[c] = P.mark(x)
                V.wait(mod_state[c])
                RB.put(b, V(ve.tensor_copy(TM, bank[b][:, 0:16])))
                tm = TM.rearrange("p (k v) -> p k v", v=4)
                o = MODT[:, slot[which], 8 * half:8 * half + 8].rearrange("p (k v) -> p k v", v=2)
                V(ve.tensor_tensor(o, tm[:, :, 0:2], tm[:, :, 2:4], ADD))
                bb = prm("b_mod", 8 * which + 4 * half, 4).rearrange("p (k v) -> p k v", v=1).to_broadcast([128, 4, 2])
                V(ve.tensor_tensor(o, o, bb, ADD))
            else:
                x = pe.matmul(bank[b][:, :], CST[0:4, C_SEL:C_SEL + 128], mr, start=True, stop=True)
                mod_state[c] = P.mark(x)
                V.wait(mod_state[c], t_gb)
                g = (G1B if which == 2 else G2B)[:, 512 * half:512 * half + 512]
                RB.put(b, V(ve.tensor_tensor(g, g, bank[b][:, :], ADD)))

        tm_ = {}
        sum_squares(X, t_x)
        for c in range(5):
            if c < 4:
                tm_[c] = mod_rows(c, R)
            if c:
                mod_cols(c - 1, tm_[c - 1], R)
            if c == 2:
                sum_squares(XC, t_x, 4)
        MS = SM[:, 224:256]
        for v in range(2):
            sc = MODT[:, 1, :].rearrange("p (t v) -> p v t", v=2)[:, v, :]
            V(ve.scalar_tensor_tensor(MS[:, 8 * v:8 * v + 8], sc, 1.0, prm("norm1_g", 0, 8), ADD, MUL))
        sh1 = MODT[:, 0, :].rearrange("p (t v) -> p v t", v=2)

        def hi_lo(hi, lo, src):
            A.wait(V.now())
            V.wait(A.mark(ac.copy(hi, src)))
            return V(ve.tensor_tensor(lo, src, f32(hi), SUB))

        x_done[:] = [t_x] * 4
        ready = norm(X, MS[:, 0:8], sh1[:, 0, :], [h[:, :, 0:256] for h in H16])
        for k in range(1, 5):
            columns(k, t_in)

        LB, LB1 = SM[:, 18:34], SM[:, 34:50]
        for d, name in enumerate(("hg_lb_fwd", "hg_lb_bwd")):
            a0, a1 = prm(name, 0, 8), prm(name, 8, 8)
            mx, e0, e1 = SM[:, 50:58], SM[:, 58:66], SM[:, 66:74]
            V(ve.tensor_tensor(mx, a0, a1, ALU.max))
            V(ve.tensor_tensor(e0, a0, mx, SUB))
            V(ve.tensor_tensor(e1, a1, mx, SUB))
            A.wait(V.now())
            A(ac.activation(SM[:, 58:74], SM[:, 58:74], ACT.Exp))
            V.wait(A.now())
            V(ve.tensor_tensor(mx, e0, e1, ADD))
            V(ve.reciprocal(mx, mx))
            V(ve.tensor_tensor(LB[:, 8 * d:8 * d + 8], e0, mx, MUL))
            V(ve.tensor_tensor(LB1[:, 8 * d:8 * d + 8], e1, mx, MUL))

        readyc = norm(XC, MS[:, 8:16], sh1[:, 1, :], [h[:, :, 256:512] for h in H16], 4)

        QO = ar(0, 2048).rearrange("p (t n) -> p t n", t=8)
        VT = ar(2048, 4096).rearrange("p (i n) -> p i n", i=4)
        o0 = 6144
        kk_ = ar(o0, 1024).rearrange("p (h n) -> p h n", h=2)
        cum = ar(o0 + 1024, 1024).rearrange("p (h n) -> p h n", h=2)
        tmp = ar(o0 + 2048, 1024).rearrange("p (h n) -> p h n", h=2)
        KDT = ar(o0 + 3072, 1024).rearrange("p (h i n) -> p h i n", h=2, i=4)
        QE = ar(o0 + 4096, 512).rearrange("p (h n) -> p h n", h=2)
        KE = ar(o0 + 4608, 512).rearrange("p (h n) -> p h n", h=2)
        QI = ar(o0 + 5120, 512).rearrange("p (h n) -> p h n", h=2)
        SA = ar(o0 + 5632, 1024).rearrange("p (h i n) -> p h i n", h=2, i=4)
        SC = [ar(o0 + 6656 + 512 * i, 512) for i in range(2)]
        kd2 = ar(o0 + 7680, 512).rearrange("p (h n) -> p h n", h=2)
        SG = ar(o0 + 4096, 2048).rearrange("p (t n) -> p t n", t=8)
        DEC = sb("DEC", [128, 16])

        for d in range(2):
            V(ve.memset(SC[d], 0.0))
        A.wait(ready[3], readyc[3], V.now())
        for j in range(4):
            (b,), t = proj_b(H16, 256, ready if j == 0 else None)
            A.wait(t)
            t = A(ac.activation(QO[:, 2 * j:2 * j + 2, :], bank[b][:, :], ACT.Silu))
            R.put(b, t)
        P.wait(*readyc)
        for c in range(2):
            for half in range(2):
                i, w = take()
                for m in range(4):
                    if half == 0:
                        P.wait(*acc_free[m])
                    for k in range(4):
                        q = 4 * half + k
                        cc = slice(128 * m, 128 * m + 128)
                        x = mm3(bank[m][:, :], H16[0][:, q, cc], H16[1][:, q, cc], w[0][:, k, :], w[1][:, k, :],
                                q == 0, q == 7)
                t = P.mark(x)
                done(i, t)
            A.wait(t)
            V.wait(t)
            for m in range(4):
                dst = VT[:, m, 512 * c:512 * c + 512]
                if m % 2:
                    acc_free[m] = (A(ac.copy(dst, bank[m][:, :])),)
                else:
                    acc_free[m] = (V(ve.tensor_copy(dst, bank[m][:, :])),)
        t_v = (A.now(), V.now())

        zq, vec_read = {}, {"kk": V.now()}

        def unit_proj(u):
            zq[u] = proj_b(H16, 512)

        def unit_vec(u):
            p, d = u // 2, u % 2
            bs, t = zq[u]
            A.wait(t, vec_read["kk"], vec_read.get("out"), V.now())
            V.wait(vec_read["kk"], vec_read.get("out"))
            for h in range(2):
                A.mark(ac.activation(kk_[:, h, :], bank[bs[h]][:, :], ACT.Sigmoid, scale=-1.0))
                A.mark(ac.activation(tmp[:, h, :], bank[bs[h]][:, :], ACT.Sigmoid))
                R.put(bs[h], A.now())
            A.wait(A.now())
            tl_ = []
            for h in range(2):
                q = 8 * d + 2 * p + h
                tl_.append(A.mark(ac.activation(tmp[:, h, :], tmp[:, h, :], ACT.Ln, scale=LB1[:, q:q + 1],
                                                bias=LB[:, q:q + 1])))
            for h in range(2):
                V.wait(tl_[h])
                if d == 0:
                    V.mark(ve.tensor_tensor_scan(cum[:, h, :], CST[:, C_RF:C_RF + 512], tmp[:, h, :], 0.0, MUL, ADD))
                else:
                    V.mark(ve.tensor_tensor_scan(cum[:, h, ::-1], CST[:, C_RB + 511:C_RB - 1:-1], tmp[:, h, ::-1],
                                                 0.0, MUL, ADD))
            V.wait(V.now())
            cl = cum[:, :, 0:256].rearrange("p h (c n) -> p h c n", c=4)
            tl = tmp[:, :, 0:256].rearrange("p h (c n) -> p h c n", c=4)
            kl = kd2.rearrange("p h (c n) -> p h c n", c=4)
            bc = lambda i: cl[:, :, :, i:i + 1].to_broadcast([128, 2, 4, 64])
            ref, last = (31, 63) if d == 0 else (32, 0)
            lc = 511 if d == 0 else 256
            A.wait(V.now())
            A.mark(ac.activation(DEC[:, 8 * d:8 * d + 8].rearrange("p (h c) -> p h c", h=2), cl[:, :, :, last], ACT.Exp))
            t_qi = A.mark(ac.activation(QI, cum[:, :, 0:256], ACT.Exp))
            t1 = V.mark(ve.tensor_tensor(tl, cl, bc(ref), SUB))
            t2 = V.mark(ve.tensor_tensor(kl, cl, bc(last), SUB))
            t3 = V.mark(ve.tensor_tensor(tmp[:, :, 256:512], cum[:, :, 256:512],
                                         cum[:, :, lc:lc + 1].to_broadcast([128, 2, 256]), SUB))
            A.wait(t1)
            t_qe = A.mark(ac.activation(QE, tmp[:, :, 0:256], ACT.Exp))
            t_ke = A.mark(ac.activation(KE, tmp[:, :, 0:256], ACT.Exp, scale=-1.0))
            A.wait(t2)
            A.mark(ac.activation(kd2, kd2, ACT.Exp, scale=-1.0))
            A.wait(t3)
            t_kd = A.mark(ac.activation(tmp[:, :, 256:512], tmp[:, :, 256:512], ACT.Exp, scale=-1.0))
            V.wait(t_qi)
            V.mark(ve.tensor_tensor(QI, QI, QO[:, 2 * p:2 * p + 2, :], MUL))
            V.wait(t_qe)
            V.mark(ve.tensor_tensor(QE, QE, QO[:, 2 * p:2 * p + 2, :], MUL))
            V.wait(t_ke)
            lb1 = [LB1[:, 8 * d + 2 * p + h:8 * d + 2 * p + h + 1] for h in range(2)]
            for h in range(2):
                V.mark(ve.scalar_tensor_tensor(KE[:, h, :], KE[:, h, :], lb1[h], kk_[:, h, 0:256], MUL, MUL))
            t_qe = V.now()
            V.wait(t_kd)
            for h in range(2):
                V.mark(ve.scalar_tensor_tensor(kd2[:, h, :], kd2[:, h, :], lb1[h], kk_[:, h, 0:256], MUL, MUL))
                V.mark(ve.scalar_tensor_tensor(tmp[:, h, 256:512], tmp[:, h, 256:512], lb1[h], kk_[:, h, 256:512],
                                               MUL, MUL))
            vec_read["kk"] = V.now()
            return t_qe, V.now()

        def unit_scores(u, t_qe, t_kd):
            d = u % 2
            P.wait(t_qe)
            b = R2.get()
            for h in range(2):
                for j in range(2):
                    s = slice(128 * j, 128 * j + 128)
                    q = 2 * h + j
                    x = pe.matmul(bank[b][:, 128 * q:128 * q + 128], KE[:, h, s], QE[:, h, s],
                                  start=True, stop=True)
            t = P.mark(x)
            P.wait(t_kd)
            bs = []
            for h in range(2):
                bb = R2.get()
                for i in range(4):
                    src = (kd2[:, h, 0:128], kd2[:, h, 128:256], tmp[:, h, 256:384], tmp[:, h, 384:512])[i]
                    x = pe.transpose(bank[bb][:, 128 * i:128 * i + 128], src, ident)
                bs.append((bb, P.mark(x)))
            V.wait(t)
            m = CST[:, (C_MF, C_MB)[d]:(C_MF, C_MB)[d] + 128].bitcast(I32)
            mb = m.rearrange("p (q n) -> p q n", q=1).to_broadcast([128, 4, 128])
            t = V(ve.copy_predicated(SC[d].rearrange("p (q n) -> p q n", q=4), mb,
                                     bank[b][:, :].rearrange("p (q n) -> p q n", q=4)))
            R2.put(b, t)
            A.wait(bs[0][1])
            R2.put(bs[0][0], A(ac.copy(KDT[:, 0, :, :], bank[bs[0][0]][:, :])))
            V.wait(bs[1][1])
            R2.put(bs[1][0], V(ve.tensor_copy(KDT[:, 1, :, :], bank[bs[1][0]][:, :])))
            vec_read["kdt"] = (A.now(), V.now())
            vec_read["kk"] = P.now()
            return t

        def unit_state(u):
            p, d = u // 2, u % 2
            P.wait(*vec_read["kdt"])
            order = [0, 1, 2] if d == 0 else [3, 2, 1]
            bs = [R2.get() for _ in range(3)]
            at = {}
            for h in range(2):
                hc = slice(128 * (2 * p + h), 128 * (2 * p + h) + 128)
                for i in range(2):
                    x = pe.matmul(bank[bs[h]][:, 0:128], KDT[:, h, 2 + i, :], VT[:, 2 + i, hc], start=i == 0, stop=i == 1)
            for odd in range(2):
                for h in range(2):
                    hc = slice(128 * (2 * p + h), 128 * (2 * p + h) + 128)
                    for n, c in enumerate(order):
                        if c % 2 != odd:
                            continue
                        r = slice(64 * odd, 64 * odd + 64)
                        b, o = (bs[2], 256 * h + 128 * (n // 2)) if odd else (bs[h], 128 * (n + 1))
                        at[h, n] = bank[b][:, o:o + 128]
                        x = pe.matmul(at[h, n], KDT[r, h, c // 2, :], VT[r, c // 2, hc], start=True, stop=True)
            V.wait(P.mark(x), vec_read.get("out"))
            for h in range(2):
                V.mark(ve.tensor_copy(SA[:, h, 0, :], bank[bs[h]][:, 0:128]))
            for n, c in enumerate(order):
                for h in range(2):
                    V.wait((V.sem, V.n - 1))
                    V.mark(ve.scalar_tensor_tensor(SA[:, h, n + 1, :], SA[:, h, n, :],
                                                   DEC[:, 8 * d + 4 * h + c:8 * d + 4 * h + c + 1], at[h, n], MUL, ADD))
            vec_read["state"] = V.now()
            for b in bs:
                R2.put(b, V.now())

        def unit_out(u):
            p, d = u // 2, u % 2
            P.wait(vec_read["state"])
            if d == 0:
                P.wait(*acc_free[0])
            first = d == 0
            order = [0, 1, 2, 3] if d == 0 else [3, 2, 1, 0]
            for h in range(2):
                hc = slice(128 * (2 * p + h), 128 * (2 * p + h) + 128)
                for j in range(2):
                    q = 2 * h + j
                    pe.matmul(bank[0][:, 128 * q:128 * q + 128], VT[:, j, hc], SC[d][:, 128 * q:128 * q + 128],
                              start=first, stop=False, skip_group_check=True)
                    first = False
                for n, c in enumerate(order):
                    x = pe.matmul(bank[0][:, 256 * h + 64 * c:256 * h + 64 * c + 64], SA[:, h, n, :],
                                  QI[:, h, 64 * c:64 * c + 64], start=False,
                                  stop=d == 1 and h == 1 and n == 3, skip_group_check=True)
            t = P.mark(x)
            vec_read["out"] = t
            if d == 1:
                V.wait(t)
                acc_free[0] = (V(ve.tensor_copy(QO[:, 2 * p:2 * p + 2, :], bank[0][:, :])),)

        acc_free[0] = acc_free[0] + t_v
        R2 = Banks([])
        for q in (1, 2, 3):
            R2.put(q, *acc_free[q])
        unit_proj(0)
        tk = unit_vec(0)
        unit_proj(1)
        for u in range(8):
            unit_scores(u, *tk)
            t = mod_rows(4 + u, R2)
            unit_state(u)
            mod_cols(4 + u, t, R2)
            unit_out(u)
            if u < 7:
                tk = unit_vec(u + 1)
            if u < 6:
                unit_proj(u + 2)
        for q, toks in R2.q:
            acc_free[q] = toks

        t_yj = {}
        SQ = ar(o0, 2048).rearrange("p (t n) -> p t n", t=8)
        RS = ar(o0 + 2048, 2048).rearrange("p (t n) -> p t n", t=8)
        A.wait(V.now(), P.now())
        t_sq = []
        for j in range(4):
            s = slice(2 * j, 2 * j + 2)
            t_sq.append(A.mark(ac.activation(SQ[:, s, :], QO[:, s, :], ACT.Square)))
        gs = [proj_b(H16)]
        t_ms = []
        for j in range(4):
            P.wait(t_sq[j], *acc_free[j])
            t_ms.append(P.mark(pe.matmul(bank[j][:, :], ones, SQ[:, 2 * j:2 * j + 2, :], start=True, stop=True)))
        for j in range(4):
            s = slice(2 * j, 2 * j + 2)
            A.wait(t_ms[j])
            t = A.mark(ac.activation(RS[:, s, :], bank[j][:, :], ACT.Sqrt, bias=eps, scale=1.0 / 128))
            acc_free[j] = (t,)
            V.wait(t)
            V(ve.reciprocal(RS[:, s, :], RS[:, s, :]))
            V.mark(ve.scalar_tensor_tensor(QO[:, s, :], QO[:, s, :], prm("hg_gnorm", 0), RS[:, s, :], MUL, MUL))
        V.wait(V.now())
        for j in range(4):
            s = slice(2 * j, 2 * j + 2)
            (bg,), tg = gs.pop() if gs else proj_b(H16)
            A.wait(tg)
            tg = A.mark(ac.activation(SG[:, s, :], bank[bg][:, :], ACT.Silu))
            R.put(bg, tg)
            V.wait(tg)
            V(ve.tensor_tensor(QO[:, s, :], QO[:, s, :], SG[:, s, :], MUL))
            t_yj[j] = hi_lo(Y8[0][:, s, :], Y8[1][:, s, :], QO[:, s, :])

        TMPA = [XN[1][:, 512 * i:512 * i + 512] for i in range(2)]

        def add_out(t, gate=None, bias=None):
            for q in (0, 2, 1, 3):
                V.wait(bank_done[q])
                m, h = q // 2, q % 2
                x = X[m][:, 512 * h:512 * h + 512]
                g = slice(512 * h, 512 * h + 512)
                if gate is not None:
                    acc_free[q] = (V(ve.tensor_tensor(TMPA[q // 2], bank[q][:, :], gate[:, g], MUL)),)
                    t = V.mark(ve.tensor_tensor(x, x, TMPA[q // 2], ADD))
                else:
                    t = V.mark(ve.tensor_tensor(x, x, bank[q][:, :], ADD))
                    acc_free[q] = (t,)
                    if bias is not None:
                        V.wait(t)
                        t = V.mark(ve.tensor_tensor(x, x, bias[:, g], ADD))
                A.wait(t)
                x_done[q] = t
                square_half(x, q)
            V.wait(V.now())

        for j in range(4):
            t = proj_a(Y8, 2 * j, j == 0, j == 3, (t_yj[j],))
        add_out(t, gate=G1B[:, :])

        V(ve.scalar_tensor_tensor(MS[:, 16:24], MODT[:, 3, :].rearrange("p (t v) -> p v t", v=2)[:, 0, :], 1.0,
                                  prm("norm2_g", 0, 8), ADD, MUL))
        sh2 = MODT[:, 2, :].rearrange("p (t v) -> p v t", v=2)[:, 0, :]
        ready = norm(X, MS[:, 16:24], sh2, H8)

        o0 = 4096
        FG = ar(o0 + 7424, 1024)
        t_g = small(FG, I["final_g"].rearrange("(o n) -> o n", o=1).to_broadcast([128, 1024]), "first")
        CB = ar(o0 + 256, 4096).rearrange("p (e n) -> p e n", e=16)
        o0 = o0 + 256 + 4096
        z = lambda k, n=16: ar(o0 + 64 * k, n)
        rw = RW.rearrange("p (k e) -> p k e", k=8)
        early = [proj_b(ready=ready)]
        P.wait(t_r, *ready, *acc_free[1])
        V.wait(ready[3])
        for i in range(2):
            for k in range(8):
                x = pe.matmul(bank[1][:, 16 * i:16 * i + 16], FT[:, k, 128 * i:128 * i + 128], rw[:, k, :],
                              start=k == 0, stop=k == 7)
        t = P.mark(x)
        A.wait(t, V.now())
        sg = z(0, 32)
        t = A(ac.activation(sg, bank[1][:, 0:32], ACT.Sigmoid))
        acc_free[1] = (t,)
        V.wait(t, t_r)
        cmb = z(1, 32)

        def rank(dst, v, n, tie, c1, c2):
            g = v.shape[1]
            vi = v.rearrange("p g (i j) -> p g i j", j=1).to_broadcast([128, g, n, n])
            vj = v.rearrange("p g (i j) -> p g i j", i=1).to_broadcast([128, g, n, n])
            tt = tie.rearrange("p (g i j) -> p g i j", g=1, i=n).to_broadcast([128, g, n, n])
            V(ve.tensor_tensor(c1, vj, vi, ALU.is_gt))
            V(ve.tensor_tensor(c2, vj, vi, ALU.is_equal))
            V(ve.tensor_tensor(c2, c2, tt, MUL))
            V(ve.tensor_tensor(c1, c1, c2, ADD))
            V(ve.tensor_reduce(dst, c1, AX, ADD))

        for i in range(2):
            s = sg[:, 16 * i:16 * i + 16]
            sel = z(2).rearrange("p (g e) -> p g e", g=4)
            c1 = z(3, 64).rearrange("p (g i j) -> p g i j", g=4, i=4)
            c2 = z(4, 64).rearrange("p (g i j) -> p g i j", g=4, i=4)
            rk = z(5).rearrange("p (g e) -> p g e", g=4)
            V(ve.tensor_tensor(z(2), s, RB, ADD))
            rank(rk, sel, 4, LT, c1, c2)
            V(ve.tensor_scalar(rk, rk, 1.5, None, ALU.is_lt))
            V(ve.tensor_tensor(sel, sel, rk, MUL))
            gs = z(6, 4)
            V(ve.tensor_reduce(gs, sel, AX, ADD))
            gr = z(7, 4)
            rank(gr.rearrange("p (g e) -> p g e", g=1), gs.rearrange("p (g e) -> p g e", g=1), 4, LT,
                 c1[:, 0:1], c2[:, 0:1])
            V(ve.tensor_scalar(gr, gr, 0.5, None, ALU.is_lt))
            V(ve.tensor_tensor(rk, rk, gr.rearrange("p (g e) -> p g e", e=1).to_broadcast([128, 4, 4]), MUL))
            V(ve.tensor_tensor(z(5), z(5), s, MUL))
            V(ve.tensor_reduce(z(8, 1), z(5), AX, ADD))
            V(ve.reciprocal(z(8, 1), z(8, 1)))
            V(ve.tensor_scalar(cmb[:, 16 * i:16 * i + 16], z(5), z(8, 1), None, MUL))
        t_cmb = V.now()
        early += [proj_b(), proj_b(), proj_b()]
        P.wait(t_cmb)
        for q in range(8):
            b = q % 4
            P.wait(*acc_free[b])
            for m in range(2):
                for i in range(2):
                    e = 2 * q + m
                    w = cmb[:, 16 * i + e:16 * i + e + 1].to_broadcast([128, 128])
                    x = pe.matmul(bank[b][:, 256 * m + 128 * i:256 * m + 128 * i + 128], w, ident, start=True, stop=True)
            A.wait(P.mark(x))
            acc_free[b] = (A.mark(ac.copy(CB[:, 2 * q:2 * q + 2, :], bank[b][:, :])),)
        t_cb = A.now()
        V.wait(t_cb)

        o0 = o0 + 1024
        TG = [ar(o0 + 1024 * i, 512).rearrange("p (m n) -> p m n", m=2) for i in range(2)]
        TU = [ar(o0 + 1024 * i + 512, 512).rearrange("p (m n) -> p m n", m=2) for i in range(2)]
        ring_y = {}

        def yslot(n):
            s = 2 * (n % 4)
            return Y8[0][:, s:s + 2, :], Y8[1][:, s:s + 2, :]

        for e in range(17):
            if e < 16:
                (b,), tg = early.pop(0) if early else proj_b()
                A.wait(tg, ring_y.get(("v", e - 2)))
                tg = A.mark(ac.activation(TG[e % 2], bank[b][:, :], ACT.Silu))
                R.put(b, tg)
                (b,), tu = early.pop(0) if early else proj_b()
                V.wait(tg, tu)
                R.put(b, V(ve.tensor_tensor(TU[e % 2], TG[e % 2], bank[b][:, :], MUL)))
                cb = CB[:, e:e + 1, :].to_broadcast([128, 2, 256])
                V(ve.tensor_tensor(TU[e % 2], TU[e % 2], cb, MUL))
                A.wait(ring_y.get(("p", e - 4)))
                V.wait(ring_y.get(("p", e - 4)))
                hi, lo = yslot(e)
                ring_y["v", e] = hi_lo(hi, lo, TU[e % 2])
            if e:
                t = proj_a(Y8, 2 * ((e - 1) % 4), e == 1, e == 16, (ring_y["v", e - 1],))
                ring_y["p", e - 1] = t
        V.wait(t_g)
        add_out(t, gate=G2B[:, :])
        rstd()
        for i in range(2):
            for h in range(2):
                x = X[i][:, 512 * h:512 * h + 512]
                t = V.mark(ve.scalar_tensor_tensor(x, x, ST[:, 8 + i:9 + i], FG[:, 512 * h:512 * h + 512], MUL, MUL))
                A.wait(t)
                x_done[2 * i + h] = t
                square_half(x, 2 * i + h)
        V.wait(V.now())

        def ffn(i):
            ready = norm(X, prm("norm_ffn_2", 8 * i, 8), None, H8)
            ry = {}
            for j in range(17):
                if j < 16:
                    (b,), t = proj_b(ready=ready if j == 0 else None)
                    tr, th = TG[j % 2], TU[j % 2]
                    A.wait(t, ry.get(("v", j - 2)))
                    t = A(ac.activation(tr, bank[b][:, :], ACT.Relu))
                    R.put(b, t)
                    hi, lo = yslot(j)
                    A.wait(ry.get(("p", j - 4)))
                    th_ = A.mark(ac.activation(hi, tr, ACT.Square))
                    V.wait(t)
                    V(ve.tensor_tensor(th, tr, tr, MUL))
                    V.wait(th_, ry.get(("p", j - 4)))
                    ry["v", j] = V(ve.tensor_tensor(lo, th, f32(hi), SUB))
                if j:
                    t = proj_a(Y8, 2 * ((j - 1) % 4), j == 1, j == 16, (ry["v", j - 1],))
                    ry["p", j - 1] = t
            add_out(t)

        def head_norm(src_ps, gain, dst, t, sq):
            A.wait(t)
            ta = A.mark(ac.activation(sq, src_ps, ACT.Square))
            V.wait(ta)
            for m in range(2):
                V.mark(ve.tensor_scalar(dst[:, m, :], src_ps[:, 256 * m:256 * m + 256], gain[m], None, MUL))
            return ta, V.now()

        def ret(i, li):
            o = 4096
            S.wait(V.now(), A.now(), P.now())
            t_c = small(ar(o + 4096, 2048), I["consts"][:, C_RET:C_RET + 2048], f"ret{i}")
            ready = norm(X, prm("norm_mix_2", 8 * li, 8), None, H8)
            QK = [ar(2048 * s, 2048).rearrange("p (h m n) -> p h m n", h=4, m=2) for s in range(2)]
            VV = ar(o, 4096).rearrange("p (i n) -> p i n", i=2)
            RM = ar(o + 4096, 1536).rearrange("p (h n) -> p h n", h=4)
            COS, SIN = ar(o + 5632, 256), ar(o + 5888, 256)
            SQ2 = [ar(o + 6144, 512), ar(o + 8448, 512)]
            RSD = ar(o + 6656, 256)
            M1, M2 = ar(o + 6912, 512), ar(o + 7424, 512)
            QG = [ar(b_, 512).rearrange("p (m n) -> p m n", m=2) for b_ in (o + 7936, o + 8960)]
            o2 = o + 8448
            PP = SQ2[0][:, 0:384]
            SGT = ar(o2, 1024).rearrange("p (t n) -> p t n", t=4)
            YN = [ar(o2 + 1024 + 512 * s, 512) for s in range(2)]
            YT = ar(o + 6912, 1024).rearrange("p (t n) -> p t n", t=4)
            V.wait(t_c, P.now(), A.now(), *ready)
            A.wait(P.now(), V.now(), *ready)
            cosb = COS.rearrange("p (m n) -> p m n", m=1).to_broadcast([128, 2, 256])
            sinb = SIN.rearrange("p (m n) -> p m n", m=1).to_broadcast([128, 2, 256])
            m1, m2 = (x.rearrange("p (m n) -> p m n", m=2) for x in (M1, M2))
            pend = None

            def rotate(h8, sq_t, gain_t):
                s, h, i2 = h8 // 4, h8 % 4, h8 % 2
                b = R.get()
                P.wait(sq_t)
                for m in range(2):
                    x = pe.matmul(bank[b][:, 0:256], ones, SQ2[i2][:, 256 * m:256 * m + 256], start=m == 0, stop=m == 1)
                t = P.mark(x)
                A.wait(t, V.now())
                t = A.mark(ac.activation(RSD, bank[b][:, 0:256], ACT.Sqrt, bias=eps, scale=1.0 / 256))
                R.put(b, t)
                V.wait(t, gain_t)
                V(ve.reciprocal(RSD, RSD))
                g = QG[i2]
                V(ve.tensor_tensor(g, g, RSD.rearrange("p (m n) -> p m n", m=1).to_broadcast([128, 2, 256]), MUL))
                V.mark(ve.tensor_tensor(m1, g, cosb, MUL))
                V(ve.tensor_tensor(m2, g, sinb, MUL))
                dst = QK[s][:, h, :, :]
                V.mark(ve.tensor_tensor(dst[:, 0, :], m1[:, 0, :], m2[:, 1, :], SUB))
                V(ve.tensor_tensor(dst[:, 1, :], m2[:, 0, :], m1[:, 1, :], ADD))
                return t

            read = {}
            for h8 in range(9):
                if h8 < 8:
                    bs, t = proj_b(ready=ready if h8 == 0 else None)
                    g = [prm(("ret_q_norm_2", "ret_k_norm_2")[h8 // 4], 2 * i + m) for m in range(2)]
                    A.wait(read.get(h8 - 2))
                    ta, tv = head_norm(bank[bs[0]][:, :], g, QG[h8 % 2], t, SQ2[h8 % 2])
                    R.put(bs[0], ta, tv)
                if pend is not None:
                    read[pend[0]] = rotate(*pend)
                pend = (h8, ta, tv)
            t_qk = V.now()
            for c in range(2):
                for j in range(4):
                    t = proj_a(H8, 2 * j, j == 0, j == 3)
                A.wait(t)
                V.wait(t)
                for q in range(4):
                    m, h = q // 2, q % 2
                    dst = VV[:, m, 1024 * c + 512 * h:1024 * c + 512 * h + 512]
                    if q % 2:
                        acc_free[q] = (A(ac.copy(dst, bank[q][:, :])),)
                    else:
                        acc_free[q] = (V(ve.tensor_copy(dst, bank[q][:, :])),)
            t_vv = (A.now(), V.now())
            t_yl = t_yt = None
            for h in range(5):
                if h < 4:
                    b = R.get()
                    P.wait(*t_vv, t_qk)
                    q, k = QK[0][:, h, :, :], QK[1][:, h, :, :]
                    for m in range(2):
                        pe.matmul(bank[b][:, 0:256], k[:, m, 0:128], q[:, m, :], start=m == 0, stop=m == 1)
                    for m in range(2):
                        x = pe.matmul(bank[b][:, 256:384], k[:, m, 128:256], q[:, m, 128:256], start=m == 0, stop=m == 1)
                    t = P.mark(x)
                    V.wait(t)
                    t_p = V(ve.tensor_tensor(PP, bank[b][:, 0:384], RM[:, h, :], MUL))
                    R.put(b, t_p)
                    for j in range(2):
                        (b,), t = proj_b()
                        A.wait(t, t_yt)
                        R.put(b, A.mark(ac.activation(SGT[:, 2 * j:2 * j + 2, :], bank[b][:, :], ACT.Silu)))
                    vc = slice(512 * h, 512 * h + 512)
                    P.wait(t_p)
                    by = [R.get(), R.get()]
                    x = pe.matmul(bank[by[0]][:, :], PP[:, 0:128], VV[:, 0, vc], start=True, stop=True)
                    ty0 = P.mark(x)
                    pe.matmul(bank[by[1]][:, :], PP[:, 128:256], VV[:, 0, vc], start=True, stop=False)
                    x = pe.matmul(bank[by[1]][:, :], PP[:, 256:384], VV[:, 1, vc], start=False, stop=True)
                    ty1 = P.mark(x)
                    for m in range(2):
                        V.wait((ty0, ty1)[m])
                        V(ve.bn_stats(SM[:, 208:214], bank[by[m]][:, :]))
                        V(ve.bn_aggr(SM[:, 214 + 2 * m:216 + 2 * m], SM[:, 208:214]))
                    A.wait(V.now())
                    for m in range(2):
                        A(ac.activation(SM[:, 218 + m:219 + m], SM[:, 215 + 2 * m:216 + 2 * m], ACT.Sqrt, bias=eps))
                    V.wait(A.now())
                    V(ve.reciprocal(SM[:, 218:220], SM[:, 218:220]))
                    for m in range(2):
                        t = V(ve.tensor_scalar(YN[m], bank[by[m]][:, :], SM[:, 214 + 2 * m:215 + 2 * m],
                                               SM[:, 218 + m:219 + m], SUB, MUL))
                        R.put(by[m], t)
                if h:
                    for j in range(2):
                        k0 = 4 * ((h - 1) % 2) + 2 * j
                        t_o = proj_a(Y8, k0, h == 1 and j == 0, h == 4 and j == 1, (t_yl,))
                if h < 4:
                    P.wait(t)
                    for jj in range(2):
                        b = R.get()
                        for m in range(2):
                            for s in range(2):
                                f = 2 * jj + m
                                x = pe.transpose(bank[b][:, 256 * m + 128 * s:256 * m + 128 * s + 128],
                                                 YN[s][:, 128 * f:128 * f + 128], ident)
                        A.wait(P.mark(x), V.now())
                        for m in range(2):
                            f = 4 * h + 2 * jj + m
                            A.mark(ac.activation(YT[:, 2 * jj + m, :], bank[b][:, 256 * m:256 * m + 256], ACT.Identity,
                                                 scale=prm("ret_gn_w_2", 16 * i + f), bias=prm("ret_gn_b_2", 16 * i + f)))
                        R.put(b, A.now())
                    V.wait(A.now())
                    t_yt = V(ve.tensor_tensor(YT, YT, SGT, MUL))
                    A.wait(P.now())
                    V.wait(P.now())
                    s = slice(4 * (h % 2), 4 * (h % 2) + 4)
                    t_yl = hi_lo(Y8[0][:, s, :], Y8[1][:, s, :], YT)
            add_out(t_o)

        ret(0, 0)
        ffn(0)

        o = 4096
        HP = ar(o, 2288).rearrange("p (t n) -> p t n", t=8)
        CA = ar(o + 2288, 2048).rearrange("p (t n) -> p t n", t=8)
        CG = ar(o + 4336, 512).rearrange("p (m n) -> p m n", m=2)
        CQ = ar(o + 4848, 2048).rearrange("p (t n) -> p t n", t=8)
        BO = ar(o + 6896, 1024)
        LR = ar(o + 7920, 256)
        LRR = ar(o + 8176, 256)
        NDG = 16
        DG = ar(0, 128 * NDG).rearrange("p (w n) -> p w n", w=NDG)
        S.wait(V.now(), A.now(), P.now())
        t_bo = small(BO, I["conv_pw2_b_2"].to_broadcast([128, 1024]), "conv")
        ready = norm(X, prm("norm_mix_2", 8, 8), None, H8)
        V(ve.memset(HP[:, :, 0:30], 0.0))
        ON_PE = (6, 7)
        taps = [(f, w) for f in ON_PE for w in range(31)] + [(5, w) for w in range(16, 31)]
        dgt, dgu = {}, {}

        def diagonal(n):
            if n < len(taps):
                f, w = taps[n]
                A.wait(dgu.get(n - NDG))
                dgt[n] = A.mark(ac.mul(DG[:, n % NDG, :], ident, prm("conv_dw_w_2", 8 * w + f)))

        A.wait(A.now(), *ready)
        for n in range(NDG):
            diagonal(n)
        t_tile = {}

        def dve_taps():
            for pair in ((0, 1), (2, 3), (4, 5)):
                for f in pair:
                    V.mark(ve.tensor_scalar(CA[:, f, :], HP[:, f, 0:256], prm("conv_dw_w_2", f),
                                            prm("conv_dw_b_2", f), MUL, ADD))
                yield
                for w in range(1, 31):
                    both = pair if w < 16 or pair[1] != 5 else pair[:1]
                    for f in both:
                        V.wait((V.sem, V.n - len(both) + 1))
                        V.mark(ve.scalar_tensor_tensor(CA[:, f, :], HP[:, f, w:w + 256], prm("conv_dw_w_2", 8 * w + f),
                                                       CA[:, f, :], MUL, ADD))
                    yield
                for f in pair:
                    t_tile[f] = V.now()

        steps = dve_taps()
        for j in range(4):
            (ba,), ta = proj_b(ready=ready if j == 0 else None)
            (bg,), tg = proj_b()
            A.wait(tg, V.now())
            for m in range(2):
                A.mark(ac.activation(CG[:, m, :], bank[bg][:, 256 * m:256 * m + 256], ACT.Sigmoid,
                                     bias=prm("conv_pw1_b_2", 8 + 2 * j + m)))
            R.put(bg, A.now())
            V.wait(ta, A.now())
            for m in range(2):
                f = 2 * j + m
                V.mark(ve.scalar_tensor_tensor(HP[:, f, 30:286], bank[ba][:, 256 * m:256 * m + 256],
                                               prm("conv_pw1_b_2", f), CG[:, m, :], ADD, MUL))
            R.put(ba, V.now())
            V.wait(V.now())
            t_hp = V.now()
            if j < 3:
                for _ in range(11):
                    next(steps)
        P.wait(t_hp)
        bp, bh = R.get(), R.get()
        for n, (f, w) in enumerate(taps):
            P.wait(dgt[n])
            bf, c = (bh, 0) if f == 5 else (bp, 256 * ON_PE.index(f))
            x = pe.matmul(bank[bf][:, c:c + 256], DG[:, n % NDG, :], HP[:, f, w:w + 256],
                          start=w == (16 if f == 5 else 0), stop=w == 30)
            if n % 4 == 3 or n == len(taps) - 1:
                t = P.mark(x)
                for q in range(n - n % 4, n + 1):
                    dgu[q] = t
            if n % 4 == 3 or n == len(taps) - 1:
                for q in range(NDG + n - n % 4, NDG + n + 1):
                    diagonal(q)
        A.wait(t)
        for f in ON_PE:
            c = 256 * ON_PE.index(f)
            A.mark(ac.activation(CA[:, f, :], bank[bp][:, c:c + 256], ACT.Identity, bias=prm("conv_dw_b_2", f)))
            t_tile[f] = A.now()
        R.put(bp, A.now())
        for _ in steps:
            pass
        V.wait(t, V.now())
        V(ve.tensor_tensor(CA[:, 5, :], CA[:, 5, :], bank[bh][:, 0:256], ADD))
        t_tile[5] = V.now()
        R.put(bh, V.now())

        b = R.get()
        order = list(ON_PE) + [f for f in range(8) if f not in ON_PE]
        for n, f in enumerate(order):
            P.wait(t_tile[f])
            x = pe.matmul(bank[b][:, 0:256], ones, CA[:, f, :], start=n == 0, stop=n == 7)
        V.wait(P.mark(x), t_tile[ON_PE[-1]])
        t = V(ve.tensor_scalar(LR, bank[b][:, 0:256], 1.0 / D, None, MUL))
        R.put(b, t)
        pairs = lambda ap: ap.rearrange("p (t n) -> p t n", t=1).to_broadcast([128, 2, 256])
        b = R.get()
        for q in range(4):
            s = slice(2 * q, 2 * q + 2)
            t = V.mark(ve.tensor_tensor(CA[:, s, :], CA[:, s, :], pairs(LR), SUB))
            A.wait(t)
            t = A.mark(ac.activation(CQ[:, s, :], CA[:, s, :], ACT.Square))
            P.wait(t)
            for f in (2 * q, 2 * q + 1):
                x = pe.matmul(bank[b][:, 0:256], ones, CQ[:, f, :], start=f == 0, stop=f == 7)
        V.wait(V.now())
        A.wait(P.mark(x))
        t = A.mark(ac.activation(LRR, bank[b][:, 0:256], ACT.Sqrt, bias=eps, scale=1.0 / D))
        R.put(b, t)
        V.wait(t)
        V(ve.reciprocal(LRR, LRR))
        tq = []
        for q in range(4):
            s = slice(2 * q, 2 * q + 2)
            tq.append(V.mark(ve.tensor_tensor(CA[:, s, :], CA[:, s, :], pairs(LRR), MUL)))
        t_yj = {}
        for q in range(4):
            s = slice(2 * q, 2 * q + 2)
            A.wait(tq[q])
            for f in (2 * q, 2 * q + 1):
                A.mark(ac.activation(CQ[:, f, :], CA[:, f, :], ACT.Silu, scale=prm("conv_ln_w_2", f),
                                     bias=prm("conv_ln_b_2", f)))
            A.wait(A.now())
            t = A.mark(ac.copy(Y8[0][:, s, :], CQ[:, s, :]))
            V.wait(t)
            t_yj[q] = V.mark(ve.tensor_tensor(Y8[1][:, s, :], CQ[:, s, :], f32(Y8[0][:, s, :]), SUB))
        for j in range(4):
            t = proj_a(Y8, 2 * j, j == 0, j == 3, (t_yj[j],))
        V.wait(t_bo)
        add_out(t, bias=BO)
        ffn(1)

        QK = [ar(2048 * s, 2048).rearrange("p (k n) -> p k n", k=8) for s in range(2)]
        o = 4096
        VS = ar(o, 2048).rearrange("p (i n) -> p i n", i=2)
        YS = [ar(o + 2048 + 1024 * i, 1024) for i in range(2)]
        SQ3 = [ar(o + 4096 + 4900 * i, 512) for i in range(2)]
        RS3 = ar(o + 4608, 512)
        MSK = ar(o + 5120, 384)
        ZERO = ar(o + 5504, 256)
        ZZ = [ar(o + 5760 + 384 * i, 384) for i in range(2)]
        UU = [ar(o + 6528 + 384 * i, 384) for i in range(2)]
        GG = [ar(o + 7296 + 384 * i, 384) for i in range(2)]
        CC = [ar(o + 8064 + 386 * i, 386) for i in range(2)]
        AT = [ar(o + 9508 + 384 * i, 384) for i in range(2)]
        S.wait(V.now(), A.now(), P.now())
        t_m = small(MSK, I["consts"][:, C_SB:C_SB + 384], "sb")
        ready = norm(X, prm("norm_mix_2", 16, 8), None, H8)
        V.wait(t_m, *ready)
        A.wait(V.now(), *ready)
        V(ve.memset(ZERO, 0.0))
        for i in range(2):
            V(ve.memset(CC[i], 1.0))
        pend = None

        def fin_norm(j, ta, tv):
            dst = QK[j // 4][:, 2 * (j % 4):2 * (j % 4) + 2, :]
            b = R.get()
            P.wait(ta)
            tp = P.mark(pe.matmul(bank[b][:, :], blk, SQ3[j % 2], start=True, stop=True))
            A.wait(tp, V.now())
            t = A.mark(ac.activation(RS3, bank[b][:, :], ACT.Sqrt, bias=eps, scale=1.0 / 64))
            R.put(b, t)
            V.wait(t, tv)
            V(ve.reciprocal(RS3, RS3))
            V(ve.tensor_tensor(dst, dst, RS3.rearrange("p (m n) -> p m n", m=2), MUL))
            return tp

        read = {}
        for j in range(9):
            if j < 8:
                bs, t = proj_b(ready=ready if j == 0 else None)
                g = [prm(("sb_q_norm_2", "sb_k_norm_2")[j // 4], 0)] * 2
                A.wait(read.get(j - 2))
                ta, tv = head_norm(bank[bs[0]][:, :], g, QK[j // 4][:, 2 * (j % 4):2 * (j % 4) + 2, :], t, SQ3[j % 2])
                R.put(bs[0], ta, tv)
            if pend is not None:
                read[pend[0]] = fin_norm(*pend)
            pend = (j, ta, tv)
        for j in range(4):
            t = proj_a(H8, 2 * j, j == 0, j == 3)
        A.wait(t)
        V.wait(t)
        for q in range(4):
            m, h = q // 2, q % 2
            dst = VS[:, m, 512 * h:512 * h + 512]
            if q % 2:
                acc_free[q] = (A(ac.copy(dst, bank[q][:, :])),)
            else:
                acc_free[q] = (V(ve.tensor_copy(dst, bank[q][:, :])),)
        P.wait(A.now(), V.now())
        hist = {}

        def sb_scores(h):
            q, k = QK[0], QK[1]
            r, f = slice(64 * (h % 2), 64 * (h % 2) + 64), h // 2
            b = R.get()
            pe.matmul(bank[b][:, 0:128], q[r, f, 0:128], k[r, f, 0:128], start=True, stop=True)
            x = pe.matmul(bank[b][:, 128:384], q[r, f, 128:256], k[r, f, 0:256], start=True, stop=True)
            return b, P.mark(x)

        def sb_vec(h, b, t):
            i = h % 2
            V.wait(t, hist.get(("a", h - 2)))
            t = V.mark(ve.scalar_tensor_tensor(ZZ[i], bank[b][:, 0:384], 0.125, MSK, MUL, ADD))
            R.put(b, t)
            A.wait(t, hist.get(("scan", h - 2)), hist.get(("p", h - 2)))
            tu = A.mark(ac.activation(UU[i], ZZ[i], ACT.Sigmoid, scale=-1.0))
            hist["a", h] = A.mark(ac.activation(GG[i], ZZ[i], ACT.Sigmoid))
            hist["u", h] = tu

        def sb_scan(h):
            i = h % 2
            c = CC[i]
            V.wait(hist["u", h])
            V.mark(ve.tensor_tensor_scan(c[:, 127::-1], UU[i][:, 127::-1], ZERO[:, 0:128], 1.0, MUL, ADD))
            V.mark(ve.tensor_tensor_scan(c[:, 384:128:-1], UU[i][:, 383:127:-1], ZERO, 1.0, MUL, ADD))
            hist["scan", h] = V.now()
            V.wait(V.now(), hist["a", h])
            V.mark(ve.tensor_tensor(GG[i][:, 0:128], GG[i][:, 0:128], c[:, 1:129], MUL))
            V.mark(ve.tensor_tensor(GG[i][:, 128:384], GG[i][:, 128:384], c[:, 130:386], MUL))
            return V.now()

        def sb_turn(h, t):
            i = h % 2
            P.wait(t)
            b = R.get()
            for s in range(3):
                x = pe.transpose(bank[b][:, 128 * s:128 * s + 128], GG[i][:, 128 * s:128 * s + 128], ident)
            t = P.mark(x)
            hist["p", h] = t
            A.wait(t, hist.get(("y", h - 2)))
            hist["at", h] = A.mark(ac.copy(AT[i], bank[b][:, 0:384]))
            R.put(b, hist["at", h])

        def sb_out(h):
            i = h % 2
            P.wait(hist["at", h])
            vc = slice(64 * h, 64 * h + 64)
            q, oc = h // 8, slice(64 * (h % 8), 64 * (h % 8) + 64)
            pe.matmul(bank[q][:, oc], AT[i][:, 0:128], VS[:, 0, vc], start=True, stop=True)
            pe.matmul(bank[2 + q][:, oc], AT[i][:, 128:256], VS[:, 0, vc], start=True, stop=False)
            x = pe.matmul(bank[2 + q][:, oc], AT[i][:, 256:384], VS[:, 1, vc], start=False, stop=True)
            hist["y", h] = P.mark(x)

        def sb_rows(half):
            A.wait(hist["y", 8 * half + 7])
            for i in range(2):
                q = half + 2 * i
                acc_free[q] = (A.mark(ac.copy(YS[i][:, 512 * half:512 * half + 512], bank[q][:, :])),)
            return A.now()

        tt, sc, rows = {}, {0: sb_scores(0)}, {}
        for h in range(19):
            if h < 15:
                sc[h + 1] = sb_scores(h + 1)
            if h < 16:
                sb_vec(h, *sc[h])
            if 1 <= h < 17:
                tt[h - 1] = sb_scan(h - 1)
                sb_turn(h - 1, tt[h - 1])
            if 2 <= h < 18:
                sb_out(h - 2)
            if h in (10, 18):
                rows[h // 18] = sb_rows(h // 18)
        for q in range(4):
            P.wait(rows[q // 2])
            b = R.get()
            for m in range(2):
                for i in range(2):
                    k = 2 * q + m
                    x = pe.transpose(bank[b][:, 256 * m + 128 * i:256 * m + 128 * i + 128],
                                     YS[i][:, 128 * k:128 * k + 128], ident)
            t = P.mark(x)
            A.wait(t)
            s = slice(2 * q, 2 * q + 2)
            t = A(ac.copy(Y8[0][:, s, :], bank[b][:, :]))
            V.wait(t)
            t_y = V(ve.tensor_tensor(Y8[1][:, s, :], bank[b][:, :].rearrange("p (m n) -> p m n", m=2),
                                     f32(Y8[0][:, s, :]), SUB))
            R.put(b, t_y)
            t_yj[q] = t_y
        for j in range(4):
            t = proj_a(Y8, 2 * j, j == 0, j == 3, (t_yj[j],))
        add_out(t)
        ffn(2)
        ret(1, 3)
        ffn(3)

        FN = ar(4096, 1024)
        S.wait(V.now(), A.now(), P.now())
        t_f = small(FN, I["final_norm_2"].rearrange("(o n) -> o n", o=1).to_broadcast([128, 1024]), "final")
        rstd()
        V.wait(t_f)
        for i in range(2):
            t = V(ve.scalar_tensor_tensor(XN[i], X[i][:, :], ST[:, 8 + i:9 + i], FN, MUL, MUL))
            S.wait(t)
            nc.sync.dma_start(out[0, 128 * i:128 * i + 128, :], XN[i]).then_inc(s_out, 16)
        nc.sync.wait_ge(s_out, 32)
        assert state["next"] == len(items)


_INS = [
    "x", "c", "ctx", "c_ctx", "w_mod", "b_mod", "norm1_g", "norm2_g", "hg_w_in", "hg_lb_fwd", "hg_lb_bwd", "hg_gnorm",
    "hg_w_out", "router_w", "router_b", "moe_w_gate", "moe_w_up", "moe_w_down", "final_g", "norm_mix_2", "norm_ffn_2",
    "ret_w_in_2", "ret_q_norm_2", "ret_k_norm_2", "ret_gn_w_2", "ret_gn_b_2", "ret_w_out_2", "conv_pw1_w_2",
    "conv_pw1_b_2", "conv_dw_w_2", "conv_dw_b_2", "conv_ln_w_2", "conv_ln_b_2", "conv_pw2_w_2", "conv_pw2_b_2",
    "sb_w_in_2", "sb_q_norm_2", "sb_k_norm_2", "sb_w_out_2", "ffn_w1_2", "ffn_w2_2", "final_norm_2",
]


def constants():
    import numpy as np

    c = np.zeros((128, C_ALL), np.float32)
    p = np.arange(128)
    c[:, C_ID:C_ID + 128] = np.eye(128)
    c[:, C_ONE:C_ONE + 128] = 1.0
    c[:, C_BLK:C_BLK + 128] = p[:, None] // 64 == p[None, :] // 64
    c[[0, 2], C_SEL:C_SEL + 128] = 1.0
    same = p[:, None] // 64 == p[None, :] // 64
    c[:, C_MF:C_MF + 128] = same & (p[:, None] <= p[None, :])
    c[:, C_MB:C_MB + 128] = same & (p[:, None] >= p[None, :])
    t = np.arange(512)
    c[:, C_RF:C_RF + 512] = np.where(t < 256, t % 64 != 0, t != 256)
    c[:, C_RB:C_RB + 512] = np.where(t < 256, t % 64 != 63, t != 511)
    s, q = np.arange(256)[:, None], np.arange(256)[None, :]
    for h in range(4):
        lg = np.log(1.0 - 2.0 ** (-5.0 - h))
        m = np.where(s // 64 == q // 64, np.exp(lg * np.abs(q - s)), np.where(s // 64 < q // 64, np.exp(lg * (q - s)), 0.0))
        m = m / 16.0
        c[:, C_RET + 384 * h:C_RET + 384 * h + 256] = m[0:128, :]
        c[:, C_RET + 384 * h + 256:C_RET + 384 * h + 384] = m[128:256, 128:256]
    f = np.float32(10000.0) ** (-np.arange(128, dtype=np.float32) / np.float32(128))
    ang = (np.arange(256, dtype=np.float32)[None, :] * f[:, None].astype(np.float32)).astype(np.float64)
    c[:, C_COS:C_COS + 256] = np.cos(ang)
    c[:, C_SIN:C_SIN + 256] = np.sin(ang)
    diag = np.where(p[None, :] < p[:, None], 0.0, NEG)
    c[:, C_SB:C_SB + 128] = diag
    c[:, C_SB + 256:C_SB + 384] = diag
    c[:, C_LT:C_LT + 16] = (np.arange(4)[None, :] < np.arange(4)[:, None]).reshape(-1)
    return c


def kernel(**inputs):
    import numpy as _np
    import concourse.bacc as _bacc
    from concourse import mybir as _mybir
    from concourse.bass_utils import run_bass_kernel_spmd as _run

    nc = _bacc.Bacc("TRN2", target_bir_lowering=False, num_devices=1)
    arrays, args = {}, {}
    for name in _INS + ["consts"]:
        a = constants() if name == "consts" else _np.ascontiguousarray(inputs[name])
        arrays[f"in_{name}"] = a
        args[name] = nc.dram_tensor(f"in_{name}", a.shape, _mybir.dt.from_np(a.dtype), kind="ExternalInput").ap()
    out = nc.dram_tensor("out_0", (1, 256, 1024), F32, kind="ExternalOutput").ap()
    build(nc, args, out)
    r = _run(nc, [arrays], core_ids=[0])
    return r.results[0]["out_0"]
```

```python
from contextlib import ExitStack

import concourse.bass as bass
from concourse import mybir

F32 = mybir.dt.float32
F32R = mybir.dt.float32r
I32 = mybir.dt.int32
ALU = mybir.AluOpType
ACT = mybir.ActivationFunctionType
AX = mybir.AxisListType.X
MUL, ADD, SUB = ALU.mult, ALU.add, ALU.subtract

D = 1024
EPS = 1e-6
NRAW = 8
NEG = -1e30

C_ID, C_ONE, C_BLK, C_SEL, C_MF, C_MB, C_RF, C_RB = 0, 128, 256, 384, 512, 640, 768, 1280
C_END = 1792
C_RET, C_COS, C_SIN, C_SB, C_LT = 1792, 3328, 3584, 3840, 4224
C_ALL = 4240

PARAMS = [
    [("c", 8), ("c_ctx", 8), ("norm1_g", 8), ("norm2_g", 8), ("hg_lb_fwd", 16), ("hg_lb_bwd", 16),
     ("b_mod", 48), ("hg_gnorm", 1)],
    [("norm_mix_2", 32), ("norm_ffn_2", 32), ("ret_q_norm_2", 4), ("ret_k_norm_2", 4), ("ret_gn_w_2", 32)],
    [("ret_gn_b_2", 32), ("conv_pw1_b_2", 16), ("conv_dw_b_2", 8), ("conv_ln_w_2", 8), ("conv_ln_b_2", 8),
     ("sb_q_norm_2", 1), ("sb_k_norm_2", 1)],
    [("conv_dw_w_2", 124)],
    [("conv_dw_w_2", 124)],
]


class Engine:

    def __init__(self, eng, sem):
        self.e, self.sem, self.n, self.seen = eng, sem, 0, {}

    def mark(self, ins):
        ins.then_inc(self.sem, 1)
        self.n += 1
        return (self.sem, self.n)

    def __call__(self, ins):
        t = self.mark(ins)
        self.wait(t)
        return t

    def now(self):
        return (self.sem, self.n)

    def wait(self, *tokens):
        for t in tokens:
            if t is not None and t[1] > self.seen.get(t[0], 0):
                self.e.wait_ge(t[0], t[1])
                self.seen[t[0]] = t[1]


def build(nc, I, out):
    with ExitStack() as ctx:
        sem = lambda n: ctx.enter_context(nc.semaphore(n))
        sb = lambda n, s, d=F32: ctx.enter_context(nc.sbuf_tensor(n, s, d))
        V, A, P, G, S = (Engine(e, sem(n)) for e, n in (
            (nc.vector, "s_dve"), (nc.scalar, "s_act"), (nc.tensor, "s_pe"), (nc.gpsimd, "s_pool"), (nc.sync, "s_sp")))
        ve, ac, pe, po = nc.vector, nc.scalar, nc.tensor, nc.gpsimd
        s_out = sem("s_out")

        bank = [ctx.enter_context(nc.psum_tensor(f"bank{i}", [128, 512], F32)) for i in range(8)]

        X = [sb(f"X{i}", [128, D])[:, :] for i in range(2)]
        NR, NS = 3, 3
        raw = [sb(f"raw{i}", [128, 2048]) for i in range(NR)]
        whi = [sb(f"whi{i}", [128, 2048], F32R) for i in range(NS)]
        wlo = [sb(f"wlo{i}", [128, 2048], F32R) for i in range(NS)]
        HH, HL = sb("HH", [128, 4096], F32R), sb("HL", [128, 4096], F32R)
        YH, YL = sb("YH", [128, 2048], F32R), sb("YL", [128, 2048], F32R)
        CST = sb("CST", [128, C_END])
        PRM = sb("PRM", [128, 540])
        SM = sb("SM", [128, 256])
        CS = sb("CS", [128, 32], F32R)
        ARENA = sb("ARENA", [128, 14848])
        ar = lambda o, n: ARENA[:, o:o + n]
        ident, ones, blk = CST[:, 0:128], CST[:, 128:256], CST[:, 256:384]
        f32 = lambda ap: ap.bitcast(F32)

        s_ld = [sem(f"s_ld{i}") for i in range(NR)]
        group = {}

        def small(dst, src, name):
            if name not in group:
                group[name] = [sem(f"s_{name}"), 0]
            g = group[name]
            nc.sync.dma_start(dst, src).then_inc(g[0], 16)
            g[1] += 16
            return (g[0], g[1])

        col, pt, base = {}, [], 0

        def load_rows(k, name):
            nonlocal base
            r, dst = 0, ar(5000 if k == 0 else 7000 + 128 * k, 128)
            for what, n in PARAMS[k]:
                ap = I[what]
                if what == "conv_dw_w_2":
                    src = ap.rearrange("o w (t p) -> (o w t) p", p=128)[124 * (k - 3):124 * (k - 2), :]
                    t = small(dst[r:r + n, :], src, name)
                elif what in ("sb_q_norm_2", "sb_k_norm_2"):
                    small(dst[r:r + 1, 0:64], ap, name)
                    t = small(dst[r:r + 1, 64:128], ap, name)
                elif len(ap.shape) == 1:
                    t = small(dst[r:r + n, :], ap.rearrange("(t p) -> t p", p=128), name)
                else:
                    t = small(dst[r:r + n, :], ap.rearrange("o (t p) -> (o t) p", p=128), name)
                col.setdefault(what, base + r)
                r += n
            pt.append((dst, r, base))
            base += r
            return t

        small(CST[:, C_ID:C_ID + 128], I["consts"][:, C_ID:C_ID + 128], "first")
        t_c0 = load_rows(0, "first")
        XC = [ar(12000 + 1024 * i, 1024) for i in range(2)]
        prm = lambda name, i, n=1: PRM[:, col[name] + i:col[name] + i + n]

        def kcols(w, k0, nk, n0, nn):
            return w[128 * k0:128 * (k0 + nk), n0:n0 + nn].rearrange("(k p) n -> p k n", p=128), nk, nn

        items = []

        def plan(w, k0, nk, n0, nn):
            items.append(kcols(w, k0, nk, n0, nn))

        wm, wi = I["w_mod"][0], I["hg_w_in"][0]

        def plan_mod(c):
            plan(wm, 0, 4, 512 * c, 512)
            plan(wm, 4, 4, 512 * c, 512)

        def plan_b(w, n0, count):
            for j in range(count):
                plan(w, 0, 8, n0 + 256 * j, 256)

        for c in range(4):
            plan_mod(c)
        plan_b(wi, 0, 4)
        for c in range(2):
            plan(wi, 0, 4, 1024 + 512 * c, 512)
            plan(wi, 4, 4, 1024 + 512 * c, 512)
        def plan_z(u):
            plan_b(wi, 2048 + 1024 * (u % 2) + 256 * (u // 2), 1)

        plan_z(0)
        plan_z(1)
        for u in range(8):
            plan_mod(4 + u)
            if u < 6:
                plan_z(u + 2)
            else:
                plan_b(wi, 4096 + 256 * (u - 6), u - 5)
        plan_b(wi, 4864, 1)

        def plan_a(w, nk, n0=0):
            for j in range(nk // 2):
                plan(w, 2 * j, 2, n0, 1024)

        plan_a(I["hg_w_out"][0], 8)
        for e in range(17):
            if e < 16:
                plan(I["moe_w_gate"][0, e], 0, 8, 0, 256)
                plan(I["moe_w_up"][0, e], 0, 8, 0, 256)
            if e:
                plan(I["moe_w_down"][0, e - 1], 0, 2, 0, 1024)

        def plan_ffn(i):
            for j in range(17):
                if j < 16:
                    plan(I["ffn_w1_2"][i], 0, 8, 256 * j, 256)
                if j:
                    plan(I["ffn_w2_2"][i], 2 * (j - 1), 2, 0, 1024)

        def plan_ret(i):
            w = I["ret_w_in_2"][i]
            plan_b(w, 0, 8)
            plan_a(w, 8, 2048)
            plan_a(w, 8, 3072)
            for h in range(5):
                if h < 4:
                    plan_b(w, 4096 + 512 * h, 2)
                if h:
                    for j in range(2):
                        plan(I["ret_w_out_2"][i], 4 * (h - 1) + 2 * j, 2, 0, 1024)

        plan_ret(0)
        plan_ffn(0)
        for j in range(4):
            plan_b(I["conv_pw1_w_2"][0], 256 * j, 1)
            plan_b(I["conv_pw1_w_2"][0], 1024 + 256 * j, 1)
        plan_a(I["conv_pw2_w_2"][0], 8)
        plan_ffn(1)
        plan_b(I["sb_w_in_2"][0], 0, 8)
        plan_a(I["sb_w_in_2"][0], 8, 2048)
        plan_a(I["sb_w_out_2"][0], 8)
        plan_ffn(2)
        plan_ret(1)
        plan_ffn(3)

        loaded, low, used = {}, {}, {}
        state = {"next": 0}

        def load(i):
            if i >= len(items):
                return
            src, nk, nn = items[i]
            S.wait(low.get(i - NR))
            nc.sync.dma_start(raw[i % NR][:, :].rearrange("p (k n) -> p k n", k=nk), src).then_inc(s_ld[i % NR], 16)
            loaded[i] = (s_ld[i % NR], 16 * (i // NR + 1))

        def split(i):
            if i >= len(items):
                return
            A.wait(loaded[i], used.get(i - NS))
            t = A.mark(ac.copy(whi[i % NS][:, :], raw[i % NR][:, :]))
            E, e = (V, ve) if i <= 8 else (G, po)
            E.wait(t, loaded[i])
            low[i] = E.mark(e.tensor_tensor(wlo[i % NS][:, :], raw[i % NR][:, :], f32(whi[i % NS][:, :]), SUB))
            load(i + NR)

        for i in range(NR):
            load(i)
        for i in range(2):
            t_x = small(X[i], I["x"][0, 128 * i:128 * i + 128, :], "x")
        for i in range(2):
            t_x = small(XC[i], I["ctx"][0, 128 * i:128 * i + 128, :], "x")

        def take():
            i = state["next"]
            state["next"] += 1
            nk = items[i][1]
            if i < NRAW:
                P.wait(loaded[i])
                return i, [raw[i % NR][:, :].rearrange("p (k n) -> p k n", k=nk)]
            split(i + NS - 1)
            P.wait(low[i])
            return i, [w[i % NS][:, :].rearrange("p (k n) -> p k n", k=nk) for w in (whi, wlo)]

        def done(i, token):
            if i < NRAW:
                low[i] = token
                load(i + NR)
            else:
                used[i] = token

        class Banks:

            def __init__(self, which):
                self.q = [(b, ()) for b in which]

            def get(self):
                b, toks = self.q.pop(0)
                P.wait(*toks)
                return b

            def put(self, b, *toks):
                self.q.append((b, toks))

        R = Banks([4, 5, 6, 7])
        acc_free = [()] * 4
        bank_done = [None] * 4

        def mm3(ps, lh, ll, rh, rl, start, stop):
            pe.matmul(ps, lh, rh, start=start, stop=False)
            pe.matmul(ps, lh, rl, start=False, stop=False)
            return pe.matmul(ps, ll, rh, start=False, stop=stop)

        H8 = [h[:, 0:2048].rearrange("p (k n) -> p k n", k=8) for h in (HH, HL)]
        H16 = [h[:, :].rearrange("p (k n) -> p k n", k=8) for h in (HH, HL)]
        Y8 = [h[:, :].rearrange("p (k n) -> p k n", k=8) for h in (YH, YL)]

        def proj_b(acts=None, n=256, ready=None):
            a = acts or H8
            bs = [R.get() for _ in range(n // 256)]
            i, w = take()
            for k in range(8):
                if ready is not None and k % 2 == 0:
                    P.wait(ready[k // 2])
                for m in range(2):
                    ps = bank[bs[m]][:, 0:512] if n == 512 else bank[bs[0]][:, 256 * m:256 * m + 256]
                    c = slice(128 * m, 128 * m + 128)
                    first = k == 0 and (m == 0 or n == 512)
                    ah, al = a[0][:, k, 0:n], a[1][:, k, 0:n]
                    pe.matmul(ps, w[0][:, k, c], ah, start=first, stop=False, skip_group_check=True)
                    pe.matmul(ps, w[0][:, k, c], al, start=False, stop=False, skip_group_check=True)
                    last = pe.matmul(ps, w[1][:, k, c], ah, start=False, stop=k == 7, skip_group_check=True)
            t = P.mark(last)
            done(i, t)
            return bs, t

        def proj_a(acts, k0, first, last_, ready=()):
            i, w = take()
            P.wait(*ready)
            for h in range(2):
                for m in range(2):
                    q = 2 * m + h
                    if first:
                        P.wait(*acc_free[q])
                    for k in range(2):
                        c = slice(128 * m, 128 * m + 128)
                        r = slice(512 * h, 512 * h + 512)
                        x = mm3(bank[q][:, :], acts[0][:, k0 + k, c], acts[1][:, k0 + k, c], w[0][:, k, r],
                                w[1][:, k, r], first and k == 0, last_ and k == 1)
                    if last_:
                        bank_done[q] = P.mark(x)
            t = bank_done[q] if last_ else P.mark(x)
            done(i, t)
            return t

        eps = SM[:, 0:1]
        V(ve.memset(eps, EPS))
        RT = sb("RT", [128, 144])
        RW, RB, LT = RT[:, 0:128], RT[:, 128:144], SM[:, 176:192]

        def columns(k, t):
            src, n, off = pt[k]
            b = R.get()
            P.wait(t)
            V.wait(P.mark(pe.transpose(bank[b][:, 0:n], src[0:n, :], ident[0:n, 0:n])))
            R.put(b, V(ve.tensor_copy(PRM[:, off:off + n], bank[b][:, 0:n])))

        columns(0, t_c0)
        t_prm = V.now()

        XN = [ar(1024 * i, 1024) for i in range(2)]
        FT = ar(2048, 2048).rearrange("p (k n) -> p k n", k=8)
        ST = SM[:, 160:176]
        RBC = sb("RBC", [128, 256])
        pool_read = {"FT": None}
        x_done = [None] * 4

        def square_half(x, n):
            A.wait(A.now())
            A.mark(ac.activation(XN[0][:, 0:512], x, ACT.Square, accum_out=ST[:, n:n + 1]))

        def sum_squares(xs, t, at=0):
            A.wait(t)
            for q in range(4):
                square_half(xs[q // 2][:, 512 * (q % 2):512 * (q % 2) + 512], at + q)

        def rstd(at=0):
            V.wait(A.now())
            p = ST[:, at:at + 4].rearrange("p (i h) -> p i h", h=2)
            V(ve.tensor_tensor(ST[:, 10:12], p[:, :, 0], p[:, :, 1], ADD))
            A.wait(V.now())
            A(ac.activation(ST[:, 12:14], ST[:, 10:12], ACT.Sqrt, bias=eps, scale=1.0 / D))
            V.wait(A.now())
            return V(ve.reciprocal(ST[:, 8:10], ST[:, 12:14]))

        def rms_rows(at=0):
            P.wait(rstd(at), *acc_free[0])
            for i in range(2):
                x = pe.matmul(bank[0][:, 128 * i:128 * i + 128], ST[:, 8 + i:9 + i].to_broadcast([128, 128]), ident,
                              start=True, stop=True)
            V.wait(P.mark(x))
            t = V(ve.tensor_copy(RBC[:, :], bank[0][:, 0:256]))
            acc_free[0] = (t,)
            A.wait(t)

        def norm(xs, scale, shift, dst, at=0, late=False):
            bs = []
            for q in range(4):
                P.wait(x_done[q // 2], x_done[2 + q // 2])
                b = R.get()
                for m in range(2):
                    for i in range(2):
                        k = 2 * q + m
                        x = pe.transpose(bank[b][:, 256 * m + 128 * i:256 * m + 128 * i + 128],
                                         xs[i][:, 128 * k:128 * k + 128], ident)
                bs.append((b, P.mark(x)))
            if not late:
                rms_rows(at)
            V.wait(pool_read["FT"])
            ta, ready = [], []

            def low_part(q):
                kk = slice(2 * q, 2 * q + 2)
                E, e = (V, ve) if q % 2 == 0 else (G, po)
                E.wait(ta[q])
                ready.append(E.mark(e.tensor_tensor(dst[1][:, kk, :], FT[:, kk, :], f32(dst[0][:, kk, :]), SUB)))

            for q in range(4):
                b, t = bs[q]
                V.wait(t)
                for m in range(2):
                    k = 2 * q + m
                    src, sc = bank[b][:, 256 * m:256 * m + 256], scale[:, k:k + 1]
                    if late:
                        V.mark(ve.tensor_scalar(FT[:, k, :], src, sc, None, MUL))
                    else:
                        V.mark(ve.scalar_tensor_tensor(FT[:, k, :], src, sc, RBC[:, :], MUL, MUL))
                R.put(b, V.now())
                if shift is not None:
                    V.wait(V.now())
                    for m in range(2):
                        k = 2 * q + m
                        V.mark(ve.tensor_scalar(FT[:, k, :], FT[:, k, :], shift[:, k:k + 1], None, ADD))
                A.wait(V.now())
                ta.append(A.mark(ac.copy(dst[0][:, 2 * q:2 * q + 2, :], FT[:, 2 * q:2 * q + 2, :])))
                if q:
                    low_part(q - 1)
            low_part(3)
            pool_read["FT"] = ready[3]
            return ready

        A.wait(t_prm)
        cs = SM[:, 2:18].rearrange("p (v k) -> p k v", v=2)
        A(ac.activation(SM[:, 2:18], prm("c", 0, 16), ACT.Silu))
        CSv = CS[:, :].rearrange("p (k v) -> p k v", v=4)
        A(ac.copy(CSv[:, :, 0:2], cs))
        V.wait(A.now())
        t_cs = V(ve.tensor_tensor(CSv[:, :, 2:4], cs, f32(CSv[:, :, 0:2]), SUB))

        MODT = SM[:, 80:144].rearrange("p (v t) -> p v t", t=16)
        MR = sb("MR", [4, 512])
        G1B, G2B = sb("G1B", [128, D]), sb("G2B", [128, D])
        TM = SM[:, 208:224]
        bm = I["b_mod"]
        slot = {0: 0, 1: 1, 3: 2, 4: 3}
        mod_state = {}
        MRS = [MR[:, :], ar(6000, 512)[0:4, :]]

        def mod_rows(c, RB, between=None):
            b = RB.get()
            P.wait(t_cs)
            for half in range(2):
                i, w = take()
                for k in range(4):
                    for r in range(len(w)):
                        lhs = CSv[:, 4 * half + k, :]
                        x = pe.matmul(bank[b][0:4, :], lhs if len(w) == 2 else f32(lhs), w[r][:, k, :],
                                      start=half == 0 and k == 0 and r == 0,
                                      stop=half == 1 and k == 3 and r == len(w) - 1)
                t = P.mark(x)
                done(i, t)
                if half == 0 and between:
                    between()
            if c < 4:
                A.wait(t, mod_state.get(c - 2))
                t = A(ac.copy(MRS[c % 2], bank[b][0:4, :]))
            else:
                V.wait(t, mod_state.get(c - 1), mod_state.get(2))
                t = V(ve.tensor_copy(MR[:, :], bank[b][0:4, :]))
            RB.put(b, t)
            return t

        def mod_cols(c, t, RB):
            which, half = c // 2, c % 2
            mr = MRS[c % 2] if c < 4 else MR[:, :]
            b = RB.get()
            P.wait(t)
            if which in slot:
                for k in range(4):
                    x = pe.transpose(bank[b][:, 4 * k:4 * k + 4], mr[:, 128 * k:128 * k + 128], ident[0:4, 0:4])
                mod_state[c] = P.mark(x)
                V.wait(mod_state[c])
                RB.put(b, V(ve.tensor_copy(TM, bank[b][:, 0:16])))
                tm = TM.rearrange("p (k v) -> p k v", v=4)
                o = MODT[:, slot[which], 8 * half:8 * half + 8].rearrange("p (k v) -> p k v", v=2)
                V(ve.tensor_tensor(o, tm[:, :, 0:2], tm[:, :, 2:4], ADD))
                bb = prm("b_mod", 8 * which + 4 * half, 4).rearrange("p (k v) -> p k v", v=1).to_broadcast([128, 4, 2])
                V(ve.tensor_tensor(o, o, bb, ADD))
            else:
                x = pe.matmul(bank[b][:, :], CST[0:4, C_SEL:C_SEL + 128], mr, start=True, stop=True)
                mod_state[c] = P.mark(x)
                V.wait(mod_state[c], t_gb)
                g = (G1B if which == 2 else G2B)[:, 512 * half:512 * half + 512]
                RB.put(b, V(ve.tensor_tensor(g, g, bank[b][:, :], ADD)))

        tm_ = {}
        for c in range(5):
            if c < 4:
                tm_[c] = mod_rows(c, R)
            if c == 3:
                for j in range(NS - 1):
                    split(NRAW + j)
                t_cst = small(CST[:, 128:], I["consts"][:, 128:C_END], "consts")
                for k in range(1, 5):
                    t_in = load_rows(k, "rows")
            if c == 1:
                sum_squares(X, t_x)
            if c:
                mod_cols(c - 1, tm_[c - 1], R)
            if c == 2:
                sum_squares(XC, t_x, 4)
        t_gb = (small(G1B[:, :], bm[0:1, 2048:3072].to_broadcast([128, 1024]), "gate"),
                small(G2B[:, :], bm[0:1, 5120:6144].to_broadcast([128, 1024]), "gate"))[1]
        small(RW, I["router_w"].rearrange("(k p) e -> p k e", p=128), "router")
        small(RB, I["router_b"].rearrange("(o e) -> o e", o=1).to_broadcast([128, 16]), "router")
        t_r = small(LT, I["consts"][:, C_LT:C_LT + 16], "router")
        MS = SM[:, 224:256]
        for v in range(2):
            sc = MODT[:, 1, :].rearrange("p (t v) -> p v t", v=2)[:, v, :]
            V(ve.scalar_tensor_tensor(MS[:, 8 * v:8 * v + 8], sc, 1.0, prm("norm1_g", 0, 8), ADD, MUL))
        sh1 = MODT[:, 0, :].rearrange("p (t v) -> p v t", v=2)

        rbc2 = RBC[:, :].rearrange("p (m n) -> p m n", m=1).to_broadcast([128, 2, 256])
        two = lambda ap: ap.rearrange("p (m n) -> p m n", m=2)

        def hi_lo(hi, lo, src):
            A.wait(V.now())
            V.wait(A.mark(ac.copy(hi, src)))
            return V(ve.tensor_tensor(lo, src, f32(hi), SUB))

        x_done[:] = [t_x] * 4
        ready = norm(X, MS[:, 0:8], sh1[:, 0, :], [h[:, :, 0:256] for h in H16])
        V.wait(t_cst)
        P.wait(t_cst)
        LB, LB1 = SM[:, 18:34], SM[:, 34:50]
        for d, name in enumerate(("hg_lb_fwd", "hg_lb_bwd")):
            a0, a1 = prm(name, 0, 8), prm(name, 8, 8)
            mx, e0, e1 = SM[:, 50:58], SM[:, 58:66], SM[:, 66:74]
            V(ve.tensor_tensor(mx, a0, a1, ALU.max))
            V(ve.tensor_tensor(e0, a0, mx, SUB))
            V(ve.tensor_tensor(e1, a1, mx, SUB))
            A.wait(V.now())
            A(ac.activation(SM[:, 58:74], SM[:, 58:74], ACT.Exp))
            V.wait(A.now())
            V(ve.tensor_tensor(mx, e0, e1, ADD))
            V(ve.reciprocal(mx, mx))
            V(ve.tensor_tensor(LB[:, 8 * d:8 * d + 8], e0, mx, MUL))
            V(ve.tensor_tensor(LB1[:, 8 * d:8 * d + 8], e1, mx, MUL))

        QO = ar(0, 2048).rearrange("p (t n) -> p t n", t=8)
        VT = ar(2048, 4096).rearrange("p (i n) -> p i n", i=4)
        o0 = 6144
        kk_ = ar(o0, 1024).rearrange("p (h n) -> p h n", h=2)
        cum = ar(o0 + 1024, 1024).rearrange("p (h n) -> p h n", h=2)
        tmp = ar(o0 + 2048, 1024).rearrange("p (h n) -> p h n", h=2)
        KDT = ar(o0 + 3072, 1024).rearrange("p (h i n) -> p h i n", h=2, i=4)
        QE = ar(o0 + 4096, 512).rearrange("p (h n) -> p h n", h=2)
        KE = ar(o0 + 4608, 512).rearrange("p (h n) -> p h n", h=2)
        QI_ = [x.rearrange("p (h n) -> p h n", h=2) for x in (ar(o0 + 5120, 512), ar(o0 + 8192, 512))]
        SA = ar(o0 + 5632, 1024).rearrange("p (h i n) -> p h i n", h=2, i=4)
        SC = [ar(o0 + 6656 + 512 * i, 512) for i in range(2)]
        kd2 = ar(o0 + 7680, 512).rearrange("p (h n) -> p h n", h=2)
        SG = ar(o0 + 4096, 2048).rearrange("p (t n) -> p t n", t=8)
        DEC = SM[:, 144:160]

        for j in range(4):
            (b,), t = proj_b(H16, 256, ready if j == 0 else None)
            A.wait(t)
            t = A(ac.activation(QO[:, 2 * j:2 * j + 2, :], bank[b][:, :], ACT.Silu))
            R.put(b, t)
            if j == 0:
                readyc = norm(XC, MS[:, 8:16], sh1[:, 1, :], [h[:, :, 256:512] for h in H16], 4)
                for d in range(2):
                    V(ve.memset(SC[d], 0.0))
        A.wait(*readyc)
        V.wait(*readyc)
        P.wait(*readyc)
        for c in range(2):
            for half in range(2):
                i, w = take()
                for m in range(4):
                    if half == 0:
                        P.wait(*acc_free[m])
                    for k in range(4):
                        q = 4 * half + k
                        cc = slice(128 * m, 128 * m + 128)
                        x = mm3(bank[m][:, :], H16[0][:, q, cc], H16[1][:, q, cc], w[0][:, k, :], w[1][:, k, :],
                                q == 0, q == 7)
                t = P.mark(x)
                done(i, t)
            A.wait(t)
            V.wait(t)
            for m in range(4):
                dst = VT[:, m, 512 * c:512 * c + 512]
                if m % 2:
                    acc_free[m] = (A(ac.copy(dst, bank[m][:, :])),)
                else:
                    acc_free[m] = (V(ve.tensor_copy(dst, bank[m][:, :])),)
        t_v = (A.now(), V.now())

        for k in range(1, 5):
            columns(k, t_in)
        zq, vec_read = {}, {"kk": V.now(), "vec": V.now()}

        def unit_proj(u):
            zq[u] = proj_b(H16, 512)

        def unit_gate(u):
            p, d = u // 2, u % 2
            bs, t = zq[u]
            A.wait(t, vec_read["kk"], vec_read["vec"])
            for h in range(2):
                A.mark(ac.activation(kk_[:, h, :], bank[bs[h]][:, :], ACT.Sigmoid, scale=-1.0))
                A.mark(ac.activation(tmp[:, h, :], bank[bs[h]][:, :], ACT.Sigmoid))
                R.put(bs[h], A.now())
            A.wait(A.now())
            tl_ = []
            for h in range(2):
                q = 8 * d + 2 * p + h
                tl_.append(A.mark(ac.activation(tmp[:, h, :], tmp[:, h, :], ACT.Ln, scale=LB1[:, q:q + 1],
                                                bias=LB[:, q:q + 1])))
            return tl_

        def unit_vec(u, tl_):
            p, d = u // 2, u % 2
            QI = QI_[d]
            V.wait(vec_read["kk"])
            for h in range(2):
                V.wait(tl_[h])
                if d == 0:
                    V.mark(ve.tensor_tensor_scan(cum[:, h, :], CST[:, C_RF:C_RF + 512], tmp[:, h, :], 0.0, MUL, ADD))
                else:
                    V.mark(ve.tensor_tensor_scan(cum[:, h, ::-1], CST[:, C_RB + 511:C_RB - 1:-1], tmp[:, h, ::-1],
                                                 0.0, MUL, ADD))
            V.wait(V.now())
            cl = cum[:, :, 0:256].rearrange("p h (c n) -> p h c n", c=4)
            tl = tmp[:, :, 0:256].rearrange("p h (c n) -> p h c n", c=4)
            kl = kd2.rearrange("p h (c n) -> p h c n", c=4)
            bc = lambda i: cl[:, :, :, i:i + 1].to_broadcast([128, 2, 4, 64])
            ref, last = (31, 63) if d == 0 else (32, 0)
            lc = 511 if d == 0 else 256
            A.wait(V.now())
            A.mark(ac.activation(DEC[:, 8 * d:8 * d + 8].rearrange("p (h c) -> p h c", h=2), cl[:, :, :, last], ACT.Exp))
            t_qi = A.mark(ac.activation(QI, cum[:, :, 0:256], ACT.Exp))
            t1 = V.mark(ve.tensor_tensor(tl, cl, bc(ref), SUB))
            t2 = V.mark(ve.tensor_tensor(kl, cl, bc(last), SUB))
            t3 = V.mark(ve.tensor_tensor(tmp[:, :, 256:512], cum[:, :, 256:512],
                                         cum[:, :, lc:lc + 1].to_broadcast([128, 2, 256]), SUB))
            A.wait(t1)
            t_qe = A.mark(ac.activation(QE, tmp[:, :, 0:256], ACT.Exp))
            t_ke = A.mark(ac.activation(KE, tmp[:, :, 0:256], ACT.Exp, scale=-1.0))
            A.wait(t2)
            A.mark(ac.activation(kd2, kd2, ACT.Exp, scale=-1.0))
            A.wait(t3)
            t_kd = A.mark(ac.activation(tmp[:, :, 256:512], tmp[:, :, 256:512], ACT.Exp, scale=-1.0))
            V.wait(t_qi)
            V.mark(ve.tensor_tensor(QI, QI, QO[:, 2 * p:2 * p + 2, :], MUL))
            V.wait(t_qe)
            V.mark(ve.tensor_tensor(QE, QE, QO[:, 2 * p:2 * p + 2, :], MUL))
            V.wait(t_ke)
            lb1 = [LB1[:, 8 * d + 2 * p + h:8 * d + 2 * p + h + 1] for h in range(2)]
            for h in range(2):
                V.mark(ve.scalar_tensor_tensor(KE[:, h, :], KE[:, h, :], lb1[h], kk_[:, h, 0:256], MUL, MUL))
            t_qe = V.now()
            V.wait(t_kd)
            for h in range(2):
                V.mark(ve.scalar_tensor_tensor(kd2[:, h, :], kd2[:, h, :], lb1[h], kk_[:, h, 0:256], MUL, MUL))
                V.mark(ve.scalar_tensor_tensor(tmp[:, h, 256:512], tmp[:, h, 256:512], lb1[h], kk_[:, h, 256:512],
                                               MUL, MUL))
            vec_read["vec"] = V.now()
            return t_qe, V.now()

        def unit_scores(u, t_qe, t_kd):
            d = u % 2
            P.wait(t_qe)
            b = R2.get()
            for h in range(2):
                for j in range(2):
                    s = slice(128 * j, 128 * j + 128)
                    q = 2 * h + j
                    x = pe.matmul(bank[b][:, 128 * q:128 * q + 128], KE[:, h, s], QE[:, h, s],
                                  start=True, stop=True)
            t = P.mark(x)
            P.wait(t_kd)
            bs = []
            for h in range(2):
                bb = R2.get()
                for i in range(4):
                    src = (kd2[:, h, 0:128], kd2[:, h, 128:256], tmp[:, h, 256:384], tmp[:, h, 384:512])[i]
                    x = pe.transpose(bank[bb][:, 128 * i:128 * i + 128], src, ident)
                bs.append((bb, P.mark(x)))
            V.wait(t)
            m = CST[:, (C_MF, C_MB)[d]:(C_MF, C_MB)[d] + 128].bitcast(I32)
            mb = m.rearrange("p (q n) -> p q n", q=1).to_broadcast([128, 4, 128])
            t = V(ve.copy_predicated(SC[d].rearrange("p (q n) -> p q n", q=4), mb,
                                     bank[b][:, :].rearrange("p (q n) -> p q n", q=4)))
            R2.put(b, t)
            A.wait(bs[0][1])
            R2.put(bs[0][0], A(ac.copy(KDT[:, 0, :, :], bank[bs[0][0]][:, :])))
            V.wait(bs[1][1])
            R2.put(bs[1][0], V(ve.tensor_copy(KDT[:, 1, :, :], bank[bs[1][0]][:, :])))
            vec_read["kdt"] = (A.now(), V.now())
            vec_read["kk"] = P.now()
            return t

        def unit_state(u):
            p, d = u // 2, u % 2
            P.wait(*vec_read["kdt"])
            order = [0, 1, 2] if d == 0 else [3, 2, 1]
            bs = [R2.get() for _ in range(2)]
            at = {}
            for h in range(2):
                hc = slice(128 * (2 * p + h), 128 * (2 * p + h) + 128)
                for i in range(2):
                    x = pe.matmul(bank[bs[h]][:, 0:128], KDT[:, h, 2 + i, :], VT[:, 2 + i, hc], start=i == 0, stop=i == 1)
            for odd in range(2):
                if odd:
                    bs.append(R2.get())
                for h in range(2):
                    hc = slice(128 * (2 * p + h), 128 * (2 * p + h) + 128)
                    for n, c in enumerate(order):
                        if c % 2 != odd:
                            continue
                        r = slice(64 * odd, 64 * odd + 64)
                        b, o = (bs[2], 256 * h + 128 * (n // 2)) if odd else (bs[h], 128 * (n + 1))
                        at[h, n] = bank[b][:, o:o + 128]
                        x = pe.matmul(at[h, n], KDT[r, h, c // 2, :], VT[r, c // 2, hc], start=True, stop=True)
            V.wait(P.mark(x), vec_read.get("out"))
            for h in range(2):
                V.mark(ve.tensor_copy(SA[:, h, 0, :], bank[bs[h]][:, 0:128]))
            for n, c in enumerate(order):
                for h in range(2):
                    V.wait((V.sem, V.n - 1))
                    V.mark(ve.scalar_tensor_tensor(SA[:, h, n + 1, :], SA[:, h, n, :],
                                                   DEC[:, 8 * d + 4 * h + c:8 * d + 4 * h + c + 1], at[h, n], MUL, ADD))
            vec_read["state"] = V.now()
            for b in bs:
                R2.put(b, V.now())

        def unit_out(u):
            p, d = u // 2, u % 2
            P.wait(vec_read["state"])
            if d == 0:
                P.wait(*acc_free[0])
            first = d == 0
            order = [0, 1, 2, 3] if d == 0 else [3, 2, 1, 0]
            for h in range(2):
                hc = slice(128 * (2 * p + h), 128 * (2 * p + h) + 128)
                for j in range(2):
                    q = 2 * h + j
                    pe.matmul(bank[0][:, 128 * q:128 * q + 128], VT[:, j, hc], SC[d][:, 128 * q:128 * q + 128],
                              start=first, stop=False, skip_group_check=True)
                    first = False
                for n, c in enumerate(order):
                    x = pe.matmul(bank[0][:, 256 * h + 64 * c:256 * h + 64 * c + 64], SA[:, h, n, :],
                                  QI_[d][:, h, 64 * c:64 * c + 64], start=False,
                                  stop=d == 1 and h == 1 and n == 3, skip_group_check=True)
            t = P.mark(x)
            vec_read["out"] = t
            if d == 1:
                V.wait(t)
                acc_free[0] = (V(ve.tensor_copy(QO[:, 2 * p:2 * p + 2, :], bank[0][:, :])),)

        acc_free[0] = acc_free[0] + t_v
        R2 = Banks([])
        for q in (1, 2, 3):
            R2.put(q, *acc_free[q])
        unit_proj(0)
        tk = unit_vec(0, unit_gate(0))
        unit_proj(1)
        gs = []
        for u in range(8):
            unit_scores(u, *tk)
            tg = []
            t = mod_rows(4 + u, R2, lambda: u < 7 and tg.extend(unit_gate(u + 1)))
            unit_state(u)
            if u < 6:
                unit_proj(u + 2)
            else:
                gs += [proj_b(H16) for _ in range(u - 5)]
            if u < 7:
                tk = unit_vec(u + 1, tg)
            mod_cols(4 + u, t, R2)
            unit_out(u)
        for q, toks in R2.q:
            acc_free[q] = toks

        SQ = ar(o0, 2048).rearrange("p (t n) -> p t n", t=8)
        RS = ar(o0 + 2048, 2048).rearrange("p (t n) -> p t n", t=8)
        A.wait(V.now(), P.now())
        t_sq = []
        for j in range(4):
            s = slice(2 * j, 2 * j + 2)
            t_sq.append(A.mark(ac.activation(SQ[:, s, :], QO[:, s, :], ACT.Square)))
        t_ms = []
        for j in range(4):
            P.wait(t_sq[j], *acc_free[j])
            t_ms.append(P.mark(pe.matmul(bank[j][:, :], ones, SQ[:, 2 * j:2 * j + 2, :], start=True, stop=True)))
        gs.append(proj_b(H16))
        def silu_gate(j):
            (bg,), tg = gs[j]
            A.wait(tg)
            t = A.mark(ac.activation(SG[:, 2 * j:2 * j + 2, :], bank[bg][:, :], ACT.Silu))
            R.put(bg, t)
            return t

        t_sg = [silu_gate(j) for j in range(3)]
        t_rs = []
        for j in range(4):
            A.wait(t_ms[j])
            t_rs.append(A.mark(ac.activation(RS[:, 2 * j:2 * j + 2, :], bank[j][:, :], ACT.Sqrt, bias=eps,
                                             scale=1.0 / 128)))
            acc_free[j] = (t_rs[j],)
        for j in range(4):
            s = slice(2 * j, 2 * j + 2)
            if j == 3:
                t_sg.append(silu_gate(3))
            V.wait(t_rs[j])
            V(ve.reciprocal(RS[:, s, :], RS[:, s, :]))
            V(ve.scalar_tensor_tensor(QO[:, s, :], QO[:, s, :], prm("hg_gnorm", 0), RS[:, s, :], MUL, MUL))
            V.wait(t_sg[j])
            V(ve.tensor_tensor(QO[:, s, :], QO[:, s, :], SG[:, s, :], MUL))
            t_y = hi_lo(Y8[0][:, s, :], Y8[1][:, s, :], QO[:, s, :])
            proj_a(Y8, 2 * j, j == 0, j == 3, (t_y,))

        TMPA = [XN[1][:, 512 * i:512 * i + 512] for i in range(2)]

        def add_out(t, gate=None, bias=None):
            for q in (0, 2, 1, 3):
                V.wait(bank_done[q])
                m, h = q // 2, q % 2
                x = X[m][:, 512 * h:512 * h + 512]
                g = slice(512 * h, 512 * h + 512)
                if gate is not None:
                    acc_free[q] = (V(ve.tensor_tensor(TMPA[q // 2], bank[q][:, :], gate[:, g], MUL)),)
                    t = V.mark(ve.tensor_tensor(x, x, TMPA[q // 2], ADD))
                else:
                    t = V.mark(ve.tensor_tensor(x, x, bank[q][:, :], ADD))
                    acc_free[q] = (t,)
                    if bias is not None:
                        V.wait(t)
                        t = V.mark(ve.tensor_tensor(x, x, bias[:, g], ADD))
                A.wait(t)
                x_done[q] = t
                square_half(x, q)
            V.wait(V.now())

        add_out(t, gate=G1B[:, :])

        V(ve.scalar_tensor_tensor(MS[:, 16:24], MODT[:, 3, :].rearrange("p (t v) -> p v t", v=2)[:, 0, :], 1.0,
                                  prm("norm2_g", 0, 8), ADD, MUL))
        sh2 = MODT[:, 2, :].rearrange("p (t v) -> p v t", v=2)[:, 0, :]
        ready = norm(X, MS[:, 16:24], sh2, H8)

        o0 = 4096
        FG = ar(o0 + 7424, 1024)
        t_g = small(FG, I["final_g"].rearrange("(o n) -> o n", o=1).to_broadcast([128, 1024]), "first")
        CB = ar(o0 + 256, 4096).rearrange("p (e n) -> p e n", e=16)
        o0 = o0 + 256 + 4096
        z = lambda k, n=16: ar(o0 + 64 * k, n)
        rw = RW.rearrange("p (k e) -> p k e", k=8)
        early = [proj_b(ready=ready)]
        P.wait(t_r, *ready, *acc_free[1])
        V.wait(ready[3])
        for i in range(2):
            for k in range(8):
                x = pe.matmul(bank[1][:, 16 * i:16 * i + 16], FT[:, k, 128 * i:128 * i + 128], rw[:, k, :],
                              start=k == 0, stop=k == 7)
        t = P.mark(x)
        A.wait(t, V.now())
        sg = z(0, 32)
        t = A(ac.activation(sg, bank[1][:, 0:32], ACT.Sigmoid))
        acc_free[1] = (t,)
        V.wait(t, t_r)
        cmb = z(1, 32)

        def rank(dst, v, n, tie, c1, c2):
            g = v.shape[1]
            vi = v.rearrange("p g (i j) -> p g i j", j=1).to_broadcast([128, g, n, n])
            vj = v.rearrange("p g (i j) -> p g i j", i=1).to_broadcast([128, g, n, n])
            tt = tie.rearrange("p (g i j) -> p g i j", g=1, i=n).to_broadcast([128, g, n, n])
            V(ve.tensor_tensor(c1, vj, vi, ALU.is_gt))
            V(ve.tensor_tensor(c2, vj, vi, ALU.is_equal))
            V(ve.tensor_tensor(c2, c2, tt, MUL))
            V(ve.tensor_tensor(c1, c1, c2, ADD))
            V(ve.tensor_reduce(dst, c1, AX, ADD))

        for i in range(2):
            s = sg[:, 16 * i:16 * i + 16]
            sel = z(2).rearrange("p (g e) -> p g e", g=4)
            c1 = z(3, 64).rearrange("p (g i j) -> p g i j", g=4, i=4)
            c2 = z(4, 64).rearrange("p (g i j) -> p g i j", g=4, i=4)
            rk = z(5).rearrange("p (g e) -> p g e", g=4)
            V(ve.tensor_tensor(z(2), s, RB, ADD))
            rank(rk, sel, 4, LT, c1, c2)
            V(ve.tensor_scalar(rk, rk, 1.5, None, ALU.is_lt))
            V(ve.tensor_tensor(sel, sel, rk, MUL))
            gs = z(6, 4)
            V(ve.tensor_reduce(gs, sel, AX, ADD))
            gr = z(7, 4)
            rank(gr.rearrange("p (g e) -> p g e", g=1), gs.rearrange("p (g e) -> p g e", g=1), 4, LT,
                 c1[:, 0:1], c2[:, 0:1])
            V(ve.tensor_scalar(gr, gr, 0.5, None, ALU.is_lt))
            V(ve.tensor_tensor(rk, rk, gr.rearrange("p (g e) -> p g e", e=1).to_broadcast([128, 4, 4]), MUL))
            V(ve.tensor_tensor(z(5), z(5), s, MUL))
            V(ve.tensor_reduce(z(8, 1), z(5), AX, ADD))
            V(ve.reciprocal(z(8, 1), z(8, 1)))
            V(ve.tensor_scalar(cmb[:, 16 * i:16 * i + 16], z(5), z(8, 1), None, MUL))
        t_cmb = V.now()
        early += [proj_b(), proj_b()]
        P.wait(t_cmb)
        for q in range(8):
            b = q % 4
            P.wait(*acc_free[b])
            for m in range(2):
                for i in range(2):
                    e = 2 * q + m
                    w = cmb[:, 16 * i + e:16 * i + e + 1].to_broadcast([128, 128])
                    x = pe.matmul(bank[b][:, 256 * m + 128 * i:256 * m + 128 * i + 128], w, ident, start=True, stop=True)
            A.wait(P.mark(x))
            acc_free[b] = (A.mark(ac.copy(CB[:, 2 * q:2 * q + 2, :], bank[b][:, :])),)
        t_cb = A.now()
        early.append(proj_b())
        V.wait(t_cb)

        o0 = o0 + 1024
        TG = [ar(o0 + 1024 * i, 512).rearrange("p (m n) -> p m n", m=2) for i in range(2)]
        TU = [ar(o0 + 1024 * i + 512, 512).rearrange("p (m n) -> p m n", m=2) for i in range(2)]
        ring_y = {}

        def yslot(n):
            s = 2 * (n % 4)
            return Y8[0][:, s:s + 2, :], Y8[1][:, s:s + 2, :]

        for e in range(17):
            if e < 16:
                (b,), tg = early.pop(0) if early else proj_b()
                A.wait(tg, ring_y.get(("v", e - 2)))
                tg = A.mark(ac.activation(TG[e % 2], bank[b][:, :], ACT.Silu))
                R.put(b, tg)
                (b,), tu = early.pop(0) if early else proj_b()
                V.wait(tg, tu)
                R.put(b, V(ve.tensor_tensor(TU[e % 2], TG[e % 2], bank[b][:, :], MUL)))
                cb = CB[:, e:e + 1, :].to_broadcast([128, 2, 256])
                V(ve.tensor_tensor(TU[e % 2], TU[e % 2], cb, MUL))
                A.wait(ring_y.get(("p", e - 4)))
                V.wait(ring_y.get(("p", e - 4)))
                hi, lo = yslot(e)
                ring_y["v", e] = hi_lo(hi, lo, TU[e % 2])
            if e:
                t = proj_a(Y8, 2 * ((e - 1) % 4), e == 1, e == 16, (ring_y["v", e - 1],))
                ring_y["p", e - 1] = t
        V.wait(t_g)
        add_out(t, gate=G2B[:, :])
        rstd()
        for h in range(2):
            for i in range(2):
                x = X[i][:, 512 * h:512 * h + 512]
                t = V.mark(ve.scalar_tensor_tensor(x, x, ST[:, 8 + i:9 + i], FG[:, 512 * h:512 * h + 512], MUL, MUL))
                A.wait(t)
                x_done[2 * i + h] = t
                square_half(x, 2 * i + h)
        V.wait(V.now())

        def ffn(i):
            ready = norm(X, prm("norm_ffn_2", 8 * i, 8), None, H8, late=True)
            ry = {}
            for j in range(17):
                if j < 16:
                    (b,), t = proj_b(ready=ready if j == 0 else None)
                    if j == 0:
                        rms_rows()
                    tr, th = TG[j % 2], TU[j % 2]
                    V.wait(t)
                    t = V(ve.scalar_tensor_tensor(tr, two(bank[b][:, :]), 0.0, rbc2, ALU.max, MUL))
                    R.put(b, t)
                    hi, lo = yslot(j)
                    A.wait(t, ry.get(("p", j - 4)))
                    th_ = A.mark(ac.activation(hi, tr, ACT.Square))
                    V(ve.tensor_tensor(th, tr, tr, MUL))
                    V.wait(th_, ry.get(("p", j - 4)))
                    ry["v", j] = V(ve.tensor_tensor(lo, th, f32(hi), SUB))
                if j:
                    t = proj_a(Y8, 2 * ((j - 1) % 4), j == 1, j == 16, (ry["v", j - 1],))
                    ry["p", j - 1] = t
            add_out(t)

        def head_norm(src_ps, dst, t, sq):
            V.wait(t)
            tv = V(ve.tensor_tensor(dst, two(src_ps), rbc2, MUL))
            A.wait(tv)
            return A.mark(ac.activation(sq, dst, ACT.Square)), tv

        def evacuate(dst, q):
            rs = ST[:, 8 + q // 2:9 + q // 2]
            if q % 2:
                acc_free[q] = (A(ac.activation(dst, bank[q][:, :], ACT.Identity, scale=rs)),)
            else:
                acc_free[q] = (V(ve.tensor_scalar(dst, bank[q][:, :], rs, None, MUL)),)

        def ret(i, li):
            o = 4096
            S.wait(V.now(), A.now(), P.now())
            t_c = small(ar(o + 4096, 2048), I["consts"][:, C_RET:C_RET + 2048], f"ret{i}")
            ready = norm(X, prm("norm_mix_2", 8 * li, 8), None, H8, late=True)
            QK = [ar(2048 * s, 2048).rearrange("p (h m n) -> p h m n", h=4, m=2) for s in range(2)]
            VV = ar(o, 4096).rearrange("p (i n) -> p i n", i=2)
            RM = ar(o + 4096, 1536).rearrange("p (h n) -> p h n", h=4)
            COS, SIN = ar(o + 5632, 256), ar(o + 5888, 256)
            SQ2 = [ar(o + 6144, 512), ar(o + 8448, 512)]
            RSD = ar(o + 6656, 256)
            M1, M2 = ar(o + 6912, 512), ar(o + 7424, 512)
            QG = [ar(b_, 512).rearrange("p (m n) -> p m n", m=2) for b_ in (o + 7936, o + 8960)]
            o2 = o + 8448
            PP = SQ2[0][:, 0:384]
            SGT = ar(o2, 1024).rearrange("p (t n) -> p t n", t=4)
            YN = [ar(o2 + 1024 + 512 * s, 512) for s in range(2)]
            YT = ar(o + 6912, 1024).rearrange("p (t n) -> p t n", t=4)
            V.wait(t_c, P.now(), A.now(), *ready)
            A.wait(P.now(), V.now(), *ready)
            cosb = COS.rearrange("p (m n) -> p m n", m=1).to_broadcast([128, 2, 256])
            sinb = SIN.rearrange("p (m n) -> p m n", m=1).to_broadcast([128, 2, 256])
            m1, m2 = (x.rearrange("p (m n) -> p m n", m=2) for x in (M1, M2))
            pend = None

            def rotate(h8, sq_t, gain):
                s, h, i2 = h8 // 4, h8 % 4, h8 % 2
                b = R.get()
                P.wait(sq_t)
                for m in range(2):
                    x = pe.matmul(bank[b][:, 0:256], ones, SQ2[i2][:, 256 * m:256 * m + 256], start=m == 0, stop=m == 1)
                t = P.mark(x)
                A.wait(t, V.now())
                t = A.mark(ac.activation(RSD, bank[b][:, 0:256], ACT.Sqrt, bias=eps, scale=1.0 / 256))
                R.put(b, t)
                V.wait(t)
                V(ve.reciprocal(RSD, RSD))
                g = QG[i2]
                for m in range(2):
                    V.mark(ve.scalar_tensor_tensor(g[:, m, :], g[:, m, :], gain[m], RSD, MUL, MUL))
                V.wait(V.now())
                V.mark(ve.tensor_tensor(m1, g, cosb, MUL))
                V(ve.tensor_tensor(m2, g, sinb, MUL))
                dst = QK[s][:, h, :, :]
                V.mark(ve.tensor_tensor(dst[:, 0, :], m1[:, 0, :], m2[:, 1, :], SUB))
                V(ve.tensor_tensor(dst[:, 1, :], m2[:, 0, :], m1[:, 1, :], ADD))
                return t

            read = {}
            for h8 in range(8):
                bs, t = proj_b(ready=ready if h8 == 0 else None)
                if h8 == 0:
                    rms_rows()
                g = [prm(("ret_q_norm_2", "ret_k_norm_2")[h8 // 4], 2 * i + m) for m in range(2)]
                A.wait(read.get(h8 - 2))
                ta, tv = head_norm(bank[bs[0]][:, :], QG[h8 % 2], t, SQ2[h8 % 2])
                R.put(bs[0], tv)
                if pend is not None:
                    read[pend[0]] = rotate(*pend)
                pend = (h8, ta, g)
            for c in range(2):
                for j in range(4):
                    t = proj_a(H8, 2 * j, j == 0, j == 3)
                    if c == 0 and j == 0:
                        rotate(*pend)
                        t_qk = V.now()
                for q in (0, 2, 1, 3):
                    m, h = q // 2, q % 2
                    (A if q % 2 else V).wait(bank_done[q])
                    evacuate(VV[:, m, 1024 * c + 512 * h:1024 * c + 512 * h + 512], q)
            t_vv = (A.now(), V.now())
            t_yl, t_yt = [None, None], None

            def gate_out(j, b, t):
                sg = SGT[:, 2 * j:2 * j + 2, :]
                V.wait(t)
                t = V.mark(ve.tensor_tensor(sg, two(bank[b][:, :]), rbc2, MUL))
                R.put(b, t)
                A.wait(t)
                A.mark(ac.activation(sg, sg, ACT.Silu))

            for h in range(5):
                if h < 4:
                    b = R.get()
                    P.wait(*t_vv, t_qk)
                    q, k = QK[0][:, h, :, :], QK[1][:, h, :, :]
                    for m in range(2):
                        pe.matmul(bank[b][:, 0:256], k[:, m, 0:128], q[:, m, :], start=m == 0, stop=m == 1)
                    for m in range(2):
                        x = pe.matmul(bank[b][:, 256:384], k[:, m, 128:256], q[:, m, 128:256], start=m == 0, stop=m == 1)
                    t = P.mark(x)
                    V.wait(t)
                    t_p = V(ve.tensor_tensor(PP, bank[b][:, 0:384], RM[:, h, :], MUL))
                    R.put(b, t_p)
                    (bg,), tg = proj_b()
                    gate_out(0, bg, tg)
                    vc = slice(512 * h, 512 * h + 512)
                    P.wait(t_p)
                    by = [R.get(), R.get()]
                    x = pe.matmul(bank[by[0]][:, :], PP[:, 0:128], VV[:, 0, vc], start=True, stop=True)
                    ty0 = P.mark(x)
                    pe.matmul(bank[by[1]][:, :], PP[:, 128:256], VV[:, 0, vc], start=True, stop=False)
                    x = pe.matmul(bank[by[1]][:, :], PP[:, 256:384], VV[:, 1, vc], start=False, stop=True)
                    ty1 = P.mark(x)
                    (bg,), tg = proj_b()
                    for m in range(2):
                        V.wait((ty0, ty1)[m])
                        V(ve.bn_stats(SM[:, 208:214], bank[by[m]][:, :]))
                        V(ve.bn_aggr(SM[:, 214 + 2 * m:216 + 2 * m], SM[:, 208:214]))
                    A.wait(V.now())
                    for m in range(2):
                        A(ac.activation(SM[:, 218 + m:219 + m], SM[:, 215 + 2 * m:216 + 2 * m], ACT.Sqrt, bias=eps))
                    V.wait(A.now())
                    V(ve.reciprocal(SM[:, 218:220], SM[:, 218:220]))
                    for m in range(2):
                        t = V(ve.tensor_scalar(YN[m], bank[by[m]][:, :], SM[:, 214 + 2 * m:215 + 2 * m],
                                               SM[:, 218 + m:219 + m], SUB, MUL))
                        R.put(by[m], t)
                    gate_out(1, bg, tg)
                made = list(t_yl)
                if h:
                    t_o = proj_a(Y8, 4 * ((h - 1) % 2), h == 1, False, (made[0],))
                if h < 4:
                    P.wait(t)
                    A.wait(P.now())
                    V.wait(P.now())
                    for jj in range(2):
                        b = R.get()
                        for m in range(2):
                            for s in range(2):
                                f = 2 * jj + m
                                x = pe.transpose(bank[b][:, 256 * m + 128 * s:256 * m + 128 * s + 128],
                                                 YN[s][:, 128 * f:128 * f + 128], ident)
                        A.wait(P.mark(x), V.now())
                        for m in range(2):
                            f = 4 * h + 2 * jj + m
                            A.mark(ac.activation(YT[:, 2 * jj + m, :], bank[b][:, 256 * m:256 * m + 256], ACT.Identity,
                                                 scale=prm("ret_gn_w_2", 16 * i + f), bias=prm("ret_gn_b_2", 16 * i + f)))
                        R.put(b, A.now())
                        V.wait(A.now())
                        s = slice(2 * jj, 2 * jj + 2)
                        t_yt = V(ve.tensor_tensor(YT[:, s, :], YT[:, s, :], SGT[:, s, :], MUL))
                        y = slice(4 * (h % 2) + 2 * jj, 4 * (h % 2) + 2 * jj + 2)
                        t_yl[jj] = hi_lo(Y8[0][:, y, :], Y8[1][:, y, :], YT[:, s, :])
                if h:
                    t_o = proj_a(Y8, 4 * ((h - 1) % 2) + 2, False, h == 4, (made[1],))
            add_out(t_o)

        ret(0, 0)
        ffn(0)

        o = 4096
        HP = ar(o, 2288).rearrange("p (t n) -> p t n", t=8)
        CA = ar(o + 2288, 2048).rearrange("p (t n) -> p t n", t=8)
        CG = ar(o + 4336, 512).rearrange("p (m n) -> p m n", m=2)
        CQ = ar(o + 4848, 2048).rearrange("p (t n) -> p t n", t=8)
        BO = ar(o + 6896, 1024)
        LR = ar(o + 7920, 256)
        LRR = ar(o + 8176, 256)
        NDG = 16
        DG = ar(0, 128 * NDG).rearrange("p (w n) -> p w n", w=NDG)
        S.wait(V.now(), A.now(), P.now())
        t_bo = small(BO, I["conv_pw2_b_2"].to_broadcast([128, 1024]), "conv")
        ready = norm(X, prm("norm_mix_2", 8, 8), None, H8)
        V(ve.memset(HP[:, :, 0:30], 0.0))
        ON_PE = (6, 7)
        taps = [(f, w) for f in ON_PE for w in range(31)] + [(5, w) for w in range(9, 31)]
        dgt, dgu = {}, {}

        def diagonal(n):
            if n < len(taps):
                f, w = taps[n]
                A.wait(dgu.get(n - NDG))
                dgt[n] = A.mark(ac.mul(DG[:, n % NDG, :], ident, prm("conv_dw_w_2", 8 * w + f)))

        A.wait(A.now(), *ready)
        for n in range(NDG):
            diagonal(n)
        t_tile = {}

        def dve_taps():
            for pair in ((0, 1), (2, 3), (4, 5)):
                for f in pair:
                    V.mark(ve.tensor_scalar(CA[:, f, :], HP[:, f, 0:256], prm("conv_dw_w_2", f),
                                            prm("conv_dw_b_2", f), MUL, ADD))
                yield
                for w in range(1, 31):
                    both = pair if w < 9 or pair[1] != 5 else pair[:1]
                    for f in both:
                        V.wait((V.sem, V.n - len(both) + 1))
                        V.mark(ve.scalar_tensor_tensor(CA[:, f, :], HP[:, f, w:w + 256], prm("conv_dw_w_2", 8 * w + f),
                                                       CA[:, f, :], MUL, ADD))
                    yield
                for f in pair:
                    t_tile[f] = V.now()

        steps = dve_taps()
        for j in range(4):
            (ba,), ta = proj_b(ready=ready if j == 0 else None)
            (bg,), tg = proj_b()
            A.wait(tg, V.now())
            for m in range(2):
                A.mark(ac.activation(CG[:, m, :], bank[bg][:, 256 * m:256 * m + 256], ACT.Sigmoid,
                                     bias=prm("conv_pw1_b_2", 8 + 2 * j + m)))
            R.put(bg, A.now())
            V.wait(ta, A.now())
            for m in range(2):
                f = 2 * j + m
                V.mark(ve.scalar_tensor_tensor(HP[:, f, 30:286], bank[ba][:, 256 * m:256 * m + 256],
                                               prm("conv_pw1_b_2", f), CG[:, m, :], ADD, MUL))
            R.put(ba, V.now())
            V.wait(V.now())
            t_hp = V.now()
            if j < 3:
                for _ in range(11):
                    next(steps)
        P.wait(t_hp)
        bp, bh = R.get(), R.get()
        for n, (f, w) in enumerate(taps):
            P.wait(dgt[n])
            bf, c = (bh, 0) if f == 5 else (bp, 256 * ON_PE.index(f))
            x = pe.matmul(bank[bf][:, c:c + 256], DG[:, n % NDG, :], HP[:, f, w:w + 256],
                          start=w == (9 if f == 5 else 0), stop=w == 30)
            if n % 4 == 3 or n == len(taps) - 1:
                t = P.mark(x)
                for q in range(n - n % 4, n + 1):
                    dgu[q] = t
            if n % 4 == 3 or n == len(taps) - 1:
                for q in range(NDG + n - n % 4, NDG + n + 1):
                    diagonal(q)
        A.wait(t)
        for f in ON_PE:
            c = 256 * ON_PE.index(f)
            A.mark(ac.activation(CA[:, f, :], bank[bp][:, c:c + 256], ACT.Identity, bias=prm("conv_dw_b_2", f)))
            t_tile[f] = A.now()
        R.put(bp, A.now())
        for _ in steps:
            pass
        V.wait(t, V.now())
        V(ve.tensor_tensor(CA[:, 5, :], CA[:, 5, :], bank[bh][:, 0:256], ADD))
        t_tile[5] = V.now()
        R.put(bh, V.now())

        b = R.get()
        order = list(ON_PE) + [f for f in range(8) if f not in ON_PE]
        for n, f in enumerate(order):
            P.wait(t_tile[f])
            x = pe.matmul(bank[b][:, 0:256], ones, CA[:, f, :], start=n == 0, stop=n == 7)
        V.wait(P.mark(x), t_tile[ON_PE[-1]])
        t = V(ve.tensor_scalar(LR, bank[b][:, 0:256], 1.0 / D, None, MUL))
        R.put(b, t)
        pairs = lambda ap: ap.rearrange("p (t n) -> p t n", t=1).to_broadcast([128, 2, 256])
        b = R.get()
        for q in range(4):
            s = slice(2 * q, 2 * q + 2)
            t = V.mark(ve.tensor_tensor(CA[:, s, :], CA[:, s, :], pairs(LR), SUB))
            A.wait(t)
            t = A.mark(ac.activation(CQ[:, s, :], CA[:, s, :], ACT.Square))
            P.wait(t)
            for f in (2 * q, 2 * q + 1):
                x = pe.matmul(bank[b][:, 0:256], ones, CQ[:, f, :], start=f == 0, stop=f == 7)
        V.wait(V.now())
        A.wait(P.mark(x))
        t = A.mark(ac.activation(LRR, bank[b][:, 0:256], ACT.Sqrt, bias=eps, scale=1.0 / D))
        R.put(b, t)
        V.wait(t)
        V(ve.reciprocal(LRR, LRR))
        tq = []
        for q in range(4):
            s = slice(2 * q, 2 * q + 2)
            tq.append(V.mark(ve.tensor_tensor(CA[:, s, :], CA[:, s, :], pairs(LRR), MUL)))
        t_yj = {}
        for q in range(4):
            s = slice(2 * q, 2 * q + 2)
            A.wait(tq[q])
            for f in (2 * q, 2 * q + 1):
                A.mark(ac.activation(CQ[:, f, :], CA[:, f, :], ACT.Silu, scale=prm("conv_ln_w_2", f),
                                     bias=prm("conv_ln_b_2", f)))
            A.wait(A.now())
            t = A.mark(ac.copy(Y8[0][:, s, :], CQ[:, s, :]))
            V.wait(t)
            t = V.mark(ve.tensor_tensor(Y8[1][:, s, :], CQ[:, s, :], f32(Y8[0][:, s, :]), SUB))
            t = proj_a(Y8, 2 * q, q == 0, q == 3, (t,))
        V.wait(t_bo)
        add_out(t, bias=BO)
        ffn(1)

        QK = [ar(2048 * s, 2048).rearrange("p (k n) -> p k n", k=8) for s in range(2)]
        o = 4096
        VS = ar(o, 2048).rearrange("p (i n) -> p i n", i=2)
        YS = [ar(o + 2048 + 1024 * i, 1024) for i in range(2)]
        SQ3 = [ar(o + 4096 + 4900 * i, 512) for i in range(2)]
        RS3 = ar(o + 4608, 512)
        MSK = ar(o + 5120, 384)
        ZERO = ar(o + 5504, 256)
        ZZ = [ar(o + 5760 + 384 * i, 384) for i in range(2)]
        UU = [ar(o + 6528 + 384 * i, 384) for i in range(2)]
        GG = [ar(o + 7296 + 384 * i, 384) for i in range(2)]
        CC = [ar(o + 8064 + 386 * i, 386) for i in range(2)]
        AT = [ar(o + 9508 + 384 * i, 384) for i in range(2)]
        S.wait(V.now(), A.now(), P.now())
        t_m = small(MSK, I["consts"][:, C_SB:C_SB + 384], "sb")
        ready = norm(X, prm("norm_mix_2", 16, 8), None, H8, late=True)
        V.wait(t_m, *ready)
        A.wait(V.now(), *ready)
        V(ve.memset(ZERO, 0.0))
        for i in range(2):
            V(ve.memset(CC[i], 1.0))
        pend = None

        def fin_norm(j, ta, gain):
            dst = QK[j // 4][:, 2 * (j % 4):2 * (j % 4) + 2, :]
            b = R.get()
            P.wait(ta)
            tp = P.mark(pe.matmul(bank[b][:, :], blk, SQ3[j % 2], start=True, stop=True))
            A.wait(tp, V.now())
            t = A.mark(ac.activation(RS3, bank[b][:, :], ACT.Sqrt, bias=eps, scale=1.0 / 64))
            R.put(b, t)
            V.wait(t)
            V(ve.reciprocal(RS3, RS3))
            V(ve.scalar_tensor_tensor(dst, dst, gain, two(RS3), MUL, MUL))
            return tp

        read = {}
        for j in range(8):
            bs, t = proj_b(ready=ready if j == 0 else None)
            if j == 0:
                rms_rows()
            g = prm(("sb_q_norm_2", "sb_k_norm_2")[j // 4], 0)
            A.wait(read.get(j - 2))
            ta, tv = head_norm(bank[bs[0]][:, :], QK[j // 4][:, 2 * (j % 4):2 * (j % 4) + 2, :], t, SQ3[j % 2])
            R.put(bs[0], tv)
            if pend is not None:
                read[pend[0]] = fin_norm(*pend)
            pend = (j, ta, g)
        for j in range(4):
            t = proj_a(H8, 2 * j, j == 0, j == 3)
            if j == 0:
                fin_norm(*pend)
        for q in (0, 2, 1, 3):
            m, h = q // 2, q % 2
            (A if q % 2 else V).wait(bank_done[q])
            evacuate(VS[:, m, 512 * h:512 * h + 512], q)
        P.wait(A.now(), V.now())
        hist = {}

        def sb_scores(h):
            q, k = QK[0], QK[1]
            r, f = slice(64 * (h % 2), 64 * (h % 2) + 64), h // 2
            b = R.get()
            pe.matmul(bank[b][:, 0:128], q[r, f, 0:128], k[r, f, 0:128], start=True, stop=True)
            x = pe.matmul(bank[b][:, 128:384], q[r, f, 128:256], k[r, f, 0:256], start=True, stop=True)
            return b, P.mark(x)

        def sb_vec(h, b, t):
            i = h % 2
            V.wait(t, hist.get(("a", h - 2)))
            t = V.mark(ve.scalar_tensor_tensor(ZZ[i], bank[b][:, 0:384], 0.125, MSK, MUL, ADD))
            R.put(b, t)
            A.wait(t, hist.get(("scan", h - 2)), hist.get(("p", h - 2)))
            tu = A.mark(ac.activation(UU[i], ZZ[i], ACT.Sigmoid, scale=-1.0))
            hist["a", h] = A.mark(ac.activation(GG[i], ZZ[i], ACT.Sigmoid))
            hist["u", h] = tu

        def sb_scan(h):
            i = h % 2
            c = CC[i]
            V.wait(hist["u", h])
            V.mark(ve.tensor_tensor_scan(c[:, 127::-1], UU[i][:, 127::-1], ZERO[:, 0:128], 1.0, MUL, ADD))
            V.mark(ve.tensor_tensor_scan(c[:, 384:128:-1], UU[i][:, 383:127:-1], ZERO, 1.0, MUL, ADD))
            hist["scan", h] = V.now()
            V.wait(V.now(), hist["a", h])
            V.mark(ve.tensor_tensor(GG[i][:, 0:128], GG[i][:, 0:128], c[:, 1:129], MUL))
            V.mark(ve.tensor_tensor(GG[i][:, 128:384], GG[i][:, 128:384], c[:, 130:386], MUL))
            return V.now()

        def sb_turn(h, t):
            i = h % 2
            P.wait(t)
            b = R.get()
            for s in range(3):
                x = pe.transpose(bank[b][:, 128 * s:128 * s + 128], GG[i][:, 128 * s:128 * s + 128], ident)
            t = P.mark(x)
            hist["p", h] = t
            A.wait(t, hist.get(("y", h - 2)))
            hist["at", h] = A.mark(ac.copy(AT[i], bank[b][:, 0:384]))
            R.put(b, hist["at", h])

        def sb_out(h):
            i = h % 2
            P.wait(hist["at", h])
            vc = slice(64 * h, 64 * h + 64)
            q, oc = h // 8, slice(64 * (h % 8), 64 * (h % 8) + 64)
            pe.matmul(bank[q][:, oc], AT[i][:, 0:128], VS[:, 0, vc], start=True, stop=True)
            pe.matmul(bank[2 + q][:, oc], AT[i][:, 128:256], VS[:, 0, vc], start=True, stop=False)
            x = pe.matmul(bank[2 + q][:, oc], AT[i][:, 256:384], VS[:, 1, vc], start=False, stop=True)
            hist["y", h] = P.mark(x)

        def sb_rows(half):
            A.wait(hist["y", 8 * half + 7])
            for i in range(2):
                q = half + 2 * i
                acc_free[q] = (A.mark(ac.copy(YS[i][:, 512 * half:512 * half + 512], bank[q][:, :])),)
            return A.now()

        tt, sc, rows = {}, {0: sb_scores(0)}, {}
        for h in range(19):
            if h < 15:
                sc[h + 1] = sb_scores(h + 1)
            if h < 16:
                sb_vec(h, *sc[h])
            if h >= 3:
                sb_out(h - 3)
            if 1 <= h < 17:
                tt[h - 1] = sb_scan(h - 1)
                sb_turn(h - 1, tt[h - 1])
            if h in (11, 18):
                rows[h // 18] = sb_rows(h // 18)
        for q in range(4):
            P.wait(rows[q // 2])
            b = R.get()
            for m in range(2):
                for i in range(2):
                    k = 2 * q + m
                    x = pe.transpose(bank[b][:, 256 * m + 128 * i:256 * m + 128 * i + 128],
                                     YS[i][:, 128 * k:128 * k + 128], ident)
            t = P.mark(x)
            A.wait(t)
            s = slice(2 * q, 2 * q + 2)
            t = A(ac.copy(Y8[0][:, s, :], bank[b][:, :]))
            V.wait(t)
            t_y = V(ve.tensor_tensor(Y8[1][:, s, :], bank[b][:, :].rearrange("p (m n) -> p m n", m=2),
                                     f32(Y8[0][:, s, :]), SUB))
            R.put(b, t_y)
            t_yj[q] = t_y
        for j in range(4):
            t = proj_a(Y8, 2 * j, j == 0, j == 3, (t_yj[j],))
        add_out(t)
        ffn(2)
        ret(1, 3)
        ffn(3)

        FN = ar(4096, 1024)
        S.wait(V.now(), A.now(), P.now())
        t_f = small(FN, I["final_norm_2"].rearrange("(o n) -> o n", o=1).to_broadcast([128, 1024]), "final")
        rstd()
        V.wait(t_f)
        for i in range(2):
            t = V(ve.scalar_tensor_tensor(XN[i], X[i][:, :], ST[:, 8 + i:9 + i], FN, MUL, MUL))
            S.wait(t)
            nc.sync.dma_start(out[0, 128 * i:128 * i + 128, :], XN[i]).then_inc(s_out, 16)
        nc.sync.wait_ge(s_out, 32)
        assert state["next"] == len(items)


_INS = [
    "x", "c", "ctx", "c_ctx", "w_mod", "b_mod", "norm1_g", "norm2_g", "hg_w_in", "hg_lb_fwd", "hg_lb_bwd", "hg_gnorm",
    "hg_w_out", "router_w", "router_b", "moe_w_gate", "moe_w_up", "moe_w_down", "final_g", "norm_mix_2", "norm_ffn_2",
    "ret_w_in_2", "ret_q_norm_2", "ret_k_norm_2", "ret_gn_w_2", "ret_gn_b_2", "ret_w_out_2", "conv_pw1_w_2",
    "conv_pw1_b_2", "conv_dw_w_2", "conv_dw_b_2", "conv_ln_w_2", "conv_ln_b_2", "conv_pw2_w_2", "conv_pw2_b_2",
    "sb_w_in_2", "sb_q_norm_2", "sb_k_norm_2", "sb_w_out_2", "ffn_w1_2", "ffn_w2_2", "final_norm_2",
]


def constants():
    import numpy as np

    c = np.zeros((128, C_ALL), np.float32)
    p = np.arange(128)
    c[:, C_ID:C_ID + 128] = np.eye(128)
    c[:, C_ONE:C_ONE + 128] = 1.0
    c[:, C_BLK:C_BLK + 128] = p[:, None] // 64 == p[None, :] // 64
    c[[0, 2], C_SEL:C_SEL + 128] = 1.0
    same = p[:, None] // 64 == p[None, :] // 64
    c[:, C_MF:C_MF + 128] = same & (p[:, None] <= p[None, :])
    c[:, C_MB:C_MB + 128] = same & (p[:, None] >= p[None, :])
    t = np.arange(512)
    c[:, C_RF:C_RF + 512] = np.where(t < 256, t % 64 != 0, t != 256)
    c[:, C_RB:C_RB + 512] = np.where(t < 256, t % 64 != 63, t != 511)
    s, q = np.arange(256)[:, None], np.arange(256)[None, :]
    for h in range(4):
        lg = np.log(1.0 - 2.0 ** (-5.0 - h))
        m = np.where(s // 64 == q // 64, np.exp(lg * np.abs(q - s)), np.where(s // 64 < q // 64, np.exp(lg * (q - s)), 0.0))
        m = m / 16.0
        c[:, C_RET + 384 * h:C_RET + 384 * h + 256] = m[0:128, :]
        c[:, C_RET + 384 * h + 256:C_RET + 384 * h + 384] = m[128:256, 128:256]
    f = np.float32(10000.0) ** (-np.arange(128, dtype=np.float32) / np.float32(128))
    ang = (np.arange(256, dtype=np.float32)[None, :] * f[:, None].astype(np.float32)).astype(np.float64)
    c[:, C_COS:C_COS + 256] = np.cos(ang)
    c[:, C_SIN:C_SIN + 256] = np.sin(ang)
    diag = np.where(p[None, :] < p[:, None], 0.0, NEG)
    c[:, C_SB:C_SB + 128] = diag
    c[:, C_SB + 256:C_SB + 384] = diag
    c[:, C_LT:C_LT + 16] = (np.arange(4)[None, :] < np.arange(4)[:, None]).reshape(-1)
    return c


def kernel(**inputs):
    import numpy as _np
    import concourse.bacc as _bacc
    from concourse import mybir as _mybir
    from concourse.bass_utils import run_bass_kernel_spmd as _run

    nc = _bacc.Bacc("TRN2", target_bir_lowering=False, num_devices=1)
    arrays, args = {}, {}
    for name in _INS + ["consts"]:
        a = constants() if name == "consts" else _np.ascontiguousarray(inputs[name])
        arrays[f"in_{name}"] = a
        args[name] = nc.dram_tensor(f"in_{name}", a.shape, _mybir.dt.from_np(a.dtype), kind="ExternalInput").ap()
    out = nc.dram_tensor("out_0", (1, 256, 1024), F32, kind="ExternalOutput").ap()
    build(nc, args, out)
    r = _run(nc, [arrays], core_ids=[0])
    return r.results[0]["out_0"]
```
